# Optimizing a Trainium2 kernel written in Bass

```python
import math
import jax, jax.numpy as jnp
from jax import lax
import numpy as np

D_MODEL = 1024
BATCH = 1
SEQ = 256
DEPTH = 2

HEAD_DIM = 64
N_DIFF_HEADS = 4
DIFF_V_DIM = 2 * HEAD_DIM
DIFF_QK = N_DIFF_HEADS * 2 * HEAD_DIM
DIFF_WIDTH = N_DIFF_HEADS * DIFF_V_DIM
N_FOX_HEADS = 8
FOX_WIDTH = N_FOX_HEADS * HEAD_DIM
N_BUCKETS = 32
MAX_DISTANCE = 128
Q_BLOCK = 128
N_KEYS = 128
N_EXPERTS = N_KEYS * N_KEYS
PEER_HEADS = 8
PEER_TOPK = 16
PEER_QDIM = 256
PEER_HALF = PEER_QDIM // 2
TOKEN_BLOCK = 128
EPS = 1e-6
IN_SIZES = (DIFF_QK, DIFF_QK, DIFF_WIDTH, FOX_WIDTH, FOX_WIDTH, FOX_WIDTH, N_FOX_HEADS, D_MODEL, D_MODEL)
IN_WIDTH = sum(IN_SIZES)


def rms_norm(x, g):
    xf = x.astype(jnp.float32)
    y = xf * lax.rsqrt(jnp.mean(xf * xf, axis=-1, keepdims=True) + EPS)
    return (y * g.astype(jnp.float32)).astype(x.dtype)

def t5_bucket(dist):
    n = jnp.maximum(dist, 0)
    max_exact = N_BUCKETS // 2
    nf = jnp.maximum(n, 1).astype(jnp.float32)
    large = max_exact + (jnp.log(nf / max_exact) / math.log(MAX_DISTANCE / max_exact)
                         * (N_BUCKETS - max_exact)).astype(jnp.int32)
    large = jnp.minimum(large, N_BUCKETS - 1)
    return jnp.where(n < max_exact, n, large)

def diff_attention(q, k, v, rel_bias, lam, lam_init, subln_g):
    B, S = q.shape[0], q.shape[1]
    scale = HEAD_DIM ** -0.5
    lf = lam.astype(jnp.float32)
    lam_full = jnp.exp(jnp.sum(lf[0] * lf[1])) - jnp.exp(jnp.sum(lf[2] * lf[3])) + lam_init
    outs = []
    for blk in range(S // Q_BLOCK):
        q0 = blk * Q_BLOCK
        end = q0 + Q_BLOCK
        logits = jnp.einsum('bqhmd,bkhmd->bhmqk', q[:, q0:end], k[:, :end]).astype(jnp.float32) * scale
        dist = (q0 + jnp.arange(Q_BLOCK))[:, None] - jnp.arange(end)[None, :]
        bias = jnp.transpose(rel_bias[t5_bucket(dist)], (2, 0, 1))[:, None]
        logits = jnp.where(dist >= 0, logits + bias.astype(jnp.float32), -jnp.inf)
        probs = jax.nn.softmax(logits, axis=-1)
        weights = probs[:, :, 0] - lam_full * probs[:, :, 1]
        outs.append(jnp.einsum('bhqk,bkhd->bqhd', weights.astype(v.dtype), v[:, :end]))
    o = jnp.concatenate(outs, axis=1)
    o = rms_norm(o, subln_g) * (1.0 - lam_init)
    return o.reshape(B, S, DIFF_WIDTH)

def forgetting_attention(q, k, v, f_logit):
    B, S = q.shape[0], q.shape[1]
    scale = HEAD_DIM ** -0.5
    c = jnp.swapaxes(jnp.cumsum(jax.nn.log_sigmoid(f_logit.astype(jnp.float32)), axis=1), 1, 2)
    outs = []
    for blk in range(S // Q_BLOCK):
        q0 = blk * Q_BLOCK
        end = q0 + Q_BLOCK
        logits = jnp.einsum('bqhd,bkhd->bhqk', q[:, q0:end], k[:, :end]).astype(jnp.float32) * scale
        decay = c[:, :, q0:end, None] - c[:, :, None, :end]
        dist = (q0 + jnp.arange(Q_BLOCK))[:, None] - jnp.arange(end)[None, :]
        logits = jnp.where(dist >= 0, logits + decay, -jnp.inf)
        probs = jax.nn.softmax(logits, axis=-1)
        outs.append(jnp.einsum('bhqk,bkhd->bqhd', probs.astype(v.dtype), v[:, :end]))
    return jnp.concatenate(outs, axis=1).reshape(B, S, FOX_WIDTH)

def peer_ffn(h, w_query, sub_keys, expert_u, expert_v):
    B, S, D = h.shape
    T = B * S
    t = h.reshape(T, D)
    q = (t @ w_query).reshape(T, PEER_HEADS, 2, PEER_HALF)
    s = jnp.einsum('thpd,pnd->thpn', q, sub_keys).astype(jnp.float32)
    top_s, top_i = lax.top_k(s, PEER_TOPK)
    cand_s = (top_s[:, :, 0, :, None] + top_s[:, :, 1, None, :]).reshape(T, PEER_HEADS, PEER_TOPK * PEER_TOPK)
    cand_i = (top_i[:, :, 0, :, None] * N_KEYS + top_i[:, :, 1, None, :]).reshape(T, PEER_HEADS, PEER_TOPK * PEER_TOPK)
    best_s, best_pos = lax.top_k(cand_s, PEER_TOPK)
    experts = jnp.take_along_axis(cand_i, best_pos, axis=-1).reshape(T, PEER_HEADS * PEER_TOPK)
    gates = jax.nn.softmax(best_s, axis=-1).reshape(T, PEER_HEADS * PEER_TOPK)
    nblk = T // TOKEN_BLOCK

    def expert_block(args):
        tb, eb, gb = args
        act = jax.nn.gelu(jnp.einsum('td,ted->te', tb, expert_u[eb]).astype(jnp.float32), approximate=False)
        return jnp.einsum('te,ted->td', (gb * act).astype(tb.dtype), expert_v[eb])

    out = lax.map(expert_block, (t.reshape(nblk, TOKEN_BLOCK, D),
                                 experts.reshape(nblk, TOKEN_BLOCK, -1),
                                 gates.reshape(nblk, TOKEN_BLOCK, -1)))
    return out.reshape(B, S, D)

def first_inputs(seed: int = 0) -> dict:
    key = jax.random.key(seed)
    ks = jax.random.split(key, 17)
    nrm = lambda k, shape, scale: jax.random.normal(k, shape, jnp.float32) * scale
    return {
        "x": nrm(ks[0], (BATCH, SEQ, D_MODEL), 1.0),
        "norm1_g": 1.0 + nrm(ks[1], (DEPTH, D_MODEL), 0.02),
        "w_in": nrm(ks[2], (DEPTH, D_MODEL, IN_WIDTH), D_MODEL ** -0.5),
        "b_forget": 2.0 + nrm(ks[3], (DEPTH, N_FOX_HEADS), 0.1),
        "diff_lambda": nrm(ks[4], (DEPTH, 4, HEAD_DIM), 0.1),
        "diff_subln_g": 1.0 + nrm(ks[5], (DEPTH, DIFF_V_DIM), 0.02),
        "w_diff_o": nrm(ks[6], (DEPTH, DIFF_WIDTH, D_MODEL), DIFF_WIDTH ** -0.5),
        "w_fox_o": nrm(ks[7], (DEPTH, FOX_WIDTH, D_MODEL), FOX_WIDTH ** -0.5),
        "w_out": nrm(ks[8], (DEPTH, D_MODEL, D_MODEL), D_MODEL ** -0.5),
        "norm2_g": 1.0 + nrm(ks[9], (DEPTH, D_MODEL), 0.02),
        "w_query": nrm(ks[10], (DEPTH, D_MODEL, PEER_HEADS * PEER_QDIM), D_MODEL ** -0.5),
        "sub_keys": nrm(ks[11], (DEPTH, 2, N_KEYS, PEER_HALF), PEER_HALF ** -0.5),
        "expert_u": nrm(ks[12], (DEPTH, N_EXPERTS, D_MODEL), D_MODEL ** -0.5),
        "expert_v": nrm(ks[13], (DEPTH, N_EXPERTS, D_MODEL), (PEER_HEADS * PEER_TOPK) ** -0.5),
        "rel_bias": nrm(ks[14], (N_BUCKETS, N_DIFF_HEADS), 0.5),
        "final_norm_g": 1.0 + nrm(ks[15], (D_MODEL,), 0.02),
    }

def first_block(x, norm1_g, w_in, b_forget, diff_lambda, diff_subln_g, w_diff_o, w_fox_o, w_out,
              norm2_g, w_query, sub_keys, expert_u, expert_v, rel_bias, final_norm_g):
    B, S, D = x.shape
    split_points = np.cumsum(IN_SIZES)[:-1].tolist()
    for layer in range(DEPTH):
        lam_init = 0.8 - 0.6 * math.exp(-0.3 * layer)
        h = rms_norm(x, norm1_g[layer])
        proj = h @ w_in[layer]
        dq, dk, dv, fq, fk, fv, ff, ga, gb = jnp.split(proj, split_points, axis=-1)
        y_diff = diff_attention(dq.reshape(B, S, N_DIFF_HEADS, 2, HEAD_DIM),
                                dk.reshape(B, S, N_DIFF_HEADS, 2, HEAD_DIM),
                                dv.reshape(B, S, N_DIFF_HEADS, DIFF_V_DIM),
                                rel_bias, diff_lambda[layer], lam_init, diff_subln_g[layer])
        y_fox = forgetting_attention(fq.reshape(B, S, N_FOX_HEADS, HEAD_DIM),
                                     fk.reshape(B, S, N_FOX_HEADS, HEAD_DIM),
                                     fv.reshape(B, S, N_FOX_HEADS, HEAD_DIM),
                                     ff + b_forget[layer])
        merged = jax.nn.sigmoid(ga) * (y_diff @ w_diff_o[layer]) + jax.nn.sigmoid(gb) * (y_fox @ w_fox_o[layer])
        x = x + merged @ w_out[layer]
        x = x + peer_ffn(rms_norm(x, norm2_g[layer]), w_query[layer], sub_keys[layer],
                         expert_u[layer], expert_v[layer])
    return rms_norm(x, final_norm_g)


CTX_LEN = 256
GRID_W = 64
N_MOD = 9
D_FF = 2816

FNET_GROUPS = 4
FNET_GROUP_DIM = 128
FNET_DIM = FNET_GROUPS * FNET_GROUP_DIM
NA_HEADS = 8
NA_HEAD_DIM = 64
NA_DIM = NA_HEADS * NA_HEAD_DIM
NA_KH = 8
NA_KW = 16
AB_IN_DIM = FNET_DIM + 3 * NA_DIM
AB_OUT_DIM = FNET_DIM + NA_DIM
MLA_HEADS = 8
MLA_NOPE = 128
MLA_ROPE = 64
MLA_V = 128
MLA_Q_RANK = 384
MLA_KV_RANK = 128
MLA_IN_DIM = MLA_Q_RANK + MLA_KV_RANK + MLA_ROPE
ROPE_BASE = 10000.0

N_EVEN = (DEPTH + 1) // 2
N_ODD = DEPTH // 2


def rmsnorm(x, g):
    xf = x.astype(jnp.float32)
    y = xf * lax.rsqrt(jnp.mean(xf * xf, axis=-1, keepdims=True) + EPS)
    return (y * g.astype(jnp.float32)).astype(x.dtype)

def swiglu(h, w_gate, w_up, w_down):
    return (jax.nn.silu(h @ w_gate) * (h @ w_up)) @ w_down

def half_ffn(x, shift, scale, gate, g, w_gate, w_up, w_down):
    h = rmsnorm(x, g) * (1 + scale) + shift
    return x + 0.5 * gate * swiglu(h, w_gate, w_up, w_down)

def axial_rope_tables(n_tok, rot_dim):
    pos = jnp.arange(n_tok)
    row = (pos // GRID_W).astype(jnp.float32)
    col = (pos % GRID_W).astype(jnp.float32)
    half = rot_dim // 2
    inv = ROPE_BASE ** (-jnp.arange(0, half, 2, dtype=jnp.float32) / half)
    ang_r = row[:, None] * inv[None]
    ang_c = col[:, None] * inv[None]
    ang = jnp.concatenate([ang_r, ang_r, ang_c, ang_c], axis=-1)
    return jnp.cos(ang), jnp.sin(ang)

def apply_axial_rope(x, cos, sin):
    xf = x.astype(jnp.float32)
    a, b, cc, d = jnp.split(xf, 4, axis=-1)
    rot = jnp.concatenate([-b, a, -d, cc], axis=-1)
    return (xf * cos + rot * sin).astype(x.dtype)

def fourier_mix(u):
    b, n, _ = u.shape
    ug = u.astype(jnp.float32).reshape(b, n, FNET_GROUPS, FNET_GROUP_DIM)
    f = jnp.fft.fft2(ug, axes=(1, 3), norm="ortho").real
    return f.reshape(b, n, FNET_DIM).astype(u.dtype)

def dense_attention(q, k, v):
    s = jnp.einsum('bqhd,bkhd->bhqk', q, k, preferred_element_type=jnp.float32) * (q.shape[-1] ** -0.5)
    p = jax.nn.softmax(s, axis=-1).astype(v.dtype)
    return jnp.einsum('bhqk,bkhd->bqhd', p, v)

def neighbourhood_attention(q, k, v, k_ctx, v_ctx, rpb):
    b, s, h, dh = q.shape
    rows = s // GRID_W
    kh = min(NA_KH, rows)
    kw = NA_KW
    scale = dh ** -0.5
    qg = q.reshape(b, rows, GRID_W, h, dh)
    kg = k.reshape(b, rows, GRID_W, h, dh)
    vg = v.reshape(b, rows, GRID_W, h, dh)
    cols = jnp.arange(GRID_W)
    col_start = jnp.clip(cols - kw // 2, 0, GRID_W - kw)
    col_idx = col_start[:, None] + jnp.arange(kw)[None, :]
    col_off = col_idx - cols[:, None] + (NA_KW - 1)

    def one_row(r):
        r0 = jnp.clip(r - kh // 2, 0, rows - kh)
        row_off = r0 + jnp.arange(kh) - r + (NA_KH - 1)
        k_band = lax.dynamic_slice_in_dim(kg, r0, kh, axis=1)
        v_band = lax.dynamic_slice_in_dim(vg, r0, kh, axis=1)
        k_win = k_band[:, :, col_idx]
        v_win = v_band[:, :, col_idx]
        qr = lax.dynamic_index_in_dim(qg, r, axis=1, keepdims=False)
        bias = rpb[:, row_off[:, None, None], col_off[None, :, :]]
        bias = jnp.transpose(bias, (0, 2, 1, 3)).reshape(h, GRID_W, kh * kw).astype(jnp.float32)
        s_win = jnp.einsum('bqhd,biqjhd->bhqij', qr, k_win, preferred_element_type=jnp.float32)
        s_win = s_win.reshape(b, h, GRID_W, kh * kw) * scale + bias[None]
        s_ctx = jnp.einsum('bqhd,blhd->bhql', qr, k_ctx, preferred_element_type=jnp.float32) * scale
        p = jax.nn.softmax(jnp.concatenate([s_win, s_ctx], axis=-1), axis=-1).astype(v.dtype)
        p_win = p[..., :kh * kw].reshape(b, h, GRID_W, kh, kw)
        p_ctx = p[..., kh * kw:]
        return (jnp.einsum('bhqij,biqjhd->bqhd', p_win, v_win)
                + jnp.einsum('bhql,blhd->bqhd', p_ctx, v_ctx))

    o = lax.map(one_row, jnp.arange(rows))
    return jnp.transpose(o, (1, 0, 2, 3, 4)).reshape(b, s, h * dh)

def fourier_na_mixer(h_lat, h_ctx, w_in, rpb, w_out, need_ctx_out):
    def split(z):
        u = z[..., :FNET_DIM]
        qkv = z[..., FNET_DIM:].reshape(z.shape[0], z.shape[1], 3, NA_HEADS, NA_HEAD_DIM)
        return u, qkv[:, :, 0], qkv[:, :, 1], qkv[:, :, 2]

    u_l, q_l, k_l, v_l = split(h_lat @ w_in)
    u_c, q_c, k_c, v_c = split(h_ctx @ w_in)
    a_l = fourier_mix(u_l)
    b_l = neighbourhood_attention(q_l, k_l, v_l, k_c, v_c, rpb)
    y_lat = jnp.concatenate([a_l, b_l], axis=-1) @ w_out
    if not need_ctx_out:
        return y_lat, None
    a_c = fourier_mix(u_c)
    b_c = dense_attention(q_c, k_c, v_c).reshape(h_ctx.shape[0], h_ctx.shape[1], NA_DIM)
    y_ctx = jnp.concatenate([a_c, b_c], axis=-1) @ w_out
    return y_lat, y_ctx

def mla_block_attention(q_nope, q_rope, k_nope, k_rope, v):
    b, n, h, _ = q_nope.shape
    nb = n // Q_BLOCK
    scale = (MLA_NOPE + MLA_ROPE) ** -0.5
    qn = q_nope.reshape(b, nb, Q_BLOCK, h, MLA_NOPE).swapaxes(0, 1)
    qr = q_rope.reshape(b, nb, Q_BLOCK, h, MLA_ROPE).swapaxes(0, 1)

    def one_block(args):
        qn_b, qr_b = args
        s = (jnp.einsum('bqhd,bkhd->bhqk', qn_b, k_nope, preferred_element_type=jnp.float32)
             + jnp.einsum('bqhr,bkr->bhqk', qr_b, k_rope, preferred_element_type=jnp.float32)) * scale
        p = jax.nn.softmax(s, axis=-1).astype(v.dtype)
        return jnp.einsum('bhqk,bkhd->bqhd', p, v)

    o = lax.map(one_block, (qn, qr))
    return o.swapaxes(0, 1).reshape(b, n, h * MLA_V)

def mla_mixer(h_lat, h_ctx, w_in, g_q, g_kv, w_uq, w_uk, w_uv, w_o, cos, sin, need_ctx_out):
    def project(hh):
        bb, nn = hh.shape[0], hh.shape[1]
        z = hh @ w_in
        c_q = rmsnorm(z[..., :MLA_Q_RANK], g_q)
        c_kv = rmsnorm(z[..., MLA_Q_RANK:MLA_Q_RANK + MLA_KV_RANK], g_kv)
        k_rope = z[..., MLA_Q_RANK + MLA_KV_RANK:]
        q = (c_q @ w_uq).reshape(bb, nn, MLA_HEADS, MLA_NOPE + MLA_ROPE)
        k_nope = (c_kv @ w_uk).reshape(bb, nn, MLA_HEADS, MLA_NOPE)
        v = (c_kv @ w_uv).reshape(bb, nn, MLA_HEADS, MLA_V)
        return q[..., :MLA_NOPE], q[..., MLA_NOPE:], k_nope, k_rope, v

    qn_l, qr_l, kn_l, kr_l, v_l = project(h_lat)
    qn_c, qr_c, kn_c, kr_c, v_c = project(h_ctx)
    qr_l = apply_axial_rope(qr_l, cos[:, None, :], sin[:, None, :])
    kr_l = apply_axial_rope(kr_l, cos, sin)
    kn_all = jnp.concatenate([kn_l, kn_c], axis=1)
    kr_all = jnp.concatenate([kr_l, kr_c], axis=1)
    v_all = jnp.concatenate([v_l, v_c], axis=1)
    y_lat = mla_block_attention(qn_l, qr_l, kn_all, kr_all, v_all) @ w_o
    if not need_ctx_out:
        return y_lat, None
    y_ctx = mla_block_attention(qn_c, qr_c, kn_c, kr_c, v_c) @ w_o
    return y_lat, y_ctx

def second_inputs(seed: int = 0) -> dict:
    key = jax.random.key(seed)
    ks = jax.random.split(key, 24)
    f32 = jnp.float32

    def nrm(k, shape, std):
        return jax.random.normal(k, shape, f32) * std

    return {
        "x": nrm(ks[0], (BATCH, SEQ, D_MODEL), 1.0),
        "c": nrm(ks[1], (BATCH, D_MODEL), 1.0),
        "ctx": nrm(ks[2], (BATCH, CTX_LEN, D_MODEL), 1.0),
        "c_ctx": nrm(ks[3], (D_MODEL,), 1.0),
        "ada_w": nrm(ks[4], (DEPTH, D_MODEL, N_MOD * D_MODEL), 0.5 * D_MODEL ** -0.5),
        "ada_b": nrm(ks[5], (DEPTH, N_MOD * D_MODEL), 0.02),
        "norm_g": 1.0 + nrm(ks[6], (DEPTH, 3, D_MODEL), 0.02),
        "ffn_w_gate": nrm(ks[7], (DEPTH, 2, D_MODEL, D_FF), D_MODEL ** -0.5),
        "ffn_w_up": nrm(ks[8], (DEPTH, 2, D_MODEL, D_FF), D_MODEL ** -0.5),
        "ffn_w_down": nrm(ks[9], (DEPTH, 2, D_FF, D_MODEL), D_FF ** -0.5),
        "ab_w_in": nrm(ks[10], (N_EVEN, D_MODEL, AB_IN_DIM), D_MODEL ** -0.5),
        "ab_rpb": nrm(ks[11], (N_EVEN, NA_HEADS, 2 * NA_KH - 1, 2 * NA_KW - 1), 0.1),
        "ab_w_out": nrm(ks[12], (N_EVEN, AB_OUT_DIM, D_MODEL), AB_OUT_DIM ** -0.5),
        "mla_w_in": nrm(ks[13], (N_ODD, D_MODEL, MLA_IN_DIM), D_MODEL ** -0.5),
        "mla_g_q": 1.0 + nrm(ks[14], (N_ODD, MLA_Q_RANK), 0.02),
        "mla_g_kv": 1.0 + nrm(ks[15], (N_ODD, MLA_KV_RANK), 0.02),
        "mla_w_uq": nrm(ks[16], (N_ODD, MLA_Q_RANK, MLA_HEADS * (MLA_NOPE + MLA_ROPE)), MLA_Q_RANK ** -0.5),
        "mla_w_uk": nrm(ks[17], (N_ODD, MLA_KV_RANK, MLA_HEADS * MLA_NOPE), MLA_KV_RANK ** -0.5),
        "mla_w_uv": nrm(ks[18], (N_ODD, MLA_KV_RANK, MLA_HEADS * MLA_V), MLA_KV_RANK ** -0.5),
        "mla_w_o": nrm(ks[19], (N_ODD, MLA_HEADS * MLA_V, D_MODEL), (MLA_HEADS * MLA_V) ** -0.5),
        "final_g": 1.0 + nrm(ks[20], (D_MODEL,), 0.02),
    }

def second_block(x, c, ctx, c_ctx, ada_w, ada_b, norm_g, ffn_w_gate, ffn_w_up, ffn_w_down,
              ab_w_in, ab_rpb, ab_w_out, mla_w_in, mla_g_q, mla_g_kv, mla_w_uq, mla_w_uk,
              mla_w_uv, mla_w_o, final_g):
    n_lat = x.shape[1]
    cos, sin = axial_rope_tables(n_lat, MLA_ROPE)
    sc = jax.nn.silu(c)
    scc = jax.nn.silu(c_ctx)
    x_l, x_c = x, ctx
    for layer in range(DEPTH):
        last = layer == DEPTH - 1
        mod_l = (sc @ ada_w[layer] + ada_b[layer]).reshape(-1, N_MOD, D_MODEL)[:, :, None, :]
        mod_c = (scc @ ada_w[layer] + ada_b[layer]).reshape(N_MOD, D_MODEL)

        x_l = half_ffn(x_l, mod_l[:, 0], mod_l[:, 1], mod_l[:, 2], norm_g[layer, 0],
                       ffn_w_gate[layer, 0], ffn_w_up[layer, 0], ffn_w_down[layer, 0])
        x_c = half_ffn(x_c, mod_c[0], mod_c[1], mod_c[2], norm_g[layer, 0],
                       ffn_w_gate[layer, 0], ffn_w_up[layer, 0], ffn_w_down[layer, 0])

        h_l = rmsnorm(x_l, norm_g[layer, 1]) * (1 + mod_l[:, 4]) + mod_l[:, 3]
        h_c = rmsnorm(x_c, norm_g[layer, 1]) * (1 + mod_c[4]) + mod_c[3]
        i = layer // 2
        if layer % 2 == 0:
            y_l, y_c = fourier_na_mixer(h_l, h_c, ab_w_in[i], ab_rpb[i], ab_w_out[i], not last)
        else:
            y_l, y_c = mla_mixer(h_l, h_c, mla_w_in[i], mla_g_q[i], mla_g_kv[i], mla_w_uq[i],
                                 mla_w_uk[i], mla_w_uv[i], mla_w_o[i], cos, sin, not last)
        x_l = x_l + mod_l[:, 5] * y_l

        x_l = half_ffn(x_l, mod_l[:, 6], mod_l[:, 7], mod_l[:, 8], norm_g[layer, 2],
                       ffn_w_gate[layer, 1], ffn_w_up[layer, 1], ffn_w_down[layer, 1])
        if not last:
            x_c = x_c + mod_c[5] * y_c
            x_c = half_ffn(x_c, mod_c[6], mod_c[7], mod_c[8], norm_g[layer, 2],
                           ffn_w_gate[layer, 1], ffn_w_up[layer, 1], ffn_w_down[layer, 1])
    return rmsnorm(x_l, final_g)


def setup_inputs(seed=0):
    out = dict(first_inputs(seed))
    for name, value in second_inputs(seed + 1).items():
        if name != "x":
            out[name + "_2"] = value
    return out


def reference(
    x, norm1_g, w_in, b_forget, diff_lambda, diff_subln_g, w_diff_o, w_fox_o, w_out, norm2_g,
    w_query, sub_keys, expert_u, expert_v, rel_bias, final_norm_g, c_2, ctx_2, c_ctx_2, ada_w_2,
    ada_b_2, norm_g_2, ffn_w_gate_2, ffn_w_up_2, ffn_w_down_2, ab_w_in_2, ab_rpb_2, ab_w_out_2,
    mla_w_in_2, mla_g_q_2, mla_g_kv_2, mla_w_uq_2, mla_w_uk_2, mla_w_uv_2, mla_w_o_2, final_g_2,
):
    x = first_block(
        x, norm1_g, w_in, b_forget, diff_lambda, diff_subln_g, w_diff_o, w_fox_o, w_out,
        norm2_g, w_query, sub_keys, expert_u, expert_v, rel_bias, final_norm_g,
    )
    return second_block(
        x, c_2, ctx_2, c_ctx_2, ada_w_2, ada_b_2, norm_g_2, ffn_w_gate_2, ffn_w_up_2,
        ffn_w_down_2, ab_w_in_2, ab_rpb_2, ab_w_out_2, mla_w_in_2, mla_g_q_2, mla_g_kv_2,
        mla_w_uq_2, mla_w_uk_2, mla_w_uv_2, mla_w_o_2, final_g_2,
    )


_drawn_inputs = setup_inputs


def setup_inputs(seed=0):
    import zlib

    import numpy as np

    out = dict(_drawn_inputs(seed))
    spreads = {}
    factors = {'b_forget': 2.676,
     'diff_subln_g': 4.432,
     'norm2_g': 6.366,
     'final_norm_g': 2.815,
     'norm_g_2': 8.0,
     'ab_rpb_2': 8.0,
     'mla_g_q_2': 8.0,
     'mla_g_kv_2': 26.296,
     'final_g_2': 7.883}
    for name, (base, spread) in spreads.items():
        noise = np.random.default_rng([zlib.crc32(name.encode()), seed]).standard_normal(out[name].shape)
        drawn = base * np.exp(spread * noise) if base else spread * noise
        out[name] = __import__('jax').numpy.asarray(drawn.astype(out[name].dtype))
    for name, factor in factors.items():
        out[name] = (out[name] * factor).astype(out[name].dtype)
    return out
```

```python
import math
from contextlib import ExitStack

import numpy as np

import concourse.bass as bass
from concourse import mybir

F32 = mybir.dt.float32
U32 = mybir.dt.uint32
ALU = mybir.AluOpType
ACT = mybir.ActivationFunctionType
AX = mybir.AxisListType.X

P = 128
D = 1024
KD = D // P
S = 256
NB = S // P
DEPTH = 2
EPS = 1e-6
HD = 64
NH = 8
ND = 4
NKEYS = 128
TOPK = 16
PH = 8
SLOTS = PH * TOPK
DFF = 2816
KF = DFF // P
NMOD = 9
NEG = -1e30
RING = 8
UW = 1024
GROUP = 8
GBUF = 4


ORDER = ("one0", "ada0", "ada1", "ffn00", "one1", "ab", "ffn01", "ffn00", "ab", "ffn01", "ffn10", "mla", "ffn11")


def lam_init(layer):
    return 0.8 - 0.6 * math.exp(-0.3 * layer)


class Queues:

    ENGINES = ("pe", "act", "dve", "pool", "sp")

    def __init__(self, sem):
        self.sem = {e: sem(f"{e}_done") for e in self.ENGINES}
        self.count = {e: 0 for e in self.ENGINES}
        self.work = {e: [] for e in self.ENGINES}
        self.seen = {e: {} for e in self.ENGINES}

    def wait(self, e, eng, tokens):
        for s, v in tokens:
            if self.seen[e].get(id(s), 0) < v:
                eng.wait_ge(s, v)
                self.seen[e][id(s)] = v

    def op(self, e, tokens, emit):
        self.count[e] += 1

        def run(eng):
            self.wait(e, eng, tokens)
            emit(eng).then_inc(self.sem[e], 1)
        self.work[e].append(run)
        return (self.sem[e], self.count[e])

    def many(self, e, tokens, emits):
        self.count[e] += 1

        def run(eng):
            self.wait(e, eng, tokens)
            for emit in emits:
                last = emit(eng)
            last.then_inc(self.sem[e], 1)
        self.work[e].append(run)
        return (self.sem[e], self.count[e])

    def part(self, e, tokens, run_part):
        def run(eng):
            self.wait(e, eng, tokens)
            run_part(eng)
        self.work[e].append(run)

    def dma(self, e, tokens, out, in_, sem_count):
        sem_count[1] += 16
        value = sem_count[1]

        def run(eng):
            self.wait(e, eng, tokens)
            eng.dma_start(out, in_).then_inc(sem_count[0], 16)
        self.work[e].append(run)
        return (sem_count[0], value)


def turns(eng, n, body, head=0, tail=0, width=RING):
    for st in range(head):
        body(0, st)
    k = (n - head - tail) // width
    at = head
    if k >= 2:
        with eng.Fori(0, k) as i:
            for j in range(width):
                body(i, head + j)
        at = head + k * width
    for st in range(at, n):
        body(0, st)


class Steps:

    def __init__(self, steps):
        self.steps, self.live, self.result = steps, True, None

    def step(self):
        try:
            next(self.steps)
        except StopIteration as end:
            self.live, self.result = False, end.value

    def finish(self):
        while self.live:
            self.step()
        return self.result


def drain(steps):
    return Steps(steps).finish()


def program(nc, io, places):
    with ExitStack() as ctx:
        sem = lambda name: ctx.enter_context(nc.semaphore(name))
        q = Queues(sem)
        pe = lambda t, f: q.op("pe", t, f)
        act = lambda t, f: q.op("act", t, f)
        dve = lambda t, f: q.op("dve", t, f)
        pool = lambda t, f: q.op("pool", t, f)

        bank = [ctx.enter_context(nc.psum_tensor(f"bank{i}", [P, 512], F32)) for i in range(8)]

        def sb(stack, name, shape, dt=F32):
            return stack.enter_context(nc.sbuf_tensor(name, shape, dt))

        ring = sb(ctx, "ring", [P, RING, UW])
        slot_full = [sem(f"slot_full{i}") for i in range(RING)]
        unit_done = sem("unit_done")
        evac = sem("evac")
        half_done = sem("half_done")
        state = dict(unit=0, evac=0, half=0)
        segments = [places[name] for name in ORDER]
        n_units = sum(n for _, n in segments)

        loads = [sem("loads"), 0]
        small = {}

        def load(name, stack=ctx):
            a = io[name]
            small[name] = sb(stack, name + "_sb", list(a.shape))
            return q.dma("act", [], small[name][:], a, loads)

        load("ident")
        load("half")
        for name in ("cond", "ada_b", "norm_g", "ones", "cdft", "tdft"):
            load(name)
        stat = sb(ctx, "stat", [P, 2, 16])
        attn_p = sb(ctx, "attn_p", [P, 2, 512])
        attn_pt = sb(ctx, "attn_pt", [P, 2, 512])
        bufs = dict(p=[attn_p[:, i, :] for i in range(2)], pt=[attn_pt[:, i, :] for i in range(2)], stat=stat)
        hT = sb(ctx, "hT", [P, KD, S])
        xc = sb(ctx, "xc", [P, KD, S])
        ctxK = sb(ctx, "ctxK", [P, 4, S])
        ctxV = sb(ctx, "ctxV", [P, NB, 512])
        gs = sb(ctx, "gs", [P, 2, 512])
        rs = sb(ctx, "rs", [P, 2, 512])
        mods = sb(ctx, "mods", [P, DEPTH, NMOD * KD, 2])
        gA = sb(ctx, "gA", [P, DEPTH, 3, KD, 2])
        cond = sb(ctx, "cond_s", [P, KD, 2])
        q.dma("act", [], xc[:], io["ctxT"], loads)

        block1 = ExitStack()
        x = sb(block1, "x", [P, NB, D])
        loaded = q.dma("act", [], x[:], io["x"], loads)
        for name in ("causal", "norm1_g", "norm2_g", "final_norm_g", "subln_g", "lam", "b_forget",
                     "tri", "pick", "relb", "w_ff", "keysT", "iota16"):
            loaded = load(name, block1)
        ident = small["ident"]

        def stream(sp):
            u0 = 0
            for start, n in segments:
                def step(i, st, start=start, u0=u0):
                    u = u0 + st
                    if u >= RING:
                        sp.wait_ge(unit_done, i * RING + (u - RING + 1))
                    sp.dma_start(ring[:, u % RING, :], io["stream"][i * RING + start + st]
                                 ).then_inc(slot_full[u % RING], 16)
                turns(sp, n, step, head=0 if u0 else RING)
                u0 += n
        q.part("sp", [], stream)

        def unit_wait(eng, u0, i, st):
            u = u0 + st
            eng.wait_ge(slot_full[u % RING], (i + (u // RING + 1)) * 16)
            return ring[:, u % RING, :]

        def project(after, n, mms, evacs, dve_evac=False):
            u0, e0 = state["unit"], state["evac"]
            state["unit"] += n
            state["evac"] += n

            def pe_part(eng):
                def step(i, st):
                    w = unit_wait(eng, u0, i, st)
                    eng.wait_ge(evac, i * RING + max(0, e0 + st - 3))
                    out = bank[st % 4]
                    for cols, terms in mms(w, st):
                        for t, (lhsT, rhs) in enumerate(terms):
                            last = eng.matmul(out[:, cols], lhsT, rhs, start=(t == 0), stop=(t == len(terms) - 1))
                    last.then_inc(unit_done, 1)
                turns(eng, n, step, head=4 if n >= 4 else 0)
            q.part("pe", after, pe_part)

            def out_part(eng):
                def step(i, st):
                    eng.wait_ge(unit_done, i * RING + (u0 + st + 1))
                    evacs(eng, bank[st % 4], i * RING + st).then_inc(evac, 1)
                turns(eng, n, step, head=4 if n >= 4 else 0)
            q.part("dve" if dve_evac else "act", after, out_part)
            return [(evac, e0 + n)]

        def two_heads(e, bk, dst, t, first, T):
            for m in range(2):
                last = e.activation(dst[:, first + 2 * t + m, 0:T], bk[:, 0:T], ACT.Copy, scale=small["half"][:, m:m + 1])
            return last

        def feature_major(w, actT, cols, kt=KD, first=0):
            return [(slice(0, cols.stop - cols.start),
                     [(w[:, (first + k) * P:(first + k + 1) * P], actT[:, k, cols]) for k in range(kt)])]

        def token_major(after, n, act_of, width, kpu, blocks):
            u0 = state["unit"]
            state["unit"] += n

            def pe_part(eng):
                for st in range(n):
                    w = unit_wait(eng, u0, 0, st)
                    for kk in range(kpu):
                        k = st * kpu + kk
                        for b in range(blocks):
                            for c in range(width // 512):
                                last = eng.matmul(bank[b * (width // 512) + c][:, :], act_of(k, b),
                                                  w[:, kk * width + c * 512:kk * width + (c + 1) * 512],
                                                  start=(k == 0), stop=(k == n * kpu - 1))
                    last.then_inc(unit_done, 1)
            q.part("pe", after, pe_part)
            return [(unit_done, u0 + n)]

        def unit_mm(tokens, mms):
            u0 = state["unit"]
            state["unit"] += 1

            def part(eng):
                w = unit_wait(eng, u0, 0, 0)
                for o, a, b, first, last_ in mms(w):
                    last = eng.matmul(o, a, b, start=first, stop=last_)
                last.then_inc(unit_done, 1)
            q.part("pe", tokens, part)
            return (unit_done, u0 + 1)

        def attention(after, jobs, bufs):
            hist = []
            for n, job in enumerate(jobs):
                g, nk = job["g"], job["nk"]
                lb, tb, ob = bank[n % 2], bank[2 + n % 2], bank[4 + n % 2]
                pr, pt = bufs["p"][n % 2], bufs["pt"][n % 2]
                mx, sm = bufs["stat"][:, n % 2, 0:g], bufs["stat"][:, n % 2, 4:4 + g]
                rc = bufs["stat"][:, n % 2, 8:8 + g]
                old = hist[n - 2] if n >= 2 else None
                lw = after + (old["exp"] if old else [])
                mm = []
                parts = job["logits"]
                wide = g * nk // len(parts)
                for gg, terms in enumerate(parts):
                    for t, (lhsT, rhs) in enumerate(terms):
                        mm.append(lambda e, o=lb[:, gg * wide:(gg + 1) * wide], a=lhsT, b=rhs, s=(t == 0),
                                  z=(t == len(terms) - 1): e.matmul(o, a, b, start=s, stop=z))
                lg = q.many("pe", lw, mm)
                l3 = lb[:, 0:g * nk].rearrange("p (g k) -> p g k", g=g)
                mt = dve([lg] + (old["exp"] + old["w"] if old else []),
                         lambda e, o=mx, i=l3: e.tensor_reduce(o, i, AX, ALU.max, negate=True))
                ex = []
                for gg in range(g):
                    ex.append(act([mt] + ([old["tr"]] if old else []),
                                  lambda e, o=pr[:, gg * nk:(gg + 1) * nk], i=lb[:, gg * nk:(gg + 1) * nk],
                                  b=mx[:, gg:gg + 1], s=sm[:, gg:gg + 1]:
                                  e.activation(o, i, ACT.Exp, bias=b, accum_out=s)))
                rt = dve([ex[-1]], lambda e, o=rc, i=sm: e.reciprocal(o, i))
                wt = []
                if job.get("mix") is not None:
                    lt = dve([rt], lambda e, o=rc[:, 1:2], m=job["mix"]: e.tensor_scalar(o, o, m, None, ALU.mult))
                    w0 = dve([rt], lambda e, o=pr[:, 0:nk], r=rc[:, 0:1]: e.tensor_scalar(o, o, r, None, ALU.mult))
                    wt = [dve([lt, w0], lambda e, o=pr[:, 0:nk], i=pr[:, nk:2 * nk], r=rc[:, 1:2]:
                              e.scalar_tensor_tensor(out=o, in0=i, scalar=r, in1=o, op0=ALU.mult, op1=ALU.add))]
                    wide = nk
                else:
                    for gg in range(g):
                        wt.append(dve([rt], lambda e, o=pr[:, gg * nk:(gg + 1) * nk], r=rc[:, gg:gg + 1]:
                                      e.tensor_scalar(o, o, r, None, ALU.mult)))
                    wide = g * nk
                nt = wide // P
                hist.append(dict(exp=ex, w=wt, wide=wide, nt=nt, job=job, wt=wt, pr=pr, pt=pt, tb=tb, ob=ob))
                if n >= 1:
                    finish(hist, n - 1)
                yield
            finish(hist, len(jobs) - 1)
            return [hist[-1]["out"], hist[-1]["copy"]] + ([hist[-2]["out"]] if len(hist) > 1 else [])

        def finish(hist, n):
            h = hist[n]
            old = hist[n - 2] if n >= 2 else None
            job, pr, pt, tb, ob, nt = h["job"], h["pr"], h["pt"], h["tb"], h["ob"], h["nt"]
            h["tr"] = q.many("pe", h["wt"] + ([old["copy"]] if old else []), [
                (lambda e, c=c: e.transpose(tb[:, c * P:(c + 1) * P], pr[:, c * P:(c + 1) * P], ident[:]))
                for c in range(nt)])
            h["copy"] = act([h["tr"]] + ([old["pv"]] if old else []),
                            lambda e: e.activation(pt[:, 0:nt * P], tb[:, 0:nt * P], ACT.Copy))
            mm = []
            for orow, terms in job["values"](pt):
                for t, (lhsT, rhs) in enumerate(terms):
                    mm.append(lambda e, o=ob[orow, 0:P], a=lhsT, b=rhs, s=(t == 0), z=(t == len(terms) - 1):
                              e.matmul(o, a, b, start=s, stop=z))
            h["pv"] = q.many("pe", [h["copy"]] + ([old["out"]] if old else []), mm)
            h["out"] = job["out"]([h["pv"]], ob)

        def rstd_of(after, ss, tmp, scale):
            a = dve(after, lambda e: e.tensor_scalar(tmp, ss, scale, EPS, ALU.mult, ALU.add))
            b = act([a], lambda e: e.activation(ss, tmp, ACT.Sqrt))
            c = dve([b], lambda e: e.reciprocal(tmp, ss))
            return dve([c], lambda e: e.tensor_copy(ss, tmp))

        t_tok = sb(block1, "t_tok", [P, NB, D])
        sq = sb(block1, "sq", [P, NB, D])
        qkT = sb(block1, "qkT", [P, 24, S])
        gring = sb(block1, "gring", [P, GROUP, D])
        gateT = gring[:, 0:4, :].rearrange("p a (b t) -> p (a b) t", t=S)
        mergedT = gring[:, 4:6, :].rearrange("p a (b t) -> p (a b) t", t=S)
        v_tok = gring[:, 6:8, :]
        heads = sb(block1, "heads", [P, 2 * ND, S])
        dT, fT1 = heads[:, 0:ND, :], heads[:, ND:2 * ND, :]
        cand = sb(block1, "cand", [P, 2, TOPK * TOPK])
        scores = [qkT[:, 16:24, :].rearrange("p a (b n) -> p (a b) n", n=NKEYS),
                  heads[:, :, :].rearrange("p a (b n) -> p (a b) n", n=NKEYS)]
        ss = sb(block1, "ss", [P, 8])
        ss2 = sb(block1, "ss2", [P, 8])
        fl = sb(block1, "fl", [P, 4, NB * NH])
        cT = sb(block1, "cT", [NH, S])
        lamb = sb(block1, "lamb", [P, 8])
        lprod = sb(block1, "lprod", [P, 2, HD])
        topv = sb(block1, "topv", [P, 2 * PH, TOPK])
        topi = sb(block1, "topi", [P, 2 * PH, TOPK], U32)
        topf = sb(block1, "topf", [P, 2 * PH, TOPK])
        bestv = sb(block1, "bestv", [P, PH, TOPK])
        besti = sb(block1, "besti", [P, PH, TOPK], U32)
        bi2 = sb(block1, "bi2", [P, 2, PH, TOPK], U32)
        bf2 = sb(block1, "bf2", [P, 2, PH, TOPK])
        expf = sb(block1, "expf", [P, NB, SLOTS])
        gates = sb(block1, "gates", [P, NB, SLOTS])
        gsum = sb(block1, "gsum", [P, PH])
        idx = sb(block1, "idx", [P, 2, GROUP], U32)
        pre = sb(block1, "pre", [P, 2, GROUP])
        gel = sb(block1, "gel", [P, GROUP])
        wts = sb(block1, "wts", [P, GROUP])

        def norm_tokens(after, g, out_tok=None, outT=hT, cols=0):
            s0 = [act(after, lambda e, b=b: e.activation(sq[:, b, :], x[:, b, :], ACT.Square,
                                                        accum_out=ss[:, b:b + 1])) for b in range(NB)]
            r = rstd_of(s0, ss[:, 0:NB], ss2[:, 0:NB], 1.0 / D)
            n = [dve([r], lambda e, b=b: e.tensor_scalar(sq[:, b, :], x[:, b, :], ss[:, b:b + 1], None, ALU.mult))
                 for b in range(NB)]
            ends = []
            for b in range(NB):
                for c in range(2):
                    i = b * 2 + c
                    tr = q.many("pe", [n[b]] + after, [
                        (lambda e, i=i, k=k, b=b, c=c: e.transpose(
                            bank[i][:, k * P:(k + 1) * P], sq[:, b, (c * 4 + k) * P:(c * 4 + k + 1) * P], ident[:]))
                        for k in range(4)])
                    for k in range(4):
                        kk = c * 4 + k
                        o, s, gg = outT[:, kk, cols + b * P:cols + (b + 1) * P], bank[i][:, k * P:(k + 1) * P], g[:, kk:kk + 1]
                        if c:
                            ends.append(dve([tr], lambda e, o=o, s=s, gg=gg: e.tensor_scalar(o, s, gg, None, ALU.mult)))
                        else:
                            ends.append(act([tr], lambda e, o=o, s=s, gg=gg: e.activation(o, s, ACT.Copy, scale=gg)))
            if out_tok is not None:
                gr = io_rows["norm2"]
                ends += [dve([n[b]] + gr[1], lambda e, b=b: e.tensor_tensor(out_tok[:, b, :], sq[:, b, :], gr[0], ALU.mult))
                         for b in range(NB)]
            return ends

        g2row = sb(block1, "g2row", [P, D])
        io_rows = {}

        def layer_one(layer, after):
            L = layer
            rowt = q.dma("act", after, g2row[:], io["norm2_rows"][L], loads)
            io_rows["norm2"] = (g2row[:, :], [rowt])
            h = norm_tokens(after, small["norm1_g"][:, L])
            lm = small["lam"]
            a = [dve(after, lambda e, j=j: e.tensor_tensor(lprod[:, j, :], lm[:, L, 2 * j, :], lm[:, L, 2 * j + 1, :], ALU.mult))
                 for j in range(2)]
            a = dve(a, lambda e: e.tensor_reduce(lamb[:, 0:2], lprod[:], AX, ALU.add))
            a = act([a], lambda e: e.activation(lamb[:, 2:4], lamb[:, 0:2], ACT.Exp))
            a = dve([a], lambda e: e.tensor_tensor(lamb[:, 4:5], lamb[:, 3:4], lamb[:, 2:3], ALU.subtract))
            neg_lam = dve([a], lambda e: e.tensor_scalar(lamb[:, 5:6], lamb[:, 4:5], -lam_init(L), None, ALU.add))
            sg = dve([neg_lam], lambda e: e.tensor_scalar(lamb[:, 6:7], small["subln_g"][:, L:L + 1], 1.0 - lam_init(L),
                                                          None, ALU.mult))
            allT = slice(0, S)
            qd = project(h, 8, lambda w, t: feature_major(w, hT, allT),
                         lambda e, b, t: two_heads(e, b, qkT, t, 0, S))
            kd = project([], 8, lambda w, t: feature_major(w, hT, allT),
                         lambda e, b, t: e.activation(qkT[:, t + 16, :], b[:, 0:S], ACT.Copy))
            gd = project([], 16, lambda w, t: feature_major(w, hT, allT),
                         lambda e, b, t: e.activation(gateT[:, t, :], b[:, 0:S], ACT.Sigmoid))
            vd = token_major(gd, KD, lambda k, b: hT[:, k, b * P:(b + 1) * P], D, 1, NB)
            ve = []
            for b in range(NB):
                for c in range(2):
                    f = act if c else dve
                    ve.append(f(vd, lambda e, b=b, c=c: (e.activation(v_tok[:, b, c * 512:(c + 1) * 512], bank[2 * b + c][:], ACT.Copy)
                                                         if c else e.tensor_copy(v_tok[:, b, c * 512:(c + 1) * 512], bank[2 * b + c][:]))))
            ffm = q.many("pe", vd + gd, [
                (lambda e, k=k, b=b: e.matmul(bank[4 + b][:, 0:NH], hT[:, k, b * P:(b + 1) * P], small["w_ff"][:, L, k, :],
                                              start=(k == 0), stop=(k == KD - 1)))
                for b in range(NB) for k in range(KD)])
            z, az, ez, ls = (fl[:, j, :] for j in range(4))
            a = [dve([ffm], lambda e, b=b: e.tensor_tensor(z[:, b * NH:(b + 1) * NH], bank[4 + b][:, 0:NH],
                                                           small["b_forget"][:, L, :], ALU.add)) for b in range(NB)]
            b_ = dve(a, lambda e: e.tensor_scalar(az, z, -1.0, None, ALU.mult))
            b_ = dve([b_], lambda e: e.tensor_tensor(az, az, z, ALU.min))
            b_ = act([b_], lambda e: e.activation(ez, az, ACT.Exp))
            b_ = dve([b_], lambda e: e.tensor_scalar(ez, ez, 1.0, None, ALU.add))
            b_ = act([b_], lambda e: e.activation(az, ez, ACT.Ln))
            b_ = dve([b_], lambda e: e.scalar_tensor_tensor(out=ls, in0=z, scalar=0.0, in1=az, op0=ALU.min, op1=ALU.subtract))
            cm = q.many("pe", [b_], [
                (lambda e, b=b: e.matmul(bank[6][0:NH, 0:S], ls[:, b * NH:(b + 1) * NH], small["tri"][:, b, :],
                                         start=(b == 0), stop=(b == NB - 1))) for b in range(NB)])
            cd = act([cm], lambda e: e.activation(cT[:, :], bank[6][0:NH, 0:S], ACT.Copy))
            ready = ve + [cd, neg_lam, sg] + qd + kd
            jobs = []
            o_tok = sq
            for b in range(NB):
                nk = (b + 1) * P
                for hh in range(ND):
                    def out_diff(t, ob, b=b, hh=hh):
                        c = dve(t, lambda e: e.tensor_copy(o_tok[:, b, hh * P:(hh + 1) * P], ob[:, 0:P]))
                        return act([c], lambda e: e.activation(o_tok[:, b, 512 + hh * P:512 + (hh + 1) * P],
                                                               o_tok[:, b, hh * P:(hh + 1) * P], ACT.Square,
                                                               accum_out=ss[:, b * ND + hh:b * ND + hh + 1]))
                    qs = [qkT[:, 2 * hh + m, b * P:(b + 1) * P] for m in range(2)]
                    ks = qkT[:, 16 + hh, 0:nk]
                    jobs.append(dict(
                        g=2, nk=nk, mix=lamb[:, 5:6],
                        logits=[[(qs[m], ks),
                                 (ident[:], small["relb"][:, hh, S - nk:S])] for m in range(2)],
                        values=lambda pt, b=b, hh=hh: [(slice(0, P), [
                            (pt[:, kb * P:(kb + 1) * P], v_tok[:, kb, hh * P:(hh + 1) * P]) for kb in range(b + 1)])],
                        out=out_diff))
            for b in range(NB):
                nk = (b + 1) * P
                for hp in range(NH // 2):
                    qs = [qkT[:, 8 + 2 * hp + m, b * P:(b + 1) * P] for m in range(2)]
                    ks = qkT[:, 20 + hp, 0:nk]
                    jobs.append(dict(
                        g=2, nk=nk,
                        logits=[[(qs[m], ks),
                                 (ident[:], small["causal"][:, S - nk:S]),
                                 (cT[:, b * P:(b + 1) * P], small["pick"][:, 2 * hp + m:2 * hp + m + 1].to_broadcast([NH, nk])),
                                 (small["pick"][:, NH + 2 * hp + m:NH + 2 * hp + m + 1].to_broadcast([NH, P]), cT[:, 0:nk])] for m in range(2)],
                        values=lambda pt, b=b, hp=hp, nk=nk: [(slice(m * HD, (m + 1) * HD), [
                            (v_tok[:, kb, 512 + (2 * hp + m) * HD:512 + (2 * hp + m + 1) * HD],
                             pt[:, m * nk + kb * P:m * nk + (kb + 1) * P]) for kb in range(b + 1)]) for m in range(2)],
                        out=lambda t, ob, b=b, hp=hp: dve(t, lambda e: e.tensor_copy(
                            fT1[:, hp, b * P:(b + 1) * P], ob[:, 0:P]))))
            at = drain(attention(ready, jobs, bufs))
            r = rstd_of(at, ss[:, 0:8], ss2[:, 0:8], 1.0 / P)
            dd = []
            for b in range(NB):
                n = [dve([r], lambda e, b=b, hh=hh: e.tensor_scalar(
                    o_tok[:, b, hh * P:(hh + 1) * P], o_tok[:, b, hh * P:(hh + 1) * P],
                    ss[:, b * ND + hh:b * ND + hh + 1], None, ALU.mult)) for hh in range(ND)]
                tr = q.many("pe", [n[-1]] + at, [
                    (lambda e, b=b, hh=hh: e.transpose(bank[b][:, hh * P:(hh + 1) * P], o_tok[:, b, hh * P:(hh + 1) * P], ident[:]))
                    for hh in range(ND)])
                dd.append(act([tr], lambda e, b=b: e.activation(
                    dT[:, :, b * P:(b + 1) * P], bank[b][:, :].rearrange("p (h t) -> p h t", h=ND), ACT.Copy,
                    scale=lamb[:, 6:7])))
            ev0 = state["evac"]

            def merge(e, b, t):
                d = mergedT[:, t, :]
                return e.tensor_tensor(d, d, sq[:, 0, 0:S], ALU.add)

            u0, e0 = state["unit"], state["evac"]
            state["unit"] += KD
            state["evac"] += KD

            def merge_pe(eng):
                for st in range(KD):
                    w = unit_wait(eng, u0, 0, st)
                    eng.wait_ge(evac, e0 + st - 3)
                    for j, src in enumerate((dT, fT1)):
                        for k in range(ND):
                            last = eng.matmul(bank[st % 4][:, j * S:(j + 1) * S], w[:, (j * ND + k) * P:(j * ND + k + 1) * P],
                                              src[:, k, :], start=(k == 0), stop=(k == ND - 1))
                    last.then_inc(unit_done, 1)
            q.part("pe", dd + at, merge_pe)
            tok = dd + at
            for st in range(KD):
                bk = bank[st % 4]
                m1 = dve(tok + [(unit_done, u0 + st + 1)], lambda e, st=st, bk=bk: e.tensor_tensor(
                    mergedT[:, st, :], bk[:, 0:S], gateT[:, st, :], ALU.mult))
                m2 = dve([], lambda e, st=st, bk=bk: e.tensor_tensor(
                    sq[:, 0, (st % 2) * S:(st % 2 + 1) * S], bk[:, S:2 * S], gateT[:, KD + st, :], ALU.mult))
                q.part("dve", [m1, m2], lambda e, st=st: e.tensor_tensor(
                    mergedT[:, st, :], mergedT[:, st, :], sq[:, 0, (st % 2) * S:(st % 2 + 1) * S], ALU.add).then_inc(evac, 1))
            od = token_major([(evac, e0 + KD)], KD, lambda k, b: mergedT[:, k, b * P:(b + 1) * P], D, 1, NB)
            xe = []
            for b in range(NB):
                for c in range(2):
                    xs = x[:, b, c * 512:(c + 1) * 512]
                    xe.append(dve(od, lambda e, xs=xs, b=b, c=c: e.tensor_tensor(xs, bank[2 * b + c][:], xs, ALU.add)))
            h = norm_tokens(xe, small["norm2_g"][:, L], out_tok=t_tok)
            qd = project(h, 16, lambda w, t: feature_major(w, hT, allT),
                         lambda e, b, t: e.activation(qkT[:, t, :], b[:, 0:S], ACT.Copy))
            last_block = qd + h
            sc_all = []
            for b in range(NB):
                for j in range(4):
                    m = q.many("pe", last_block, [
                        (lambda e, c=c, j=j, b=b: e.matmul(bank[4 * b + j][:, c * P:(c + 1) * P],
                                                           qkT[:, 4 * j + c, b * P:(b + 1) * P],
                                                           small["keysT"][:, L, (4 * j + c) % 2, :], start=True, stop=True))
                        for c in range(4)])
                    sc_all.append(act([m], lambda e, b=b, j=j: e.activation(
                        scores[b][:, 4 * j:4 * j + 4, :], bank[4 * b + j][:, :].rearrange("p (c n) -> p c n", c=4),
                        ACT.Copy)))
            done = drain(route(0, sc_all))
            if L == 0:
                ada = modulation_mm([loaded, cs] + sc_all)
                side = Steps(chain(route(1, []), context_before_first_ffn(ada), pause=12))
            else:
                side = Steps(chain(route(1, []), mixer_ctx(), pause=0))
            first = gather(L, 0, done, 0, SLOTS // GROUP, side=side)
            d1, ctx_ready = side.finish()
            up = FfnUp(ctx_ready, hT, qkT, S)
            down = up.down(side=True)
            gather(L, 1, d1 + first, 0, up.groups, beside=up)
            last = gather(L, 1, [], up.groups, SLOTS // GROUP - up.groups)
            ctx_done = residuals(down, 0, 2 * L, [CTX])
            return last + [ctx_done]

        def chain(a, b, pause):
            a, b, n = Steps(a), Steps(b), 0
            while a.live or b.live:
                if a.live:
                    a.step()
                if b.live and n >= pause:
                    b.step()
                n += 1
                yield
            return a.result, b.result

        def top16(src, vals, ids, after):
            a = dve(after, lambda e: e.max(out=vals[:, 0:8], in_=src))
            i = dve([a], lambda e: e.max_index(out=ids[:, 0:8], in_max=vals[:, 0:8], in_values=src))
            m = dve([i], lambda e: e.match_replace(out=src, in_to_replace=vals[:, 0:8], in_values=src, imm_value=-3e38))
            a = dve([m], lambda e: e.max(out=vals[:, 8:16], in_=src))
            return dve([a], lambda e: e.max_index(out=ids[:, 8:16], in_max=vals[:, 8:16], in_values=src))

        def route(b, after):
            ends = []
            for hp in range(2 * PH):
                ends = [top16(scores[b][:, hp, :], topv[:, hp, :], topi[:, hp, :], after)]
                after = []
                if hp % 2:
                    yield
            f = dve(ends, lambda e: e.tensor_copy(topf[:], topi[:]))
            for h in range(PH):
                c3 = cand[:, h % 2, :].rearrange("p (i j) -> p i j", i=TOPK)
                v1 = topv[:, 2 * h, :].unsqueeze(2).to_broadcast([P, TOPK, TOPK])
                v2 = topv[:, 2 * h + 1, :].unsqueeze(1).to_broadcast([P, TOPK, TOPK])
                c = dve(ends, lambda e, c3=c3, v1=v1, v2=v2: e.tensor_tensor(c3, v1, v2, ALU.add))
                g = top16(cand[:, h % 2, :], bestv[:, h, :], besti[:, h, :], [c])
                if h % 2:
                    yield
            a = dve([g], lambda e: e.tensor_scalar(bi2[:, 0], besti[:], 4, None, ALU.logical_shift_right))
            c = dve([g], lambda e: e.tensor_scalar(bi2[:, 1], besti[:], 15, None, ALU.bitwise_and))
            a = dve([a, c], lambda e: e.tensor_copy(bf2[:], bi2[:]))
            oh = scores[b].rearrange("p a n -> p (a n)").rearrange("p (h s j) -> p h s j", h=PH, s=TOPK)
            t3 = topf[:, :, :].rearrange("p (h two) j -> p h two j", two=2)
            for half in range(2):
                sel = bf2[:, half].unsqueeze(3).to_broadcast([P, PH, TOPK, TOPK])
                io4 = small["iota16"][:, :].unsqueeze(1).unsqueeze(1).to_broadcast([P, PH, TOPK, TOPK])
                src = t3[:, :, half, :].unsqueeze(2).to_broadcast([P, PH, TOPK, TOPK])
                c = dve([a, f], lambda e, sel=sel, io4=io4: e.tensor_tensor(oh, sel, io4, ALU.is_equal))
                c = dve([c], lambda e, src=src: e.tensor_tensor(oh, oh, src, ALU.mult))
                a = dve([c], lambda e, half=half: e.tensor_reduce(bf2[:, half], oh, AX, ALU.add))
            ex = expf[:, b, :].rearrange("p (h s) -> p h s", h=PH)
            a = dve([a], lambda e: e.scalar_tensor_tensor(out=ex, in0=bf2[:, 0], scalar=float(NKEYS), in1=bf2[:, 1],
                                                          op0=ALU.mult, op1=ALU.add))
            gt = gates[:, b, :].rearrange("p (h s) -> p h s", h=PH)
            c = dve([g], lambda e: e.tensor_tensor(gt, bestv[:], bestv[:, :, 0:1].to_broadcast([P, PH, TOPK]), ALU.subtract))
            c = act([c], lambda e: e.activation(gates[:, b, :], gates[:, b, :], ACT.Exp))
            c = dve([c], lambda e: e.tensor_reduce(gsum[:], gt, AX, ALU.add))
            c = dve([c], lambda e: e.reciprocal(gsum[:], gsum[:]))
            c = dve([c], lambda e: e.tensor_tensor(gt, gt, gsum[:].unsqueeze(2).to_broadcast([P, PH, TOPK]), ALU.mult))
            return [a, c]

        row_full = [sem(f"row_full{i}") for i in range(GROUP)]
        rows_used, g_idx, g_gel, g_wts, g_iss = (sem(n) for n in (
            "rows_used", "idx_ready", "gelu_ready", "weights_ready", "gathers_issued"))
        state["g"] = 0
        NG = SLOTS // GROUP

        def gather(L, b, after, first, n, beside=None, side=None):
            g0 = state["g"]
            state["g"] += n
            per = 2 * GROUP

            def used(eng, i, g, value):
                if value + (g0 + g) * per > 0:
                    eng.wait_ge(rows_used, i * (2 * per) + ((g0 + g) * per + value))

            def pool_part(eng):
                def step(i, g):
                    eng.wait_ge(g_idx, i * 2 + (g0 + g + 1))
                    for t, tab in enumerate((io[f"expert_u{L}"], io[f"expert_v{L}"])):
                        for s in range(GROUP):
                            used(eng, i, g, (t - 1) * GROUP + s + 1)
                            eng.sem_inc(g_iss, 1)
                            eng.indirect_dma_start(
                                out=gring[:, s, :], out_offset=None, in_=tab,
                                in_offset=bass.IndirectOffsetOnAxis(ap=idx[:, (first + g) % 2, s:s + 1], axis=0)
                            ).then_inc(row_full[s], 16)
                turns(eng, n, step, head=1 if n % 2 else 2, width=2)
            q.part("pool", after, pool_part)

            def take(eng, i, g):
                used(eng, i, g - 1, 0)
                eng.activation(idx[:, (first + g) % 2, :], expf[:, b, bass.ds(i * (2 * GROUP) + (first + g) * GROUP, GROUP)],
                               ACT.Copy).then_inc(g_idx, 1)

            def act_step(eng, i, g):
                if first + g < NG - 1:
                    take(eng, i, g + 1)
                if beside:
                    beside.act(eng, i, g)
                used(eng, i, g, GROUP)
                if g0 + g > 0:
                    eng.wait_ge(g_wts, i * 2 + (g0 + g))
                eng.activation(gel[:], pre[:, (first + g) % 2, :], ACT.Gelu).then_inc(g_gel, 1)

            def dve_step(eng, i, g):
                for s in range(GROUP):
                    eng.wait_ge(row_full[s], i * 64 + (2 * (g0 + g) + 1) * 16)
                    eng.tensor_tensor_reduce(out=gring[:, s, :], in0=gring[:, s, :], in1=t_tok[:, b, :],
                                             scale=1.0, scalar=0.0, op0=ALU.mult, op1=ALU.add,
                                             accum_out=pre[:, (first + g) % 2, s:s + 1]).then_inc(rows_used, 1)
                if beside:
                    beside.dve(eng, i, g)
                eng.wait_ge(g_gel, i * 2 + (g0 + g + 1))
                used(eng, i, g, 0)
                eng.tensor_tensor(wts[:], gel[:], gates[:, b, bass.ds(i * (2 * GROUP) + (first + g) * GROUP, GROUP)],
                                  ALU.mult).then_inc(g_wts, 1)
                eng.wait_ge(g_wts, i * 2 + (g0 + g + 1))
                for s in range(GROUP):
                    eng.wait_ge(row_full[s], i * 64 + (2 * (g0 + g) + 2) * 16)
                    used(eng, i, g, GROUP + s)
                    eng.scalar_tensor_tensor(out=x[:, b, :], in0=gring[:, s, :], scalar=wts[:, s:s + 1],
                                             in1=x[:, b, :], op0=ALU.mult, op1=ALU.add).then_inc(rows_used, 1)

            if first == 0:
                q.part("act", after, lambda eng: take(eng, 0, 0))
            if side is None:
                q.part("act", after, lambda eng: turns(eng, n, lambda i, g: act_step(eng, i, g), head=1 if n % 2 else 2,
                                                       tail=2 if first + n == NG else 0, width=2))
                q.part("dve", after, lambda eng: turns(eng, n, lambda i, g: dve_step(eng, i, g), head=1 if n % 2 else 2, width=2))
            else:
                for g in range(n):
                    q.part("act", after, lambda eng, g=g: act_step(eng, 0, g))
                    q.part("dve", after, lambda eng, g=g: dve_step(eng, 0, g))
                    if g < n - 1 and side.live:
                        side.step()
            return [(rows_used, (g0 + n) * per), (g_gel, g0 + n), (g_wts, g0 + n)]

        LAT, CTX = 0, 1
        xs = [hT, xc]
        onesT = {D: small["ones"][:, 0, :], 384: small["ones"][:, 1, :], P: small["ones"][:, 2, :]}

        def feature_rstd(after, tiles, T):
            mm = []
            for k, tile_ in enumerate(tiles):
                a = act(after + (mm[k - 2:k - 1] if k >= 2 else []),
                        lambda e, k=k, t=tile_: e.activation(gs[:, k % 2, 0:T], t, ACT.Square))
                mm.append(pe([a] + after, lambda e, k=k, n=len(tiles): e.matmul(
                    bank[7][:, 0:T], onesT[n * P], gs[:, k % 2, 0:T], start=(k == 0), stop=(k == n - 1))))
            a = dve([mm[-1]] + after, lambda e: e.tensor_scalar(rs[:, 1, 0:T], bank[7][:, 0:T], EPS, None, ALU.add))
            a = act([a], lambda e: e.activation(rs[:, 0, 0:T], rs[:, 1, 0:T], ACT.Sqrt))
            return dve([a], lambda e: e.reciprocal(rs[:, 1, 0:T], rs[:, 0, 0:T]))

        def mod_norm(after, L, j, streams, out):
            ends = []
            for n, s in enumerate(streams):
                r = feature_rstd(after + ends[-1:], [xs[s][:, k, :] for k in range(KD)], S)
                old = [r]
                for k in range(KD):
                    a = dve([r] + ends[-2:-1], lambda e, k=k, s=s: e.tensor_tensor(
                        gs[:, k % 2, 0:S], xs[s][:, k, :], rs[:, 1, 0:S], ALU.mult))
                    ends.append(act([a], lambda e, k=k, s=s, n=n: e.activation(
                        out[:, k, n * S:(n + 1) * S], gs[:, k % 2, 0:S], ACT.Identity,
                        bias=mods[:, L, 3 * j * KD + k, s:s + 1], scale=gA[:, L, j, k, s:s + 1])))
            return [ends[-1]]

        def residual(after, L, j, streams, k, bk):
            for n, s in enumerate(streams):
                r = dve(after, lambda e, n=n, s=s: e.scalar_tensor_tensor(
                    out=xs[s][:, k, :], in0=bk[:, n * S:(n + 1) * S], scalar=mods[:, L, (3 * j + 2) * KD + k, s:s + 1],
                    in1=xs[s][:, k, :], op0=ALU.mult, op1=ALU.add))
            return r

        def residuals(after, L, j, streams):
            return [residual(after, L, j, streams, k, bank[k]) for k in range(KD)][-1]

        class FfnUp:

            def __init__(self, after, h, f, T):
                self.h, self.f, self.T, self.after = h, f, T, after
                self.u0, self.e0, self.h0 = state["unit"], state["evac"], state["half"]
                state["unit"] += 3 * KF
                state["evac"] += KF
                state["half"] += KF
                self.groups = KF // 2
                q.part("pe", after, self.pe)

            def place(self, st):
                if self.T == S:
                    return bank[(st // 2) % 4][:, (st % 2) * S:(st % 2 + 1) * S]
                return bank[st % 4][:, 0:self.T]

            def pe(self, eng):
                deep = 4 if self.T == S else 2

                def step(i, st):
                    w = unit_wait(eng, self.u0, i, st)
                    if st % 2 == 0:
                        eng.wait_ge(evac, i * (RING // 2) + (self.e0 + max(0, st // 2 - deep + 1)))
                    for k in range(KD):
                        last = eng.matmul(self.place(st), w[:, k * P:(k + 1) * P], self.h[:, k, 0:self.T],
                                          start=(k == 0), stop=(k == KD - 1))
                    last.then_inc(unit_done, 1)
                turns(eng, 2 * KF, step, head=4)

            def act_tile(self, eng, i, m):
                eng.wait_ge(unit_done, i * RING + (self.u0 + 2 * m + (2 if self.T == S else 1)))
                eng.wait_ge(evac, i * (RING // 2) + (self.e0 + max(0, m - 1)))
                eng.activation(gs[:, m % 2, 0:self.T], self.place(2 * m), ACT.Silu).then_inc(half_done, 1)

            def dve_tile(self, eng, i, m):
                eng.wait_ge(unit_done, i * RING + (self.u0 + 2 * m + 2))
                eng.wait_ge(half_done, i * (RING // 2) + (self.h0 + m + 1))
                eng.tensor_tensor(self.f[:, i * (RING // 2) + m, 0:self.T], gs[:, m % 2, 0:self.T], self.place(2 * m + 1),
                                  ALU.mult).then_inc(evac, 1)

            def act(self, eng, i, g):
                self.act_tile(eng, i, 2 * g)
                self.act_tile(eng, i, 2 * g + 1)

            def dve(self, eng, i, g):
                self.dve_tile(eng, i, 2 * g)
                self.dve_tile(eng, i, 2 * g + 1)

            def alone(self):
                q.part("act", self.after, lambda eng: turns(eng, KF, lambda i, m: self.act_tile(eng, i, m), head=2,
                                                            width=RING // 2))
                q.part("dve", self.after, lambda eng: turns(eng, KF, lambda i, m: self.dve_tile(eng, i, m), head=2,
                                                            width=RING // 2))
                return self

            def down(self, side=False):
                d0 = self.u0 + 2 * KF

                def part(eng):
                    def step(i, st):
                        w = unit_wait(eng, d0, i, st)
                        for m in range(KD):
                            last = eng.matmul(bank[m][:, 0:self.T], w[:, m * P:(m + 1) * P],
                                              self.f[:, i * RING + st, 0:self.T], start=(st == 0),
                                              stop=(isinstance(i, int) and st == KF - 1))
                        last.then_inc(unit_done, 1)
                    turns(eng, KF, step, head=3, tail=3)
                q.part("pe", [(evac, self.e0 + KF), (half_done, self.h0 + KF)], part)
                return [(unit_done, d0 + KF)]

        def ffn(after, L, j, streams, h, f):
            hh = mod_norm(after, L, j, streams, h)
            up = FfnUp(hh, h, f, S * len(streams))
            return [residuals(up.alone().down() + hh, L, j, streams)]

        cs = act([loaded], lambda e: e.activation(cond[:], small["cond"][:], ACT.Silu))

        def modulation_mm(after):
            n = DEPTH * NMOD * KD
            u0 = state["unit"]
            state["unit"] += n

            def part(eng):
                def step(i, st):
                    w = unit_wait(eng, u0, i, st)
                    for k in range(KD):
                        last = eng.matmul(bank[0][:, bass.ds(i * (2 * RING) + 2 * st, 2)], w[:, k * P:(k + 1) * P],
                                          cond[:, k, :], start=(k == 0), stop=(k == KD - 1))
                    last.then_inc(unit_done, 1)
                turns(eng, n, step)
            q.part("pe", after, part)
            return [(unit_done, u0 + n)]

        def modulation(after):
            n = NMOD * KD
            for L in range(DEPTH):
                a = dve(after, lambda e, L=L: e.tensor_tensor(
                    mods[:, L], bank[0][:, 2 * n * L:2 * n * (L + 1)].rearrange("p (n s) -> p n s", s=2),
                    small["ada_b"][:, L, :].unsqueeze(2).to_broadcast([P, n, 2]), ALU.add))
                for j in range(3):
                    b = dve([a], lambda e, j=j, L=L: e.tensor_scalar(gA[:, L, j], mods[:, L, (3 * j + 1) * KD:(3 * j + 2) * KD, :],
                                                                    1.0, None, ALU.add))
                    r = dve([b], lambda e, j=j, L=L: e.tensor_tensor(
                        gA[:, L, j], gA[:, L, j], small["norm_g"][:, L, j, :].unsqueeze(2).to_broadcast([P, KD, 2]), ALU.mult))
                    if j != 1:
                        gate = mods[:, L, (3 * j + 2) * KD:(3 * j + 3) * KD, :]
                        r = dve([a], lambda e, gate=gate: e.tensor_scalar(gate, gate, 0.5, None, ALU.mult))
            return [r]

        def context_before_first_ffn(ada):
            m = modulation(ada)
            yield
            return mod_norm(m, 0, 0, [CTX], hT)

        def mixer_ctx():
            r = yield from mixer_ab([], CTX, hT, qkT, hT)
            return mod_norm(r, 0, 2, [CTX], hT)

        def back(after, L, streams, src):
            T = S * len(streams)
            for st in range(KD):
                t = unit_mm(after, lambda w, st=st: [(bank[st][:, 0:T], w[:, k * P:(k + 1) * P], src(k), k == 0, k == KD - 1)
                                                     for k in range(KD)])
                r = residual(after + [t], L, 1, streams, st, bank[st])
                yield
            return [r]

        def mixer_ab(after, s, h, f, y):
            n = mod_norm(after, 0, 1, [s], h)
            kt = ctxK if s == CTX else f[:, 12:16, :]
            vt = ctxV if s == CTX else f[:, 16:20, :].rearrange("p (b c) t -> p b (c t)", b=NB)
            yield
            ev, tiles = [], []
            for t in range(12):
                m = unit_mm(n + ev[t - 4:t - 3] if t >= 4 else n, lambda w, t=t: [
                    (bank[t % 4][:, 0:S], w[:, k * P:(k + 1) * P], h[:, k, 0:S], k == 0, k == KD - 1) for k in range(KD)])
                bk = bank[t % 4][:, 0:S]
                if t < 4:
                    ev.append(act([m], lambda e, t=t, bk=bk: e.activation(f[:, t, :], bk, ACT.Copy)))
                elif t < 8:
                    for head in range(2):
                        e_ = act([m], lambda e, t=t, bk=bk, head=head: e.activation(
                            f[:, 4 + 2 * (t - 4) + head, :], bk, ACT.Copy, scale=small["half"][:, head:head + 1]))
                    ev.append(e_)
                else:
                    ev.append(act([m], lambda e, t=t, bk=bk: e.activation(kt[:, t - 8, :], bk, ACT.Copy)))
                if t % 2:
                    yield
            for i in range(4):
                vm = unit_mm(n, lambda w, i=i: [(bank[4 + b][:, :], h[:, 2 * i + kk, b * P:(b + 1) * P],
                                                 w[:, kk * 512:(kk + 1) * 512], i == 0 and kk == 0, i == 3 and kk == 1)
                                                for kk in range(2) for b in range(NB)])
            ve = [act([vm], lambda e, b=b: e.activation(vt[:, b, :], bank[4 + b][:], ACT.Copy)) for b in range(NB)]
            yield
            cd, td = small["cdft"], small["tdft"]
            ready = ev[-4:] + ve
            out, second = [], []
            for g in range(4):
                bk, bo, buf = bank[g % 2], bank[2 + g % 2], attn_p[:, g % 2, :]
                m = q.many("pe", ready + second[g - 2:g - 1] * (g >= 2), [
                    (lambda e, b=b, g=g, bk=bk: e.matmul(bk[:, b * 256:(b + 1) * 256], f[:, g, b * P:(b + 1) * P], cd[:, :],
                                                         start=True, stop=True)) for b in range(NB)])
                c = dve([m] + (second[g - 2:g - 1] if g >= 2 else []), lambda e, bk=bk, buf=buf: e.tensor_copy(buf, bk[:]))
                second.append(q.many("pe", [c] + (out[g - 2:g - 1] if g >= 2 else []), [
                    (lambda e, b=b, r=r, bo=bo, buf=buf: e.matmul(
                        bo[:, 0:S], buf[:, b * 256 + r * P:b * 256 + (r + 1) * P], td[:, b, r, :],
                        start=(b == 0 and r == 0), stop=(b == 1 and r == 1))) for b in range(NB) for r in range(2)]))
                out.append(act([second[-1]] + ready, lambda e, g=g, bo=bo: e.activation(y[:, g, 0:S], bo[:, 0:S], ACT.Copy)))
                yield
            jobs = []
            for b in range(NB):
                if s == LAT:
                    for hh in range(NH):
                        r_ = slice((hh % 2) * HD, (hh % 2 + 1) * HD)
                        qs = f[:, 4 + hh, b * P:(b + 1) * P]
                        jobs.append(dict(
                            g=1, nk=2 * S,
                            logits=[[(qs, kt[:, hh // 2, :]), (ident[:], small["na_bias"][:, b * NH + hh, :])],
                                    [(qs, ctxK[:, hh // 2, :])]],
                            values=lambda pt, hh=hh: [(slice(0, HD), [
                                ((vt if kb < NB else ctxV)[:, kb % NB, hh * HD:(hh + 1) * HD], pt[:, kb * P:(kb + 1) * P])
                                for kb in range(4)])],
                            out=lambda t, ob, b=b, hh=hh, r_=r_: dve(t, lambda e: e.tensor_copy(
                                y[r_, 4 + hh // 2, b * P:(b + 1) * P], ob[0:HD, 0:P]))))
                else:
                    for hp in range(NH // 2):
                        jobs.append(dict(
                            g=2, nk=S,
                            logits=[[(f[:, 4 + 2 * hp + m, b * P:(b + 1) * P], kt[:, hp, :])] for m in range(2)],
                            values=lambda pt, hp=hp: [(slice(m * HD, (m + 1) * HD), [
                                (vt[:, kb, (2 * hp + m) * HD:(2 * hp + m + 1) * HD],
                                 pt[:, m * S + kb * P:m * S + (kb + 1) * P]) for kb in range(2)]) for m in range(2)],
                            out=lambda t, ob, b=b, hp=hp: dve(t, lambda e: e.tensor_copy(
                                y[:, 4 + hp, b * P:(b + 1) * P], ob[:, 0:P]))))
            at = yield from attention(out[-2:] + ready, jobs, bufs)
            return (yield from back(at, 0, [s], lambda k: y[:, k, 0:S]))

        def mixer_mla(after):
            h = mod_norm(after, 1, 1, [LAT, CTX], hT2)
            both = slice(0, 2 * S)
            cq = lambda k: fT[:, k, 0:S]
            ckv = fT[:, 3, :]
            kr = fT[:, 4, :]
            a = project(h, 5, lambda w, t: feature_major(w, hT2, both),
                        lambda e, b, t: e.activation(fT[:, t, :], b[:, :], ACT.Copy))
            r = feature_rstd(a, [fT[:, k, 0:S] for k in range(3)], S)
            n = [dve([r], lambda e, k=k: e.scalar_tensor_tensor(
                out=fT[:, k, 0:S], in0=fT[:, k, 0:S], scalar=small["mla_gq"][:, k:k + 1], in1=rs[:, 1, 0:S],
                op0=ALU.mult, op1=ALU.mult)) for k in range(3)]
            r = feature_rstd([n[-1]], [fT[:, 3, :]], 2 * S)
            n2 = dve([r], lambda e: e.scalar_tensor_tensor(
                out=fT[:, 3, :], in0=fT[:, 3, :], scalar=small["mla_gkv"][:, 0:1], in1=rs[:, 1, :],
                op0=ALU.mult, op1=ALU.mult))
            sc = (P + HD) ** -0.5
            u_q = project([n2], 8, lambda w, t: [(slice(m * S, (m + 1) * S), [
                (w[:, m * 384 + k * P:m * 384 + (k + 1) * P], fT[:, k, 0:S]) for k in range(3)]) for m in range(2)],
                lambda e, b, t: e.activation(fT[:, t + 5, :], b[:, :], ACT.Copy, scale=sc))
            qt = lambda m: fT[:, 5 + m // 2, (m % 2) * S:(m % 2 + 1) * S]
            u0 = state["unit"]
            state["unit"] += 2
            kt_ = lambda hh: hT2[:, hh, :]
            ke = []

            def kpart(eng):
                w = unit_wait(eng, u0, 0, 0)
                for hh in range(KD):
                    last = eng.matmul(bank[hh][:, :], w[:, hh * P:(hh + 1) * P], ckv, start=True, stop=True)
                last.then_inc(unit_done, 1)
            q.part("pe", u_q, kpart)
            ke = [(act if hh % 2 else dve)([(unit_done, u0 + 1)] + a, lambda e, hh=hh: (
                e.activation(kt_(hh), bank[hh][:], ACT.Copy) if hh % 2 else e.tensor_copy(kt_(hh), bank[hh][:])))
                for hh in range(KD)]

            def vpart(eng):
                w = unit_wait(eng, u0, 0, 1)
                for b in range(4):
                    for c in range(2):
                        last = eng.matmul(bank[2 * b + c][:, :], ckv[:, b * P:(b + 1) * P], w[:, c * 512:(c + 1) * 512],
                                          start=True, stop=True)
                last.then_inc(unit_done, 1)
            q.part("pe", ke[-2:], vpart)
            vt = lambda b, hh: fT[:, 13 + 2 * b + hh // 4, (hh % 4) * P:(hh % 4 + 1) * P]
            ve = [(act if c else dve)([(unit_done, u0 + 2)], lambda e, b=b, c=c: (
                e.activation(fT[:, 13 + 2 * b + c, :], bank[2 * b + c][:], ACT.Copy) if c
                else e.tensor_copy(fT[:, 13 + 2 * b + c, :], bank[2 * b + c][:]))) for b in range(4) for c in range(2)]
            rope = small["rope"]
            ends = []
            for n_, t_ in enumerate([qt(8 + m) for m in range(8)] + [kr[:, 0:S]]):
                m = pe(ve[-2:] + ke[-2:] + (ends[n_ - 4:n_ - 3] if n_ >= 4 else []),
                       lambda e, n_=n_, t_=t_: e.matmul(bank[n_ % 4][:, 0:S], small["rotm"][:, :], t_, start=True, stop=True))
                c = dve([m] + ends[-1:], lambda e, n_=n_: e.tensor_tensor(gs[:, n_ % 2, 0:S], bank[n_ % 4][:, 0:S], rope[:, 1, :], ALU.mult))
                d = dve([m], lambda e, t_=t_: e.tensor_tensor(t_, t_, rope[:, 0, :], ALU.mult))
                ends.append(dve([c, d], lambda e, n_=n_, t_=t_: e.tensor_tensor(t_, t_, gs[:, n_ % 2, 0:S], ALU.add)))
            oT = lambda hh: attn_o[:, hh, :]
            jobs = []
            for b in range(NB):
                for hh in range(NH):
                    r_ = slice((hh % 2) * HD, (hh % 2 + 1) * HD)
                    jobs.append(dict(
                        g=1, nk=2 * S,
                        logits=[[(qt(hh)[:, b * P:(b + 1) * P], kt_(hh)),
                                 (qt(8 + hh)[:, b * P:(b + 1) * P], kr)]],
                        values=lambda pt, hh=hh: [(slice(0, P), [
                            (vt(kb, hh), pt[:, kb * P:(kb + 1) * P]) for kb in range(4)])],
                        out=lambda t, ob, b=b, hh=hh: dve(t, lambda e: e.tensor_copy(
                            attn_o[:, hh, b * P:(b + 1) * P], ob[:, 0:P]))))
            at = drain(attention(ends + ve + ke, jobs, bufs))
            return drain(back(at, 1, [LAT], lambda k: attn_o[:, k, :]))

        done = [loaded]
        for layer in range(DEPTH):
            done = layer_one(layer, done)

        h = norm_tokens(done, small["final_norm_g"])
        block1.close()
        hT2 = sb(ctx, "hT2", [P, KD, 2 * S])
        fT = sb(ctx, "fT", [P, KF, 2 * S])
        fT_one = fT[:, 0:KF // 2, :].rearrange("p a (b t) -> p (a b) t", t=S)
        hT_one = hT2[:, 0:4, :].rearrange("p a (b t) -> p (a b) t", t=S)
        attn_o = sb(ctx, "attn_o", [P, NH, S])
        loads2 = [sem("loads2"), 0]
        for name in ("na_bias", "mla_gq", "mla_gkv", "rope", "rotm", "final_g"):
            a = io[name]
            small[name] = sb(ctx, name + "_sb", list(a.shape))
            l2 = q.dma("act", h, small[name][:], a, loads2)
        done = ffn(h, 0, 0, [LAT], hT_one, fT_one)
        done = drain(mixer_ab(done + [l2], LAT, hT_one, fT_one, hT_one))
        done = ffn(done, 0, 2, [LAT], hT_one, fT_one)
        done = ffn(done, 1, 0, [LAT, CTX], hT2, fT)
        done = mixer_mla(done)
        done = ffn(done, 1, 2, [LAT], hT_one, fT_one)
        r = feature_rstd(done, [xs[LAT][:, k, :] for k in range(KD)], S)
        f = [dve([r], lambda e, k=k: e.scalar_tensor_tensor(
            out=hT_one[:, k, :], in0=xs[LAT][:, k, :], scalar=small["final_g"][:, k:k + 1], in1=rs[:, 1, 0:S],
            op0=ALU.mult, op1=ALU.mult)) for k in range(KD)]
        stored = [sem("stored"), 0]
        o = q.dma("act", f, io["out"], hT_one, stored)
        q.part("act", [o], lambda e: None)
        assert state["unit"] == n_units, (state["unit"], n_units)

        block = ctx.enter_context(nc.Block())
        for name, deco in (("sp", block.sync), ("pe", block.tensor), ("act", block.scalar),
                           ("dve", block.vector), ("pool", block.gpsimd)):
            @deco
            def _(eng, name=name):
                for run in q.work[name]:
                    run(eng)


def _tiles(w):
    K, M = w.shape
    return w.reshape(K // P, P, M // P, P).transpose(2, 1, 0, 3).reshape(M // P, P, K)


def _rows(w, kpu=1):
    K, N = w.shape
    return w.reshape(K // P // kpu, kpu, P, N).transpose(0, 2, 1, 3).reshape(-1, P, kpu * N)


def _cols(a):
    a = np.asarray(a)
    b = a.reshape(a.shape[:-1] + (a.shape[-1] // P, P))
    return np.ascontiguousarray(np.moveaxis(b, -1, 0))


def _bucket(dist):
    n = np.maximum(dist, 0)
    nf = np.maximum(n, 1).astype(np.float32)
    large = 16 + (np.log(nf / np.float32(16)) / np.float32(math.log(8)) * np.float32(16)).astype(np.int32)
    return np.where(n < 16, n, np.minimum(large, 31))


def _layout(v):
    f = np.float32
    runs = {}
    for L in range(DEPTH):
        w = v["w_in"][L]
        dq, dk, dv, fq, fk, fv = (w[:, i * 512:(i + 1) * 512] for i in range(6))
        g = w[:, 3080:]
        runs[f"one{L}"] = [_tiles(dq), _tiles(fq), _tiles(dk), _tiles(fk), _tiles(g),
                           _rows(np.concatenate([dv, fv], 1)),
                           np.concatenate([_tiles(v["w_diff_o"][L]), _tiles(v["w_fox_o"][L])], 2),
                           _rows(v["w_out"][L]), _tiles(v["w_query"][L])]
        runs[f"ada{L}"] = [_tiles(v["ada_w_2"][L])]
        for j in range(2):
            gu = np.stack([_tiles(v["ffn_w_gate_2"][L, j]), _tiles(v["ffn_w_up_2"][L, j])], 1)
            runs[f"ffn{L}{j}"] = [gu.reshape(2 * KF, P, UW), _rows(v["ffn_w_down_2"][L, j])]
    ab = v["ab_w_in_2"][0]
    runs["ab"] = [_tiles(ab[:, 0:1536]), _rows(ab[:, 1536:], 2), _tiles(v["ab_w_out_2"][0])]
    wi = v["mla_w_in_2"][0]
    uq = v["mla_w_uq_2"][0].reshape(384, 8, 192)
    wr = np.concatenate([uq[:, :, 128:], np.zeros((384, 8, HD), f)], 2)
    uq = np.concatenate([uq[:, :, :128].reshape(384, 1024), wr.reshape(384, 1024)], 1)
    uq = _tiles(uq).reshape(8, 2, P, 384).transpose(0, 2, 1, 3).reshape(8, P, 768)
    uq = np.concatenate([uq, np.zeros((8, P, UW - 768), f)], 2)
    runs["mla"] = [_tiles(np.concatenate([wi, wi[:, 512:]], 1)), uq,
                   v["mla_w_uk_2"][0][None], v["mla_w_uv_2"][0][None], _tiles(v["mla_w_o_2"][0])]
    places, at = {}, 0
    for name, parts in runs.items():
        n = sum(a.shape[0] for a in parts)
        places[name] = (at, n)
        at += n
    io = {"stream": np.concatenate([a for parts in runs.values() for a in parts], 0)}
    io["x"] = v["x"][0].reshape(NB, P, D).transpose(1, 0, 2)
    io["half"] = np.kron(np.eye(2), np.full((HD, 1), HD ** -0.5)).astype(f)
    io["ident"] = np.eye(P, dtype=f)
    p = np.arange(P)[:, None]
    dist = P + p - np.arange(S)[None]
    io["causal"] = np.where(dist >= 0, 0, NEG).astype(f)
    rel = v["rel_bias"][_bucket(dist)].transpose(0, 2, 1)
    io["relb"] = np.where(dist[:, None, :] >= 0, rel, f(NEG))
    for n in ("norm1_g", "norm2_g", "final_norm_g"):
        io[n] = _cols(v[n])
    io["norm2_rows"] = np.repeat(v["norm2_g"][:, None], P, 1)
    io["subln_g"] = v["diff_subln_g"].T
    io["lam"] = np.repeat(v["diff_lambda"][None], P, 0)
    io["b_forget"] = np.repeat(v["b_forget"][None], P, 0)
    tri = (np.arange(S)[:, None] <= np.arange(S)[None]).astype(f)
    io["tri"] = tri.reshape(NB, P, S).transpose(1, 0, 2)
    io["pick"] = np.concatenate([np.eye(NH), -np.eye(NH)], 1).astype(f)
    io["w_ff"] = v["w_in"][:, :, 3072:3080].reshape(DEPTH, KD, P, NH).transpose(2, 0, 1, 3)
    io["keysT"] = v["sub_keys"].transpose(3, 0, 1, 2)
    io["iota16"] = np.repeat(np.arange(TOPK, dtype=f)[None], P, 0)
    for L in range(DEPTH):
        io[f"expert_u{L}"], io[f"expert_v{L}"] = v["expert_u"][L], v["expert_v"][L]
    io["ctxT"] = v["ctx_2"][0].T.reshape(KD, P, S).transpose(1, 0, 2)
    io["cond"] = np.stack([_cols(v["c_2"][0]), _cols(v["c_ctx_2"])], -1)
    io["ada_b"] = _cols(v["ada_b_2"])
    io["norm_g"] = _cols(v["norm_g_2"])
    io["ones"] = np.stack([np.full((P, P), 1.0 / n, f) for n in (D, 384, P)], 1)
    col = np.arange(64)
    start = np.clip(col - 8, 0, 48)
    inside = (col[None] >= start[:, None]) & (col[None] < start[:, None] + 16)
    off = np.clip(col[None] - col[:, None] + 15, 0, 30)
    row = np.arange(4)[None] - np.arange(4)[:, None] + 7
    rp = v["ab_rpb_2"][0][:, row[:, None, :, None], off[None, :, None, :]]
    rp = np.where(inside[None, None, :, None, :], rp, f(NEG)).reshape(NH, NB, P, S)
    io["na_bias"] = rp.transpose(2, 1, 0, 3).reshape(P, NB * NH, S)
    k = np.arange(P)
    a = 2 * np.pi * ((k[:, None] * k[None]) % P) / P
    io["cdft"] = np.concatenate([np.cos(a), np.sin(a)], 1).astype(f)
    k = np.arange(S)
    a = 2 * np.pi * ((k[:, None] * k[None]) % S) / S
    s = 1 / math.sqrt(S * P)
    td = np.stack([np.cos(a) * s, -np.sin(a) * s], 1).astype(f)
    io["tdft"] = td.reshape(NB, P, 2, S).transpose(1, 0, 2, 3)
    io["mla_gq"] = _cols(v["mla_g_q_2"][0])
    io["mla_gkv"] = _cols(v["mla_g_kv_2"][0])
    pos = np.arange(S)
    inv = f(10000.0) ** (-np.arange(0, 32, 2, dtype=f) / f(32))
    ar, ac = (pos // 64).astype(f)[:, None] * inv, (pos % 64).astype(f)[:, None] * inv
    ang = np.concatenate([ar, ar, ac, ac], -1)
    io["rope"] = np.stack([np.tile(np.cos(ang).T, (2, 1)), np.tile(np.sin(ang).T, (2, 1))], 1).astype(f)
    rot = np.zeros((P, P), f)
    for b in range(0, P, 32):
        for j in range(16):
            rot[b + 16 + j, b + j] = -1
            rot[b + j, b + 16 + j] = 1
    io["rotm"] = rot
    io["final_g"] = _cols(v["final_g_2"])
    return {k_: np.ascontiguousarray(a_) for k_, a_ in io.items()}, places


def kernel(**inputs):
    import concourse.bacc as bacc
    from concourse.bass_utils import run_bass_kernel_spmd

    arrays, places = _layout({k: np.asarray(v) for k, v in inputs.items()})
    nc = bacc.Bacc("TRN2", target_bir_lowering=False, num_devices=1)
    io = {n: nc.dram_tensor("in_" + n, a.shape, F32, kind="ExternalInput").ap() for n, a in arrays.items()}
    io["out"] = nc.dram_tensor("out_0", (P, KD, S), F32, kind="ExternalOutput").ap()
    program(nc, io, places)
    r = run_bass_kernel_spmd(nc, [{"in_" + n: a for n, a in arrays.items()}], core_ids=[0])
    got = r.results[0]["out_0"]
    return np.ascontiguousarray(got.transpose(2, 1, 0).reshape(1, S, D))
```

```python
import math
from contextlib import ExitStack

import numpy as np

import concourse.bass as bass
from concourse import mybir

F32 = mybir.dt.float32
F32R = mybir.dt.float32r
U32 = mybir.dt.uint32
ALU = mybir.AluOpType
ACT = mybir.ActivationFunctionType
AX = mybir.AxisListType.X

P = 128
D = 1024
KD = D // P
S = 256
NB = S // P
DEPTH = 2
EPS = 1e-6
HD = 64
NH = 8
ND = 4
NKEYS = 128
TOPK = 16
PH = 8
SLOTS = PH * TOPK
DFF = 2816
KF = DFF // P
NMOD = 9
NEG = -1e30
RING = 8
UW = 1024
SPLIT = 4
GROUP = 8
GBUF = 4


ORDER = ("one0", "ada0", "ada1", "ffn00", "one1", "ab", "ffn01", "ffn00", "ab", "ffn01", "ffn10", "mla", "ffn11")


def lam_init(layer):
    return 0.8 - 0.6 * math.exp(-0.3 * layer)


class Queues:

    ENGINES = ("pe", "act", "dve", "pool", "sp")

    def __init__(self, sem):
        self.sem = {e: sem(f"{e}_done") for e in self.ENGINES}
        self.count = {e: 0 for e in self.ENGINES}
        self.work = {e: [] for e in self.ENGINES}
        self.seen = {e: {} for e in self.ENGINES}

    def wait(self, e, eng, tokens):
        for s, v in tokens:
            if self.seen[e].get(id(s), 0) < v:
                eng.wait_ge(s, v)
                self.seen[e][id(s)] = v

    def op(self, e, tokens, emit):
        self.count[e] += 1

        def run(eng):
            self.wait(e, eng, tokens)
            emit(eng).then_inc(self.sem[e], 1)
        self.work[e].append(run)
        return (self.sem[e], self.count[e])

    def many(self, e, tokens, emits):
        self.count[e] += 1

        def run(eng):
            self.wait(e, eng, tokens)
            for emit in emits:
                last = emit(eng)
            last.then_inc(self.sem[e], 1)
        self.work[e].append(run)
        return (self.sem[e], self.count[e])

    def part(self, e, tokens, run_part):
        def run(eng):
            self.wait(e, eng, tokens)
            run_part(eng)
        self.work[e].append(run)

    def dma(self, e, tokens, out, in_, sem_count):
        sem_count[1] += 16
        value = sem_count[1]

        def run(eng):
            self.wait(e, eng, tokens)
            eng.dma_start(out, in_).then_inc(sem_count[0], 16)
        self.work[e].append(run)
        return (sem_count[0], value)


def turns(eng, n, body, head=0, tail=0, width=RING):
    for st in range(head):
        body(0, st)
    k = (n - head - tail) // width
    at = head
    if k >= 2:
        with eng.Fori(0, k) as i:
            for j in range(width):
                body(i, head + j)
        at = head + k * width
    for st in range(at, n):
        body(0, st)


class Steps:

    def __init__(self, steps):
        self.steps, self.live, self.result = steps, True, None

    def step(self):
        try:
            next(self.steps)
        except StopIteration as end:
            self.live, self.result = False, end.value

    def finish(self):
        while self.live:
            self.step()
        return self.result


def drain(steps):
    return Steps(steps).finish()


def program(nc, io, places):
    with ExitStack() as ctx:
        sem = lambda name: ctx.enter_context(nc.semaphore(name))
        q = Queues(sem)
        pe = lambda t, f: q.op("pe", t, f)
        act = lambda t, f: q.op("act", t, f)
        dve = lambda t, f: q.op("dve", t, f)
        pool = lambda t, f: q.op("pool", t, f)

        bank = [ctx.enter_context(nc.psum_tensor(f"bank{i}", [P, 512], F32)) for i in range(8)]

        def sb(stack, name, shape, dt=F32):
            return stack.enter_context(nc.sbuf_tensor(name, shape, dt))

        ring = sb(ctx, "ring", [P, RING, UW])
        slot_full = [sem(f"slot_full{i}") for i in range(RING)]
        unit_done = sem("unit_done")
        evac = sem("evac")
        w_high = sem("w_high")
        w_low = sem("w_low")
        f_high, f_low = sem("f_high"), sem("f_low")
        half_done = sem("half_done")
        state = dict(unit=0, evac=0, half=0, split=0, fsplit=0)
        segments = [places[name] for name in ORDER]
        n_units = sum(n for _, n in segments)

        loads = [sem("loads"), 0]
        small = {}

        def load(name, stack=ctx):
            a = io[name]
            small[name] = sb(stack, name + "_sb", list(a.shape))
            return q.dma("act", [], small[name][:], a, loads)

        load("ident")
        load("half")
        for name in ("cond", "ada_b", "norm_g", "ones", "cdft", "tdft"):
            load(name)
        stat = sb(ctx, "stat", [P, 2, 16])
        attn_p = sb(ctx, "attn_p", [P, 2, 512])
        attn_pt = sb(ctx, "attn_pt", [P, 2, 512])
        bufs = dict(p=[attn_p[:, i, :] for i in range(2)], pt=[attn_pt[:, i, :] for i in range(2)], stat=stat)
        hT = sb(ctx, "hT", [P, KD, S])
        xc = sb(ctx, "xc", [P, KD, S])
        ctxK = sb(ctx, "ctxK", [P, 4, S])
        ctxV = sb(ctx, "ctxV", [P, NB, 512])
        gs = sb(ctx, "gs", [P, 2, 512])
        rs = sb(ctx, "rs", [P, 2, 512])
        mods = sb(ctx, "mods", [P, DEPTH, NMOD * KD, 2])
        gA = sb(ctx, "gA", [P, DEPTH, 3, KD, 2])
        cond = sb(ctx, "cond_s", [P, KD, 2])
        q.dma("act", [], xc[:], io["ctxT"], loads)

        block1 = ExitStack()
        x = sb(block1, "x", [P, NB, D])
        loaded = q.dma("act", [], x[:], io["x"], loads)
        for name in ("causal", "norm1_g", "norm2_g", "final_norm_g", "subln_g", "lam", "b_forget",
                     "tri", "pick", "relb", "w_ff", "keysT", "iota16"):
            loaded = load(name, block1)
        ident = small["ident"]

        def stream(sp):
            u0 = 0
            for start, n in segments:
                def step(i, st, start=start, u0=u0):
                    u = u0 + st
                    if u >= RING:
                        sp.wait_ge(unit_done, i * RING + (u - RING + 1))
                    sp.dma_start(ring[:, u % RING, :], io["stream"][i * RING + start + st]
                                 ).then_inc(slot_full[u % RING], 16)
                turns(sp, n, step, head=0 if u0 else RING)
                u0 += n
        q.part("sp", [], stream)

        def unit_wait(eng, u0, i, st):
            u = u0 + st
            eng.wait_ge(slot_full[u % RING], (i + (u // RING + 1)) * 16)
            return ring[:, u % RING, :]

        def project(after, n, mms, evacs, dve_evac=False):
            u0, e0 = state["unit"], state["evac"]
            state["unit"] += n
            state["evac"] += n

            def pe_part(eng):
                def step(i, st):
                    w = unit_wait(eng, u0, i, st)
                    eng.wait_ge(evac, i * RING + max(0, e0 + st - 3))
                    out = bank[st % 4]
                    for cols, terms in mms(w, st):
                        for t, (lhsT, rhs) in enumerate(terms):
                            last = eng.matmul(out[:, cols], lhsT, rhs, start=(t == 0), stop=(t == len(terms) - 1))
                    last.then_inc(unit_done, 1)
                turns(eng, n, step, head=4 if n >= 4 else 0)
            q.part("pe", after, pe_part)

            def out_part(eng):
                def step(i, st):
                    eng.wait_ge(unit_done, i * RING + (u0 + st + 1))
                    evacs(eng, bank[st % 4], i * RING + st).then_inc(evac, 1)
                turns(eng, n, step, head=4 if n >= 4 else 0)
            q.part("dve" if dve_evac else "act", after, out_part)
            return [(evac, e0 + n)]

        def two_heads(e, bk, dst, t, first, T):
            for m in range(2):
                last = e.activation(dst[:, first + 2 * t + m, 0:T], bk[:, 0:T], ACT.Copy, scale=small["half"][:, m:m + 1])
            return last

        def feature_major(w, actT, cols, kt=KD, first=0):
            return [(slice(0, cols.stop - cols.start),
                     [(w[:, (first + k) * P:(first + k + 1) * P], actT[:, k, cols]) for k in range(kt)])]

        def token_major(after, n, act_of, width, kpu, blocks):
            u0 = state["unit"]
            state["unit"] += n

            def pe_part(eng):
                for st in range(n):
                    w = unit_wait(eng, u0, 0, st)
                    for kk in range(kpu):
                        k = st * kpu + kk
                        for b in range(blocks):
                            for c in range(width // 512):
                                last = eng.matmul(bank[b * (width // 512) + c][:, :], act_of(k, b),
                                                  w[:, kk * width + c * 512:kk * width + (c + 1) * 512],
                                                  start=(k == 0), stop=(k == n * kpu - 1))
                    last.then_inc(unit_done, 1)
            q.part("pe", after, pe_part)
            return [(unit_done, u0 + n)]

        def unit_mm(tokens, mms):
            u0 = state["unit"]
            state["unit"] += 1

            def part(eng):
                w = unit_wait(eng, u0, 0, 0)
                for o, a, b, first, last_ in mms(w):
                    last = eng.matmul(o, a, b, start=first, stop=last_)
                last.then_inc(unit_done, 1)
            q.part("pe", tokens, part)
            return (unit_done, u0 + 1)

        def attention(after, jobs, bufs):
            hist = []
            for n, job in enumerate(jobs):
                g, nk = job["g"], job["nk"]
                lb, tb, ob = bank[n % 2], bank[2 + n % 2], bank[4 + n % 2]
                pr, pt = bufs["p"][n % 2], bufs["pt"][n % 2]
                mx, sm = bufs["stat"][:, n % 2, 0:g], bufs["stat"][:, n % 2, 4:4 + g]
                rc = bufs["stat"][:, n % 2, 8:8 + g]
                old = hist[n - 2] if n >= 2 else None
                lw = after + (old["exp"] if old else [])
                mm = []
                parts = job["logits"]
                wide = g * nk // len(parts)
                for gg, terms in enumerate(parts):
                    for t, (lhsT, rhs) in enumerate(terms):
                        mm.append(lambda e, o=lb[:, gg * wide:(gg + 1) * wide], a=lhsT, b=rhs, s=(t == 0),
                                  z=(t == len(terms) - 1): e.matmul(o, a, b, start=s, stop=z))
                lg = q.many("pe", lw, mm)
                l3 = lb[:, 0:g * nk].rearrange("p (g k) -> p g k", g=g)
                mt = dve([lg] + (old["exp"] + old["w"] if old else []),
                         lambda e, o=mx, i=l3: e.tensor_reduce(o, i, AX, ALU.max, negate=True))
                ex = []
                for gg in range(g):
                    ex.append(act([mt] + ([old["tr"]] if old else []),
                                  lambda e, o=pr[:, gg * nk:(gg + 1) * nk], i=lb[:, gg * nk:(gg + 1) * nk],
                                  b=mx[:, gg:gg + 1], s=sm[:, gg:gg + 1]:
                                  e.activation(o, i, ACT.Exp, bias=b, accum_out=s)))
                rt = dve([ex[-1]], lambda e, o=rc, i=sm: e.reciprocal(o, i))
                wt = []
                if job.get("mix") is not None:
                    lt = dve([rt], lambda e, o=rc[:, 1:2], m=job["mix"]: e.tensor_scalar(o, o, m, None, ALU.mult))
                    w0 = dve([rt], lambda e, o=pr[:, 0:nk], r=rc[:, 0:1]: e.tensor_scalar(o, o, r, None, ALU.mult))
                    wt = [dve([lt, w0], lambda e, o=pr[:, 0:nk], i=pr[:, nk:2 * nk], r=rc[:, 1:2]:
                              e.scalar_tensor_tensor(out=o, in0=i, scalar=r, in1=o, op0=ALU.mult, op1=ALU.add))]
                    wide = nk
                else:
                    for gg in range(g):
                        wt.append(dve([rt], lambda e, o=pr[:, gg * nk:(gg + 1) * nk], r=rc[:, gg:gg + 1]:
                                      e.tensor_scalar(o, o, r, None, ALU.mult)))
                    wide = g * nk
                nt = wide // P
                hist.append(dict(exp=ex, w=wt, wide=wide, nt=nt, job=job, wt=wt, pr=pr, pt=pt, tb=tb, ob=ob))
                if n >= 1:
                    finish(hist, n - 1)
                yield
            finish(hist, len(jobs) - 1)
            return [hist[-1]["out"], hist[-1]["copy"]] + ([hist[-2]["out"]] if len(hist) > 1 else [])

        def finish(hist, n):
            h = hist[n]
            old = hist[n - 2] if n >= 2 else None
            job, pr, pt, tb, ob, nt = h["job"], h["pr"], h["pt"], h["tb"], h["ob"], h["nt"]
            h["tr"] = q.many("pe", h["wt"] + ([old["copy"]] if old else []), [
                (lambda e, c=c: e.transpose(tb[:, c * P:(c + 1) * P], pr[:, c * P:(c + 1) * P], ident[:]))
                for c in range(nt)])
            h["copy"] = act([h["tr"]] + ([old["pv"]] if old else []),
                            lambda e: e.activation(pt[:, 0:nt * P], tb[:, 0:nt * P], ACT.Copy))
            mm = []
            for orow, terms in job["values"](pt):
                for t, (lhsT, rhs) in enumerate(terms):
                    mm.append(lambda e, o=ob[orow, 0:P], a=lhsT, b=rhs, s=(t == 0), z=(t == len(terms) - 1):
                              e.matmul(o, a, b, start=s, stop=z))
            h["pv"] = q.many("pe", [h["copy"]] + ([old["out"]] if old else []), mm)
            h["out"] = job["out"]([h["pv"]], ob)

        def rstd_of(after, ss, tmp, scale):
            a = dve(after, lambda e: e.tensor_scalar(tmp, ss, scale, EPS, ALU.mult, ALU.add))
            b = act([a], lambda e: e.activation(ss, tmp, ACT.Sqrt))
            c = dve([b], lambda e: e.reciprocal(tmp, ss))
            return dve([c], lambda e: e.tensor_copy(ss, tmp))

        t_tok = sb(block1, "t_tok", [P, NB, D])
        sq = sb(block1, "sq", [P, NB, D])
        qkT = sb(block1, "qkT", [P, 24, S])
        gring = sb(block1, "gring", [P, GROUP, D])
        gateT = gring[:, 0:4, :].rearrange("p a (b t) -> p (a b) t", t=S)
        mergedT = gring[:, 4:6, :].rearrange("p a (b t) -> p (a b) t", t=S)
        v_tok = gring[:, 6:8, :]
        heads = sb(block1, "heads", [P, 2 * ND, S])
        dT, fT1 = heads[:, 0:ND, :], heads[:, ND:2 * ND, :]
        cand = sb(block1, "cand", [P, 2, TOPK * TOPK])
        scores = [qkT[:, 16:24, :].rearrange("p a (b n) -> p (a b) n", n=NKEYS),
                  heads[:, :, :].rearrange("p a (b n) -> p (a b) n", n=NKEYS)]
        ss = sb(block1, "ss", [P, 8])
        ss2 = sb(block1, "ss2", [P, 8])
        fl = sb(block1, "fl", [P, 4, NB * NH])
        cT = sb(block1, "cT", [NH, S])
        lamb = sb(block1, "lamb", [P, 8])
        lprod = sb(block1, "lprod", [P, 2, HD])
        topv = sb(block1, "topv", [P, 2 * PH, TOPK])
        topi = sb(block1, "topi", [P, 2 * PH, TOPK], U32)
        topf = sb(block1, "topf", [P, 2 * PH, TOPK])
        bestv = sb(block1, "bestv", [P, PH, TOPK])
        besti = sb(block1, "besti", [P, PH, TOPK], U32)
        bi2 = sb(block1, "bi2", [P, 2, PH, TOPK], U32)
        bf2 = sb(block1, "bf2", [P, 2, PH, TOPK])
        expf = sb(block1, "expf", [P, NB, SLOTS])
        gates = sb(block1, "gates", [P, NB, SLOTS])
        gsum = sb(block1, "gsum", [P, PH])
        idx = sb(block1, "idx", [P, 2, GROUP], U32)
        pre = sb(block1, "pre", [P, 2, GROUP])
        gel = sb(block1, "gel", [P, GROUP])
        wts = sb(block1, "wts", [P, GROUP])

        def norm_tokens(after, g, out_tok=None, outT=hT, cols=0):
            s0 = [act(after, lambda e, b=b: e.activation(sq[:, b, :], x[:, b, :], ACT.Square,
                                                        accum_out=ss[:, b:b + 1])) for b in range(NB)]
            r = rstd_of(s0, ss[:, 0:NB], ss2[:, 0:NB], 1.0 / D)
            n = [dve([r], lambda e, b=b: e.tensor_scalar(sq[:, b, :], x[:, b, :], ss[:, b:b + 1], None, ALU.mult))
                 for b in range(NB)]
            ends = []
            for b in range(NB):
                for c in range(2):
                    i = b * 2 + c
                    tr = q.many("pe", [n[b]] + after, [
                        (lambda e, i=i, k=k, b=b, c=c: e.transpose(
                            bank[i][:, k * P:(k + 1) * P], sq[:, b, (c * 4 + k) * P:(c * 4 + k + 1) * P], ident[:]))
                        for k in range(4)])
                    for k in range(4):
                        kk = c * 4 + k
                        o, s, gg = outT[:, kk, cols + b * P:cols + (b + 1) * P], bank[i][:, k * P:(k + 1) * P], g[:, kk:kk + 1]
                        if c:
                            ends.append(dve([tr], lambda e, o=o, s=s, gg=gg: e.tensor_scalar(o, s, gg, None, ALU.mult)))
                        else:
                            ends.append(act([tr], lambda e, o=o, s=s, gg=gg: e.activation(o, s, ACT.Copy, scale=gg)))
            if out_tok is not None:
                gr = io_rows["norm2"]
                ends += [dve([n[b]] + gr[1], lambda e, b=b: e.tensor_tensor(out_tok[:, b, :], sq[:, b, :], gr[0], ALU.mult))
                         for b in range(NB)]
            return ends

        g2row = sb(block1, "g2row", [P, D])
        io_rows = {}

        def layer_one(layer, after):
            L = layer
            rowt = q.dma("act", after, g2row[:], io["norm2_rows"][L], loads)
            io_rows["norm2"] = (g2row[:, :], [rowt])
            h = norm_tokens(after, small["norm1_g"][:, L])
            lm = small["lam"]
            a = [dve(after, lambda e, j=j: e.tensor_tensor(lprod[:, j, :], lm[:, L, 2 * j, :], lm[:, L, 2 * j + 1, :], ALU.mult))
                 for j in range(2)]
            a = dve(a, lambda e: e.tensor_reduce(lamb[:, 0:2], lprod[:], AX, ALU.add))
            a = act([a], lambda e: e.activation(lamb[:, 2:4], lamb[:, 0:2], ACT.Exp))
            a = dve([a], lambda e: e.tensor_tensor(lamb[:, 4:5], lamb[:, 3:4], lamb[:, 2:3], ALU.subtract))
            neg_lam = dve([a], lambda e: e.tensor_scalar(lamb[:, 5:6], lamb[:, 4:5], -lam_init(L), None, ALU.add))
            sg = dve([neg_lam], lambda e: e.tensor_scalar(lamb[:, 6:7], small["subln_g"][:, L:L + 1], 1.0 - lam_init(L),
                                                          None, ALU.mult))
            allT = slice(0, S)
            qd = project(h, 8, lambda w, t: feature_major(w, hT, allT),
                         lambda e, b, t: two_heads(e, b, qkT, t, 0, S))
            kd = project([], 8, lambda w, t: feature_major(w, hT, allT),
                         lambda e, b, t: e.activation(qkT[:, t + 16, :], b[:, 0:S], ACT.Copy))
            gd = project([], 16, lambda w, t: feature_major(w, hT, allT),
                         lambda e, b, t: e.activation(gateT[:, t, :], b[:, 0:S], ACT.Sigmoid))
            vd = token_major(gd, KD, lambda k, b: hT[:, k, b * P:(b + 1) * P], D, 1, NB)
            ve = []
            for b in range(NB):
                for c in range(2):
                    f = act if c else dve
                    ve.append(f(vd, lambda e, b=b, c=c: (e.activation(v_tok[:, b, c * 512:(c + 1) * 512], bank[2 * b + c][:], ACT.Copy)
                                                         if c else e.tensor_copy(v_tok[:, b, c * 512:(c + 1) * 512], bank[2 * b + c][:]))))
            ffm = q.many("pe", vd + gd, [
                (lambda e, k=k, b=b: e.matmul(bank[4 + b][:, 0:NH], hT[:, k, b * P:(b + 1) * P], small["w_ff"][:, L, k, :],
                                              start=(k == 0), stop=(k == KD - 1)))
                for b in range(NB) for k in range(KD)])
            z, az, ez, ls = (fl[:, j, :] for j in range(4))
            a = [dve([ffm], lambda e, b=b: e.tensor_tensor(z[:, b * NH:(b + 1) * NH], bank[4 + b][:, 0:NH],
                                                           small["b_forget"][:, L, :], ALU.add)) for b in range(NB)]
            b_ = dve(a, lambda e: e.tensor_scalar(az, z, -1.0, None, ALU.mult))
            b_ = dve([b_], lambda e: e.tensor_tensor(az, az, z, ALU.min))
            b_ = act([b_], lambda e: e.activation(ez, az, ACT.Exp))
            b_ = dve([b_], lambda e: e.tensor_scalar(ez, ez, 1.0, None, ALU.add))
            b_ = act([b_], lambda e: e.activation(az, ez, ACT.Ln))
            b_ = dve([b_], lambda e: e.scalar_tensor_tensor(out=ls, in0=z, scalar=0.0, in1=az, op0=ALU.min, op1=ALU.subtract))
            cm = q.many("pe", [b_], [
                (lambda e, b=b: e.matmul(bank[6][0:NH, 0:S], ls[:, b * NH:(b + 1) * NH], small["tri"][:, b, :],
                                         start=(b == 0), stop=(b == NB - 1))) for b in range(NB)])
            cd = act([cm], lambda e: e.activation(cT[:, :], bank[6][0:NH, 0:S], ACT.Copy))
            ready = ve + [cd, neg_lam, sg] + qd + kd
            jobs = []
            o_tok = sq
            for b in range(NB):
                nk = (b + 1) * P
                for hh in range(ND):
                    def out_diff(t, ob, b=b, hh=hh):
                        c = dve(t, lambda e: e.tensor_copy(o_tok[:, b, hh * P:(hh + 1) * P], ob[:, 0:P]))
                        return act([c], lambda e: e.activation(o_tok[:, b, 512 + hh * P:512 + (hh + 1) * P],
                                                               o_tok[:, b, hh * P:(hh + 1) * P], ACT.Square,
                                                               accum_out=ss[:, b * ND + hh:b * ND + hh + 1]))
                    qs = [qkT[:, 2 * hh + m, b * P:(b + 1) * P] for m in range(2)]
                    ks = qkT[:, 16 + hh, 0:nk]
                    jobs.append(dict(
                        g=2, nk=nk, mix=lamb[:, 5:6],
                        logits=[[(qs[m], ks),
                                 (ident[:], small["relb"][:, hh, S - nk:S])] for m in range(2)],
                        values=lambda pt, b=b, hh=hh: [(slice(0, P), [
                            (pt[:, kb * P:(kb + 1) * P], v_tok[:, kb, hh * P:(hh + 1) * P]) for kb in range(b + 1)])],
                        out=out_diff))
            for b in range(NB):
                nk = (b + 1) * P
                for hp in range(NH // 2):
                    qs = [qkT[:, 8 + 2 * hp + m, b * P:(b + 1) * P] for m in range(2)]
                    ks = qkT[:, 20 + hp, 0:nk]
                    jobs.append(dict(
                        g=2, nk=nk,
                        logits=[[(qs[m], ks),
                                 (ident[:], small["causal"][:, S - nk:S]),
                                 (cT[:, b * P:(b + 1) * P], small["pick"][:, 2 * hp + m:2 * hp + m + 1].to_broadcast([NH, nk])),
                                 (small["pick"][:, NH + 2 * hp + m:NH + 2 * hp + m + 1].to_broadcast([NH, P]), cT[:, 0:nk])] for m in range(2)],
                        values=lambda pt, b=b, hp=hp, nk=nk: [(slice(m * HD, (m + 1) * HD), [
                            (v_tok[:, kb, 512 + (2 * hp + m) * HD:512 + (2 * hp + m + 1) * HD],
                             pt[:, m * nk + kb * P:m * nk + (kb + 1) * P]) for kb in range(b + 1)]) for m in range(2)],
                        out=lambda t, ob, b=b, hp=hp: dve(t, lambda e: e.tensor_copy(
                            fT1[:, hp, b * P:(b + 1) * P], ob[:, 0:P]))))
            at = drain(attention(ready, jobs, bufs))
            r = rstd_of(at, ss[:, 0:8], ss2[:, 0:8], 1.0 / P)
            dd = []
            for b in range(NB):
                n = [dve([r], lambda e, b=b, hh=hh: e.tensor_scalar(
                    o_tok[:, b, hh * P:(hh + 1) * P], o_tok[:, b, hh * P:(hh + 1) * P],
                    ss[:, b * ND + hh:b * ND + hh + 1], None, ALU.mult)) for hh in range(ND)]
                tr = q.many("pe", [n[-1]] + at, [
                    (lambda e, b=b, hh=hh: e.transpose(bank[b][:, hh * P:(hh + 1) * P], o_tok[:, b, hh * P:(hh + 1) * P], ident[:]))
                    for hh in range(ND)])
                dd.append(act([tr], lambda e, b=b: e.activation(
                    dT[:, :, b * P:(b + 1) * P], bank[b][:, :].rearrange("p (h t) -> p h t", h=ND), ACT.Copy,
                    scale=lamb[:, 6:7])))
            ev0 = state["evac"]

            def merge(e, b, t):
                d = mergedT[:, t, :]
                return e.tensor_tensor(d, d, sq[:, 0, 0:S], ALU.add)

            u0, e0 = state["unit"], state["evac"]
            state["unit"] += KD
            state["evac"] += KD

            def merge_pe(eng):
                for st in range(KD):
                    w = unit_wait(eng, u0, 0, st)
                    eng.wait_ge(evac, e0 + st - 3)
                    for j, src in enumerate((dT, fT1)):
                        for k in range(ND):
                            last = eng.matmul(bank[st % 4][:, j * S:(j + 1) * S], w[:, (j * ND + k) * P:(j * ND + k + 1) * P],
                                              src[:, k, :], start=(k == 0), stop=(k == ND - 1))
                    last.then_inc(unit_done, 1)
            q.part("pe", dd + at, merge_pe)
            tok = dd + at
            for st in range(KD):
                bk = bank[st % 4]
                m1 = dve(tok + [(unit_done, u0 + st + 1)], lambda e, st=st, bk=bk: e.tensor_tensor(
                    mergedT[:, st, :], bk[:, 0:S], gateT[:, st, :], ALU.mult))
                m2 = dve([], lambda e, st=st, bk=bk: e.tensor_tensor(
                    sq[:, 0, (st % 2) * S:(st % 2 + 1) * S], bk[:, S:2 * S], gateT[:, KD + st, :], ALU.mult))
                q.part("dve", [m1, m2], lambda e, st=st: e.tensor_tensor(
                    mergedT[:, st, :], mergedT[:, st, :], sq[:, 0, (st % 2) * S:(st % 2 + 1) * S], ALU.add).then_inc(evac, 1))
            od = token_major([(evac, e0 + KD)], KD, lambda k, b: mergedT[:, k, b * P:(b + 1) * P], D, 1, NB)
            xe = []
            for b in range(NB):
                for c in range(2):
                    xs = x[:, b, c * 512:(c + 1) * 512]
                    xe.append(dve(od, lambda e, xs=xs, b=b, c=c: e.tensor_tensor(xs, bank[2 * b + c][:], xs, ALU.add)))
            h = norm_tokens(xe, small["norm2_g"][:, L], out_tok=t_tok)
            qd = project(h, 16, lambda w, t: feature_major(w, hT, allT),
                         lambda e, b, t: e.activation(qkT[:, t, :], b[:, 0:S], ACT.Copy))
            last_block = qd + h
            sc_all = []
            for b in range(NB):
                for j in range(4):
                    m = q.many("pe", last_block, [
                        (lambda e, c=c, j=j, b=b: e.matmul(bank[4 * b + j][:, c * P:(c + 1) * P],
                                                           qkT[:, 4 * j + c, b * P:(b + 1) * P],
                                                           small["keysT"][:, L, (4 * j + c) % 2, :], start=True, stop=True))
                        for c in range(4)])
                    sc_all.append(act([m], lambda e, b=b, j=j: e.activation(
                        scores[b][:, 4 * j:4 * j + 4, :], bank[4 * b + j][:, :].rearrange("p (c n) -> p c n", c=4),
                        ACT.Copy)))
            done = drain(route(0, sc_all))
            if L == 0:
                ada = modulation_mm([loaded, cs] + sc_all)
                side = Steps(chain(route(1, []), context_before_first_ffn(ada), pause=12))
            else:
                side = Steps(chain(route(1, []), mixer_ctx(), pause=0))
            first = gather(L, 0, done, 0, SLOTS // GROUP, side=side)
            d1, ctx_ready = side.finish()
            up = FfnUp(ctx_ready, hT, qkT)
            down = up.down()
            gather(L, 1, d1 + first, 0, up.groups, beside=up)
            last = gather(L, 1, [], up.groups, SLOTS // GROUP - up.groups)
            ctx_done = residuals(down, 0, 2 * L, [CTX])
            return last + [ctx_done]

        def chain(a, b, pause):
            a, b, n = Steps(a), Steps(b), 0
            while a.live or b.live:
                if a.live:
                    a.step()
                if b.live and n >= pause:
                    b.step()
                n += 1
                yield
            return a.result, b.result

        def top16(src, vals, ids, after):
            a = dve(after, lambda e: e.max(out=vals[:, 0:8], in_=src))
            i = dve([a], lambda e: e.max_index(out=ids[:, 0:8], in_max=vals[:, 0:8], in_values=src))
            m = dve([i], lambda e: e.match_replace(out=src, in_to_replace=vals[:, 0:8], in_values=src, imm_value=-3e38))
            a = dve([m], lambda e: e.max(out=vals[:, 8:16], in_=src))
            return dve([a], lambda e: e.max_index(out=ids[:, 8:16], in_max=vals[:, 8:16], in_values=src))

        def route(b, after):
            ends = []
            for hp in range(2 * PH):
                ends = [top16(scores[b][:, hp, :], topv[:, hp, :], topi[:, hp, :], after)]
                after = []
                if hp % 2:
                    yield
            f = dve(ends, lambda e: e.tensor_copy(topf[:], topi[:]))
            for h in range(PH):
                c3 = cand[:, h % 2, :].rearrange("p (i j) -> p i j", i=TOPK)
                v1 = topv[:, 2 * h, :].unsqueeze(2).to_broadcast([P, TOPK, TOPK])
                v2 = topv[:, 2 * h + 1, :].unsqueeze(1).to_broadcast([P, TOPK, TOPK])
                c = dve(ends, lambda e, c3=c3, v1=v1, v2=v2: e.tensor_tensor(c3, v1, v2, ALU.add))
                g = top16(cand[:, h % 2, :], bestv[:, h, :], besti[:, h, :], [c])
                if h % 2:
                    yield
            a = dve([g], lambda e: e.tensor_scalar(bi2[:, 0], besti[:], 4, None, ALU.logical_shift_right))
            c = dve([g], lambda e: e.tensor_scalar(bi2[:, 1], besti[:], 15, None, ALU.bitwise_and))
            a = dve([a, c], lambda e: e.tensor_copy(bf2[:], bi2[:]))
            oh = scores[b].rearrange("p a n -> p (a n)").rearrange("p (h s j) -> p h s j", h=PH, s=TOPK)
            t3 = topf[:, :, :].rearrange("p (h two) j -> p h two j", two=2)
            for half in range(2):
                sel = bf2[:, half].unsqueeze(3).to_broadcast([P, PH, TOPK, TOPK])
                io4 = small["iota16"][:, :].unsqueeze(1).unsqueeze(1).to_broadcast([P, PH, TOPK, TOPK])
                src = t3[:, :, half, :].unsqueeze(2).to_broadcast([P, PH, TOPK, TOPK])
                c = dve([a, f], lambda e, sel=sel, io4=io4: e.tensor_tensor(oh, sel, io4, ALU.is_equal))
                c = dve([c], lambda e, src=src: e.tensor_tensor(oh, oh, src, ALU.mult))
                a = dve([c], lambda e, half=half: e.tensor_reduce(bf2[:, half], oh, AX, ALU.add))
            ex = expf[:, b, :].rearrange("p (h s) -> p h s", h=PH)
            a = dve([a], lambda e: e.scalar_tensor_tensor(out=ex, in0=bf2[:, 0], scalar=float(NKEYS), in1=bf2[:, 1],
                                                          op0=ALU.mult, op1=ALU.add))
            gt = gates[:, b, :].rearrange("p (h s) -> p h s", h=PH)
            c = dve([g], lambda e: e.tensor_tensor(gt, bestv[:], bestv[:, :, 0:1].to_broadcast([P, PH, TOPK]), ALU.subtract))
            c = act([c], lambda e: e.activation(gates[:, b, :], gates[:, b, :], ACT.Exp))
            c = dve([c], lambda e: e.tensor_reduce(gsum[:], gt, AX, ALU.add))
            c = dve([c], lambda e: e.reciprocal(gsum[:], gsum[:]))
            c = dve([c], lambda e: e.tensor_tensor(gt, gt, gsum[:].unsqueeze(2).to_broadcast([P, PH, TOPK]), ALU.mult))
            return [a, c]

        row_full = [sem(f"row_full{i}") for i in range(GROUP)]
        rows_used, g_idx, g_gel, g_wts, g_iss = (sem(n) for n in (
            "rows_used", "idx_ready", "gelu_ready", "weights_ready", "gathers_issued"))
        state["g"] = 0
        NG = SLOTS // GROUP

        def gather(L, b, after, first, n, beside=None, side=None):
            g0 = state["g"]
            state["g"] += n
            per = 2 * GROUP

            def used(eng, i, g, value):
                if value + (g0 + g) * per > 0:
                    eng.wait_ge(rows_used, i * (2 * per) + ((g0 + g) * per + value))

            def pool_part(eng):
                def step(i, g):
                    eng.wait_ge(g_idx, i * 2 + (g0 + g + 1))
                    for t, tab in enumerate((io[f"expert_u{L}"], io[f"expert_v{L}"])):
                        for s in range(GROUP):
                            used(eng, i, g, (t - 1) * GROUP + s + 1)
                            eng.sem_inc(g_iss, 1)
                            eng.indirect_dma_start(
                                out=gring[:, s, :], out_offset=None, in_=tab,
                                in_offset=bass.IndirectOffsetOnAxis(ap=idx[:, (first + g) % 2, s:s + 1], axis=0)
                            ).then_inc(row_full[s], 16)
                turns(eng, n, step, head=1 if n % 2 else 2, width=2)
            q.part("pool", after, pool_part)

            def take(eng, i, g):
                used(eng, i, g - 1, 0)
                eng.activation(idx[:, (first + g) % 2, :], expf[:, b, bass.ds(i * (2 * GROUP) + (first + g) * GROUP, GROUP)],
                               ACT.Copy).then_inc(g_idx, 1)

            def act_step(eng, i, g):
                if first + g < NG - 1:
                    take(eng, i, g + 1)
                if beside:
                    beside.act(eng, i, g)
                used(eng, i, g, GROUP)
                if g0 + g > 0:
                    eng.wait_ge(g_wts, i * 2 + (g0 + g))
                eng.activation(gel[:], pre[:, (first + g) % 2, :], ACT.Gelu).then_inc(g_gel, 1)

            def dve_step(eng, i, g):
                for s in range(GROUP):
                    eng.wait_ge(row_full[s], i * 64 + (2 * (g0 + g) + 1) * 16)
                    eng.tensor_tensor_reduce(out=gring[:, s, :], in0=gring[:, s, :], in1=t_tok[:, b, :],
                                             scale=1.0, scalar=0.0, op0=ALU.mult, op1=ALU.add,
                                             accum_out=pre[:, (first + g) % 2, s:s + 1]).then_inc(rows_used, 1)
                if beside:
                    beside.dve(eng, i, g)
                eng.wait_ge(g_gel, i * 2 + (g0 + g + 1))
                used(eng, i, g, 0)
                eng.tensor_tensor(wts[:], gel[:], gates[:, b, bass.ds(i * (2 * GROUP) + (first + g) * GROUP, GROUP)],
                                  ALU.mult).then_inc(g_wts, 1)
                eng.wait_ge(g_wts, i * 2 + (g0 + g + 1))
                for s in range(GROUP):
                    eng.wait_ge(row_full[s], i * 64 + (2 * (g0 + g) + 2) * 16)
                    used(eng, i, g, GROUP + s)
                    eng.scalar_tensor_tensor(out=x[:, b, :], in0=gring[:, s, :], scalar=wts[:, s:s + 1],
                                             in1=x[:, b, :], op0=ALU.mult, op1=ALU.add).then_inc(rows_used, 1)

            if first == 0:
                q.part("act", after, lambda eng: take(eng, 0, 0))
            if side is None:
                q.part("act", after, lambda eng: turns(eng, n, lambda i, g: act_step(eng, i, g), head=1 if n % 2 else 2,
                                                       tail=2 if first + n == NG else 0, width=2))
                q.part("dve", after, lambda eng: turns(eng, n, lambda i, g: dve_step(eng, i, g), head=1 if n % 2 else 2, width=2))
            else:
                for g in range(n):
                    q.part("act", after, lambda eng, g=g: act_step(eng, 0, g))
                    q.part("dve", after, lambda eng, g=g: dve_step(eng, 0, g))
                    if g < n - 1 and side.live:
                        side.step()
            return [(rows_used, (g0 + n) * per), (g_gel, g0 + n), (g_wts, g0 + n)]

        LAT, CTX = 0, 1
        xs = [hT, xc]
        onesT = {D: small["ones"][:, 0, :], 384: small["ones"][:, 1, :], P: small["ones"][:, 2, :]}

        def feature_rstd(after, tiles, T):
            mm = []
            for k, tile_ in enumerate(tiles):
                a = act(after + (mm[k - 2:k - 1] if k >= 2 else []),
                        lambda e, k=k, t=tile_: e.activation(gs[:, k % 2, 0:T], t, ACT.Square))
                mm.append(pe([a] + after, lambda e, k=k, n=len(tiles): e.matmul(
                    bank[7][:, 0:T], onesT[n * P], gs[:, k % 2, 0:T], start=(k == 0), stop=(k == n - 1))))
            a = dve([mm[-1]] + after, lambda e: e.tensor_scalar(rs[:, 1, 0:T], bank[7][:, 0:T], EPS, None, ALU.add))
            a = act([a], lambda e: e.activation(rs[:, 0, 0:T], rs[:, 1, 0:T], ACT.Sqrt))
            return dve([a], lambda e: e.reciprocal(rs[:, 1, 0:T], rs[:, 0, 0:T]))

        def mod_norm(after, L, j, streams, out):
            ends, low = [], []
            for n, s in enumerate(streams):
                r = feature_rstd(after + ends[-1:] + low[-1:], [xs[s][:, k, :] for k in range(KD)], S)
                for k in range(KD):
                    cols = slice(n * S, (n + 1) * S)
                    a = dve([r] + ends[-2:-1], lambda e, k=k, s=s: e.tensor_tensor(
                        gs[:, k % 2, 0:S], xs[s][:, k, :], rs[:, 1, 0:S], ALU.mult))
                    bias, scale = mods[:, L, 3 * j * KD + k, s:s + 1], gA[:, L, j, k, s:s + 1]
                    if not isinstance(out, tuple):
                        ends.append(act([a], lambda e, k=k, bias=bias, scale=scale, cols=cols: e.activation(
                            out[:, k, cols], gs[:, k % 2, 0:S], ACT.Identity, bias=bias, scale=scale)))
                        continue
                    v = act([a] + low[-2:-1], lambda e, k=k, bias=bias, scale=scale: e.activation(
                        gs[:, k % 2, S:2 * S], gs[:, k % 2, 0:S], ACT.Identity, bias=bias, scale=scale))
                    ends.append(act([v] + after, lambda e, k=k, cols=cols: e.activation(
                        out[0][:, k, cols], gs[:, k % 2, S:2 * S], ACT.Copy)))
                    low.append(dve([ends[-1]] + after, lambda e, k=k, cols=cols: e.tensor_tensor(
                        out[1][:, k, cols], gs[:, k % 2, S:2 * S], out[0][:, k, cols], ALU.subtract)))
            return [ends[-1]] + low[-1:]

        def residual(after, L, j, streams, k, bk):
            for n, s in enumerate(streams):
                r = dve(after, lambda e, n=n, s=s: e.scalar_tensor_tensor(
                    out=xs[s][:, k, :], in0=bk[:, n * S:(n + 1) * S], scalar=mods[:, L, (3 * j + 2) * KD + k, s:s + 1],
                    in1=xs[s][:, k, :], op0=ALU.mult, op1=ALU.add))
            return r

        def residuals(after, L, j, streams):
            return [residual(after, L, j, streams, k, bank[k]) for k in range(KD)][-1]

        class FfnUp:

            def __init__(self, after, h, f):
                self.h, self.f = h, f
                self.u0, self.e0, self.h0 = state["unit"], state["evac"], state["half"]
                state["unit"] += 3 * KF
                state["evac"] += KF
                state["half"] += KF
                self.groups = KF // 2
                q.part("pe", after, self.pe)

            def place(self, st):
                return bank[(st // 2) % 4][:, (st % 2) * S:(st % 2 + 1) * S]

            def pe(self, eng):
                def step(i, st):
                    w = unit_wait(eng, self.u0, i, st)
                    if st % 2 == 0:
                        eng.wait_ge(evac, i * (RING // 2) + (self.e0 + max(0, st // 2 - 3)))
                    for k in range(KD):
                        last = eng.matmul(self.place(st), w[:, k * P:(k + 1) * P], self.h[:, k, :],
                                          start=(k == 0), stop=(k == KD - 1))
                    last.then_inc(unit_done, 1)
                turns(eng, 2 * KF, step, head=4)

            def act(self, eng, i, g):
                for m in (2 * g, 2 * g + 1):
                    eng.wait_ge(unit_done, i * RING + (self.u0 + 2 * m + 2))
                    eng.wait_ge(evac, i * (RING // 2) + (self.e0 + max(0, m - 1)))
                    eng.activation(gs[:, m % 2, 0:S], self.place(2 * m), ACT.Silu).then_inc(half_done, 1)

            def dve(self, eng, i, g):
                for m in (2 * g, 2 * g + 1):
                    eng.wait_ge(half_done, i * (RING // 2) + (self.h0 + m + 1))
                    eng.tensor_tensor(self.f[:, i * (RING // 2) + m, :], gs[:, m % 2, 0:S], self.place(2 * m + 1),
                                      ALU.mult).then_inc(evac, 1)

            def down(self):
                d0 = self.u0 + 2 * KF

                def part(eng):
                    def step(i, st):
                        w = unit_wait(eng, d0, i, st)
                        for m in range(KD):
                            last = eng.matmul(bank[m][:, 0:S], w[:, m * P:(m + 1) * P], self.f[:, i * RING + st, :],
                                              start=(st == 0), stop=(isinstance(i, int) and st == KF - 1))
                        last.then_inc(unit_done, 1)
                    turns(eng, KF, step, head=3, tail=3)
                q.part("pe", [(evac, self.e0 + KF), (half_done, self.h0 + KF)], part)
                return [(unit_done, d0 + KF)]

        def split_high(eng, u0, s0, i, st):
            w = unit_wait(eng, u0, i, st)
            eng.wait_ge(unit_done, i * RING + (u0 + st - SPLIT + 1))
            eng.activation(wr[:, (s0 + st) % SPLIT, :], w, ACT.Copy).then_inc(w_high, 1)

        def split_low(eng, u0, s0, i, st):
            eng.wait_ge(w_high, i * RING + (s0 + st + 1))
            eng.tensor_tensor(wl[:, (s0 + st) % SPLIT, :], ring[:, (u0 + st) % RING, :], wr[:, (s0 + st) % SPLIT, :],
                              ALU.subtract).then_inc(w_low, 1)

        def three(eng, out, wh, wlow, ah, al, first, last_):
            eng.matmul(out, wh, ah, start=first, stop=False)
            eng.matmul(out, wh, al, start=False, stop=False)
            return eng.matmul(out, wlow, ah, start=False, stop=last_)

        def ffn(after, L, j, streams):
            T = S * len(streams)
            hh = mod_norm(after, L, j, streams, (hr, hl))
            u0, e0, h0, s0, f0 = (state[k_] for k_ in ("unit", "evac", "half", "split", "fsplit"))
            state["unit"] += 3 * KF
            state["evac"] += KF
            state["half"] += KF
            state["split"] += 3 * KF
            state["fsplit"] += KF
            deep = 4 if T == S else 2

            def place(st):
                if T == S:
                    return bank[(st // 2) % 4][:, (st % 2) * S:(st % 2 + 1) * S]
                return bank[st % 4][:, 0:T]

            def pe_up(eng):
                def step(i, st):
                    eng.wait_ge(w_low, i * RING + (s0 + st + 1))
                    if st % 2 == 0:
                        eng.wait_ge(evac, i * (RING // 2) + (e0 + max(0, st // 2 - deep + 1)))
                    sl = (s0 + st) % SPLIT
                    for k in range(KD):
                        ks = slice(k * P, (k + 1) * P)
                        last = three(eng, place(st), wr[:, sl, ks], wl[:, sl, ks], hr[:, k, 0:T], hl[:, k, 0:T],
                                     k == 0, k == KD - 1)
                    last.then_inc(unit_done, 1)
                turns(eng, 2 * KF, step, head=4)

            def act_up(eng):
                split_high(eng, u0, s0, 0, 0)
                split_high(eng, u0, s0, 0, 1)

                def step(i, m):
                    if m < KF - 1:
                        split_high(eng, u0, s0, i, 2 * m + 2)
                        split_high(eng, u0, s0, i, 2 * m + 3)
                    eng.wait_ge(unit_done, i * RING + (u0 + 2 * m + (2 if T == S else 1)))
                    eng.wait_ge(evac, i * (RING // 2) + (e0 + max(0, m - 1)))
                    eng.activation(gs[:, m % 2, 0:T], place(2 * m), ACT.Silu).then_inc(half_done, 1)
                turns(eng, KF, step, head=2, tail=1, width=RING // 2)

            def dve_up(eng):
                split_low(eng, u0, s0, 0, 0)
                split_low(eng, u0, s0, 0, 1)

                def step(i, m):
                    if m < KF - 1:
                        split_low(eng, u0, s0, i, 2 * m + 2)
                        split_low(eng, u0, s0, i, 2 * m + 3)
                    eng.wait_ge(unit_done, i * RING + (u0 + 2 * m + 2))
                    eng.wait_ge(half_done, i * (RING // 2) + (h0 + m + 1))
                    eng.tensor_tensor(fT[:, i * (RING // 2) + m, 0:T], gs[:, m % 2, 0:T], place(2 * m + 1),
                                      ALU.mult).then_inc(evac, 1)
                turns(eng, KF, step, head=2, tail=1, width=RING // 2)

            q.part("pe", hh, pe_up)
            q.part("act", hh, act_up)
            q.part("dve", hh, dve_up)
            d0, t0 = u0 + 2 * KF, s0 + 2 * KF

            def act_down(eng):
                def step(i, st):
                    split_high(eng, d0, t0, i, st)
                    if st == 0:
                        eng.wait_ge(evac, e0 + KF)
                    eng.wait_ge(unit_done, i * RING + (d0 + st - 1))
                    eng.activation(fr[:, st % 2, 0:T], fT[:, i * RING + st, 0:T], ACT.Copy).then_inc(f_high, 1)
                turns(eng, KF, step)

            def dve_down(eng):
                def step(i, st):
                    split_low(eng, d0, t0, i, st)
                    eng.wait_ge(f_high, i * RING + (f0 + st + 1))
                    eng.tensor_tensor(fl_[:, st % 2, 0:T], fT[:, i * RING + st, 0:T], fr[:, st % 2, 0:T],
                                      ALU.subtract).then_inc(f_low, 1)
                turns(eng, KF, step)

            def pe_down(eng):
                def step(i, st):
                    eng.wait_ge(w_low, i * RING + (t0 + st + 1))
                    eng.wait_ge(f_low, i * RING + (f0 + st + 1))
                    sl = (t0 + st) % SPLIT
                    for m in range(KD):
                        ms = slice(m * P, (m + 1) * P)
                        last = three(eng, bank[m][:, 0:T], wr[:, sl, ms], wl[:, sl, ms], fr[:, st % 2, 0:T],
                                     fl_[:, st % 2, 0:T], st == 0, isinstance(i, int) and st == KF - 1)
                    last.then_inc(unit_done, 1)
                turns(eng, KF, step, head=3, tail=3)

            q.part("act", [], act_down)
            q.part("dve", [(evac, e0 + KF)], dve_down)
            q.part("pe", [(evac, e0 + KF), (half_done, h0 + KF)], pe_down)
            return [residuals([(unit_done, d0 + KF)] + hh, L, j, streams)]

        cs = act([loaded], lambda e: e.activation(cond[:], small["cond"][:], ACT.Silu))

        def modulation_mm(after):
            n = DEPTH * NMOD * KD
            u0 = state["unit"]
            state["unit"] += n

            def part(eng):
                def step(i, st):
                    w = unit_wait(eng, u0, i, st)
                    for k in range(KD):
                        last = eng.matmul(bank[0][:, bass.ds(i * (2 * RING) + 2 * st, 2)], w[:, k * P:(k + 1) * P],
                                          cond[:, k, :], start=(k == 0), stop=(k == KD - 1))
                    last.then_inc(unit_done, 1)
                turns(eng, n, step)
            q.part("pe", after, part)
            return [(unit_done, u0 + n)]

        def modulation(after):
            n = NMOD * KD
            for L in range(DEPTH):
                a = dve(after, lambda e, L=L: e.tensor_tensor(
                    mods[:, L], bank[0][:, 2 * n * L:2 * n * (L + 1)].rearrange("p (n s) -> p n s", s=2),
                    small["ada_b"][:, L, :].unsqueeze(2).to_broadcast([P, n, 2]), ALU.add))
                for j in range(3):
                    b = dve([a], lambda e, j=j, L=L: e.tensor_scalar(gA[:, L, j], mods[:, L, (3 * j + 1) * KD:(3 * j + 2) * KD, :],
                                                                    1.0, None, ALU.add))
                    r = dve([b], lambda e, j=j, L=L: e.tensor_tensor(
                        gA[:, L, j], gA[:, L, j], small["norm_g"][:, L, j, :].unsqueeze(2).to_broadcast([P, KD, 2]), ALU.mult))
                    if j != 1:
                        gate = mods[:, L, (3 * j + 2) * KD:(3 * j + 3) * KD, :]
                        r = dve([a], lambda e, gate=gate: e.tensor_scalar(gate, gate, 0.5, None, ALU.mult))
            return [r]

        def context_before_first_ffn(ada):
            m = modulation(ada)
            yield
            return mod_norm(m, 0, 0, [CTX], hT)

        def mixer_ctx():
            r = yield from mixer_ab([], CTX, hT, qkT, hT)
            return mod_norm(r, 0, 2, [CTX], hT)

        def back(after, L, streams, src):
            T = S * len(streams)
            for st in range(KD):
                t = unit_mm(after, lambda w, st=st: [(bank[st][:, 0:T], w[:, k * P:(k + 1) * P], src(k), k == 0, k == KD - 1)
                                                     for k in range(KD)])
                r = residual(after + [t], L, 1, streams, st, bank[st])
                yield
            return [r]

        def mixer_ab(after, s, h, f, y, bias_ready=[]):
            n = mod_norm(after, 0, 1, [s], h)
            kt = ctxK if s == CTX else f[:, 12:16, :]
            vt = ctxV if s == CTX else f[:, 16:20, :].rearrange("p (b c) t -> p b (c t)", b=NB)
            yield
            ev, tiles = [], []
            for t in range(12):
                m = unit_mm(n + ev[t - 4:t - 3] if t >= 4 else n, lambda w, t=t: [
                    (bank[t % 4][:, 0:S], w[:, k * P:(k + 1) * P], h[:, k, 0:S], k == 0, k == KD - 1) for k in range(KD)])
                bk = bank[t % 4][:, 0:S]
                if t < 4:
                    ev.append(act([m], lambda e, t=t, bk=bk: e.activation(f[:, t, :], bk, ACT.Copy)))
                elif t < 8:
                    for head in range(2):
                        e_ = act([m], lambda e, t=t, bk=bk, head=head: e.activation(
                            f[:, 4 + 2 * (t - 4) + head, :], bk, ACT.Copy, scale=small["half"][:, head:head + 1]))
                    ev.append(e_)
                else:
                    ev.append(act([m], lambda e, t=t, bk=bk: e.activation(kt[:, t - 8, :], bk, ACT.Copy)))
                if t % 2:
                    yield
            for i in range(4):
                vm = unit_mm(n, lambda w, i=i: [(bank[4 + b][:, :], h[:, 2 * i + kk, b * P:(b + 1) * P],
                                                 w[:, kk * 512:(kk + 1) * 512], i == 0 and kk == 0, i == 3 and kk == 1)
                                                for kk in range(2) for b in range(NB)])
            ve = [act([vm], lambda e, b=b: e.activation(vt[:, b, :], bank[4 + b][:], ACT.Copy)) for b in range(NB)]
            yield
            cd, td = small["cdft"], small["tdft"]
            ready = ev[-4:] + ve
            out, second = [], []
            for g in range(4):
                bk, bo, buf = bank[g % 2], bank[2 + g % 2], attn_p[:, g % 2, :]
                m = q.many("pe", ready + second[g - 2:g - 1] * (g >= 2), [
                    (lambda e, b=b, g=g, bk=bk: e.matmul(bk[:, b * 256:(b + 1) * 256], f[:, g, b * P:(b + 1) * P], cd[:, :],
                                                         start=True, stop=True)) for b in range(NB)])
                c = dve([m] + (second[g - 2:g - 1] if g >= 2 else []), lambda e, bk=bk, buf=buf: e.tensor_copy(buf, bk[:]))
                second.append(q.many("pe", [c] + (out[g - 2:g - 1] if g >= 2 else []), [
                    (lambda e, b=b, r=r, bo=bo, buf=buf: e.matmul(
                        bo[:, 0:S], buf[:, b * 256 + r * P:b * 256 + (r + 1) * P], td[:, b, r, :],
                        start=(b == 0 and r == 0), stop=(b == 1 and r == 1))) for b in range(NB) for r in range(2)]))
                out.append(act([second[-1]] + ready, lambda e, g=g, bo=bo: e.activation(y[:, g, 0:S], bo[:, 0:S], ACT.Copy)))
                yield
            jobs = []
            for b in range(NB):
                if s == LAT:
                    for hh in range(NH):
                        r_ = slice((hh % 2) * HD, (hh % 2 + 1) * HD)
                        qs = f[:, 4 + hh, b * P:(b + 1) * P]
                        jobs.append(dict(
                            g=1, nk=2 * S,
                            logits=[[(qs, kt[:, hh // 2, :]), (ident[:], small["na_bias"][:, b * NH + hh, :])],
                                    [(qs, ctxK[:, hh // 2, :])]],
                            values=lambda pt, hh=hh: [(slice(0, HD), [
                                ((vt if kb < NB else ctxV)[:, kb % NB, hh * HD:(hh + 1) * HD], pt[:, kb * P:(kb + 1) * P])
                                for kb in range(4)])],
                            out=lambda t, ob, b=b, hh=hh, r_=r_: dve(t, lambda e: e.tensor_copy(
                                y[r_, 4 + hh // 2, b * P:(b + 1) * P], ob[0:HD, 0:P]))))
                else:
                    for hp in range(NH // 2):
                        jobs.append(dict(
                            g=2, nk=S,
                            logits=[[(f[:, 4 + 2 * hp + m, b * P:(b + 1) * P], kt[:, hp, :])] for m in range(2)],
                            values=lambda pt, hp=hp: [(slice(m * HD, (m + 1) * HD), [
                                (vt[:, kb, (2 * hp + m) * HD:(2 * hp + m + 1) * HD],
                                 pt[:, m * S + kb * P:m * S + (kb + 1) * P]) for kb in range(2)]) for m in range(2)],
                            out=lambda t, ob, b=b, hp=hp: dve(t, lambda e: e.tensor_copy(
                                y[:, 4 + hp, b * P:(b + 1) * P], ob[:, 0:P]))))
            at = yield from attention(out[-2:] + ready + bias_ready, jobs, bufs)
            return (yield from back(at, 0, [s], lambda k: y[:, k, 0:S]))

        def mixer_mla(after):
            h = mod_norm(after, 1, 1, [LAT, CTX], hT2)
            both = slice(0, 2 * S)
            cq = lambda k: mT[:, k, 0:S]
            ckv = mT[:, 3, :]
            kr = mT[:, 4, :]
            a = project(h, 5, lambda w, t: feature_major(w, hT2, both),
                        lambda e, b, t: e.activation(mT[:, t, :], b[:, :], ACT.Copy))
            r = feature_rstd(a, [mT[:, k, 0:S] for k in range(3)], S)
            n = [dve([r], lambda e, k=k: e.scalar_tensor_tensor(
                out=mT[:, k, 0:S], in0=mT[:, k, 0:S], scalar=small["mla_gq"][:, k:k + 1], in1=rs[:, 1, 0:S],
                op0=ALU.mult, op1=ALU.mult)) for k in range(3)]
            r = feature_rstd([n[-1]], [mT[:, 3, :]], 2 * S)
            n2 = dve([r], lambda e: e.scalar_tensor_tensor(
                out=mT[:, 3, :], in0=mT[:, 3, :], scalar=small["mla_gkv"][:, 0:1], in1=rs[:, 1, :],
                op0=ALU.mult, op1=ALU.mult))
            sc = (P + HD) ** -0.5
            u_q = project([n2], 8, lambda w, t: [(slice(m * S, (m + 1) * S), [
                (w[:, m * 384 + k * P:m * 384 + (k + 1) * P], mT[:, k, 0:S]) for k in range(3)]) for m in range(2)],
                lambda e, b, t: e.activation(mT[:, t + 5, :], b[:, :], ACT.Copy, scale=sc))
            qt = lambda m: mT[:, 5 + m // 2, (m % 2) * S:(m % 2 + 1) * S]
            u0 = state["unit"]
            state["unit"] += 2
            kt_ = lambda hh: hT2[:, hh, :]
            ke = []

            def kpart(eng):
                w = unit_wait(eng, u0, 0, 0)
                for hh in range(KD):
                    last = eng.matmul(bank[hh][:, :], w[:, hh * P:(hh + 1) * P], ckv, start=True, stop=True)
                last.then_inc(unit_done, 1)
            q.part("pe", u_q, kpart)
            ke = [(act if hh % 2 else dve)([(unit_done, u0 + 1)] + a, lambda e, hh=hh: (
                e.activation(kt_(hh), bank[hh][:], ACT.Copy) if hh % 2 else e.tensor_copy(kt_(hh), bank[hh][:])))
                for hh in range(KD)]

            def vpart(eng):
                w = unit_wait(eng, u0, 0, 1)
                for b in range(4):
                    for c in range(2):
                        last = eng.matmul(bank[2 * b + c][:, :], ckv[:, b * P:(b + 1) * P], w[:, c * 512:(c + 1) * 512],
                                          start=True, stop=True)
                last.then_inc(unit_done, 1)
            q.part("pe", ke[-2:], vpart)
            vt = lambda b, hh: mT[:, 13 + 2 * b + hh // 4, (hh % 4) * P:(hh % 4 + 1) * P]
            ve = [(act if c else dve)([(unit_done, u0 + 2)], lambda e, b=b, c=c: (
                e.activation(mT[:, 13 + 2 * b + c, :], bank[2 * b + c][:], ACT.Copy) if c
                else e.tensor_copy(mT[:, 13 + 2 * b + c, :], bank[2 * b + c][:]))) for b in range(4) for c in range(2)]
            rope = small["rope"]
            ends = []
            for n_, t_ in enumerate([qt(8 + m) for m in range(8)] + [kr[:, 0:S]]):
                m = pe(ve[-2:] + ke[-2:] + (ends[n_ - 4:n_ - 3] if n_ >= 4 else []),
                       lambda e, n_=n_, t_=t_: e.matmul(bank[n_ % 4][:, 0:S], small["rotm"][:, :], t_, start=True, stop=True))
                c = dve([m] + ends[-1:], lambda e, n_=n_: e.tensor_tensor(gs[:, n_ % 2, 0:S], bank[n_ % 4][:, 0:S], rope[:, 1, :], ALU.mult))
                d = dve([m], lambda e, t_=t_: e.tensor_tensor(t_, t_, rope[:, 0, :], ALU.mult))
                ends.append(dve([c, d], lambda e, n_=n_, t_=t_: e.tensor_tensor(t_, t_, gs[:, n_ % 2, 0:S], ALU.add)))
            oT = lambda hh: attn_o[:, hh, :]
            jobs = []
            for b in range(NB):
                for hh in range(NH):
                    r_ = slice((hh % 2) * HD, (hh % 2 + 1) * HD)
                    jobs.append(dict(
                        g=1, nk=2 * S,
                        logits=[[(qt(hh)[:, b * P:(b + 1) * P], kt_(hh)),
                                 (qt(8 + hh)[:, b * P:(b + 1) * P], kr)]],
                        values=lambda pt, hh=hh: [(slice(0, P), [
                            (vt(kb, hh), pt[:, kb * P:(kb + 1) * P]) for kb in range(4)])],
                        out=lambda t, ob, b=b, hh=hh: dve(t, lambda e: e.tensor_copy(
                            attn_o[:, hh, b * P:(b + 1) * P], ob[:, 0:P]))))
            at = drain(attention(ends + ve + ke, jobs, bufs))
            return drain(back(at, 1, [LAT], lambda k: attn_o[:, k, :]))

        done = [loaded]
        for layer in range(DEPTH):
            done = layer_one(layer, done)

        h = norm_tokens(done, small["final_norm_g"])
        block1.close()
        wr = sb(ctx, "wr", [P, SPLIT, UW], F32R)
        wl = sb(ctx, "wl", [P, SPLIT, UW], F32R)
        loads2 = [sem("loads2"), 0]
        for name in ("mla_gq", "mla_gkv", "rope", "rotm", "final_g"):
            a = io[name]
            small[name] = sb(ctx, name + "_sb", list(a.shape))
            l2 = q.dma("act", h, small[name][:], a, loads2)
        with ExitStack() as for_ffn:
            fT = sb(for_ffn, "fT", [P, KF, 2 * S])
            hr = sb(for_ffn, "hr", [P, KD, 2 * S], F32R)
            hl = sb(for_ffn, "hl", [P, KD, 2 * S], F32R)
            fr = sb(for_ffn, "fr", [P, 2, 2 * S], F32R)
            fl_ = sb(for_ffn, "fl_", [P, 2, 2 * S], F32R)
        with ExitStack() as for_mixers:
            hT2 = sb(for_mixers, "hT2", [P, KD, 2 * S])
            mT = sb(for_mixers, "mT", [P, KF, 2 * S])
            attn_o = sb(for_mixers, "attn_o", [P, NH, S])
            small["na_bias"] = sb(for_mixers, "na_bias_sb", list(io["na_bias"].shape))
        mT_one = mT[:, 0:KF // 2, :].rearrange("p a (b t) -> p (a b) t", t=S)
        hT_one = hT2[:, 0:4, :].rearrange("p a (b t) -> p (a b) t", t=S)
        done = ffn(h, 0, 0, [LAT])
        bias_load = q.dma("act", done + [l2], small["na_bias"][:], io["na_bias"], [sem("bias_load"), 0])
        done = drain(mixer_ab(done, LAT, hT_one, mT_one, hT_one, [bias_load]))
        done = ffn(done, 0, 2, [LAT])
        done = ffn(done, 1, 0, [LAT, CTX])
        done = mixer_mla(done)
        done = ffn(done, 1, 2, [LAT])
        r = feature_rstd(done, [xs[LAT][:, k, :] for k in range(KD)], S)
        f = [dve([r], lambda e, k=k: e.scalar_tensor_tensor(
            out=hT_one[:, k, :], in0=xs[LAT][:, k, :], scalar=small["final_g"][:, k:k + 1], in1=rs[:, 1, 0:S],
            op0=ALU.mult, op1=ALU.mult)) for k in range(KD)]
        stored = [sem("stored"), 0]
        o = q.dma("act", f, io["out"], hT_one, stored)
        q.part("act", [o], lambda e: None)
        assert state["unit"] == n_units, (state["unit"], n_units)

        block = ctx.enter_context(nc.Block())
        for name, deco in (("sp", block.sync), ("pe", block.tensor), ("act", block.scalar),
                           ("dve", block.vector), ("pool", block.gpsimd)):
            @deco
            def _(eng, name=name):
                for run in q.work[name]:
                    run(eng)


def _tiles(w):
    K, M = w.shape
    return w.reshape(K // P, P, M // P, P).transpose(2, 1, 0, 3).reshape(M // P, P, K)


def _rows(w, kpu=1):
    K, N = w.shape
    return w.reshape(K // P // kpu, kpu, P, N).transpose(0, 2, 1, 3).reshape(-1, P, kpu * N)


def _cols(a):
    a = np.asarray(a)
    b = a.reshape(a.shape[:-1] + (a.shape[-1] // P, P))
    return np.ascontiguousarray(np.moveaxis(b, -1, 0))


def _bucket(dist):
    n = np.maximum(dist, 0)
    nf = np.maximum(n, 1).astype(np.float32)
    large = 16 + (np.log(nf / np.float32(16)) / np.float32(math.log(8)) * np.float32(16)).astype(np.int32)
    return np.where(n < 16, n, np.minimum(large, 31))


def _layout(v):
    f = np.float32
    runs = {}
    for L in range(DEPTH):
        w = v["w_in"][L]
        dq, dk, dv, fq, fk, fv = (w[:, i * 512:(i + 1) * 512] for i in range(6))
        g = w[:, 3080:]
        runs[f"one{L}"] = [_tiles(dq), _tiles(fq), _tiles(dk), _tiles(fk), _tiles(g),
                           _rows(np.concatenate([dv, fv], 1)),
                           np.concatenate([_tiles(v["w_diff_o"][L]), _tiles(v["w_fox_o"][L])], 2),
                           _rows(v["w_out"][L]), _tiles(v["w_query"][L])]
        runs[f"ada{L}"] = [_tiles(v["ada_w_2"][L])]
        for j in range(2):
            gu = np.stack([_tiles(v["ffn_w_gate_2"][L, j]), _tiles(v["ffn_w_up_2"][L, j])], 1)
            runs[f"ffn{L}{j}"] = [gu.reshape(2 * KF, P, UW), _rows(v["ffn_w_down_2"][L, j])]
    ab = v["ab_w_in_2"][0]
    runs["ab"] = [_tiles(ab[:, 0:1536]), _rows(ab[:, 1536:], 2), _tiles(v["ab_w_out_2"][0])]
    wi = v["mla_w_in_2"][0]
    uq = v["mla_w_uq_2"][0].reshape(384, 8, 192)
    wr = np.concatenate([uq[:, :, 128:], np.zeros((384, 8, HD), f)], 2)
    uq = np.concatenate([uq[:, :, :128].reshape(384, 1024), wr.reshape(384, 1024)], 1)
    uq = _tiles(uq).reshape(8, 2, P, 384).transpose(0, 2, 1, 3).reshape(8, P, 768)
    uq = np.concatenate([uq, np.zeros((8, P, UW - 768), f)], 2)
    runs["mla"] = [_tiles(np.concatenate([wi, wi[:, 512:]], 1)), uq,
                   v["mla_w_uk_2"][0][None], v["mla_w_uv_2"][0][None], _tiles(v["mla_w_o_2"][0])]
    places, at = {}, 0
    for name, parts in runs.items():
        n = sum(a.shape[0] for a in parts)
        places[name] = (at, n)
        at += n
    io = {"stream": np.concatenate([a for parts in runs.values() for a in parts], 0)}
    io["x"] = v["x"][0].reshape(NB, P, D).transpose(1, 0, 2)
    io["half"] = np.kron(np.eye(2), np.full((HD, 1), HD ** -0.5)).astype(f)
    io["ident"] = np.eye(P, dtype=f)
    p = np.arange(P)[:, None]
    dist = P + p - np.arange(S)[None]
    io["causal"] = np.where(dist >= 0, 0, NEG).astype(f)
    rel = v["rel_bias"][_bucket(dist)].transpose(0, 2, 1)
    io["relb"] = np.where(dist[:, None, :] >= 0, rel, f(NEG))
    for n in ("norm1_g", "norm2_g", "final_norm_g"):
        io[n] = _cols(v[n])
    io["norm2_rows"] = np.repeat(v["norm2_g"][:, None], P, 1)
    io["subln_g"] = v["diff_subln_g"].T
    io["lam"] = np.repeat(v["diff_lambda"][None], P, 0)
    io["b_forget"] = np.repeat(v["b_forget"][None], P, 0)
    tri = (np.arange(S)[:, None] <= np.arange(S)[None]).astype(f)
    io["tri"] = tri.reshape(NB, P, S).transpose(1, 0, 2)
    io["pick"] = np.concatenate([np.eye(NH), -np.eye(NH)], 1).astype(f)
    io["w_ff"] = v["w_in"][:, :, 3072:3080].reshape(DEPTH, KD, P, NH).transpose(2, 0, 1, 3)
    io["keysT"] = v["sub_keys"].transpose(3, 0, 1, 2)
    io["iota16"] = np.repeat(np.arange(TOPK, dtype=f)[None], P, 0)
    for L in range(DEPTH):
        io[f"expert_u{L}"], io[f"expert_v{L}"] = v["expert_u"][L], v["expert_v"][L]
    io["ctxT"] = v["ctx_2"][0].T.reshape(KD, P, S).transpose(1, 0, 2)
    io["cond"] = np.stack([_cols(v["c_2"][0]), _cols(v["c_ctx_2"])], -1)
    io["ada_b"] = _cols(v["ada_b_2"])
    io["norm_g"] = _cols(v["norm_g_2"])
    io["ones"] = np.stack([np.full((P, P), 1.0 / n, f) for n in (D, 384, P)], 1)
    col = np.arange(64)
    start = np.clip(col - 8, 0, 48)
    inside = (col[None] >= start[:, None]) & (col[None] < start[:, None] + 16)
    off = np.clip(col[None] - col[:, None] + 15, 0, 30)
    row = np.arange(4)[None] - np.arange(4)[:, None] + 7
    rp = v["ab_rpb_2"][0][:, row[:, None, :, None], off[None, :, None, :]]
    rp = np.where(inside[None, None, :, None, :], rp, f(NEG)).reshape(NH, NB, P, S)
    io["na_bias"] = rp.transpose(2, 1, 0, 3).reshape(P, NB * NH, S)
    k = np.arange(P)
    a = 2 * np.pi * ((k[:, None] * k[None]) % P) / P
    io["cdft"] = np.concatenate([np.cos(a), np.sin(a)], 1).astype(f)
    k = np.arange(S)
    a = 2 * np.pi * ((k[:, None] * k[None]) % S) / S
    s = 1 / math.sqrt(S * P)
    td = np.stack([np.cos(a) * s, -np.sin(a) * s], 1).astype(f)
    io["tdft"] = td.reshape(NB, P, 2, S).transpose(1, 0, 2, 3)
    io["mla_gq"] = _cols(v["mla_g_q_2"][0])
    io["mla_gkv"] = _cols(v["mla_g_kv_2"][0])
    pos = np.arange(S)
    inv = f(10000.0) ** (-np.arange(0, 32, 2, dtype=f) / f(32))
    ar, ac = (pos // 64).astype(f)[:, None] * inv, (pos % 64).astype(f)[:, None] * inv
    ang = np.concatenate([ar, ar, ac, ac], -1)
    io["rope"] = np.stack([np.tile(np.cos(ang).T, (2, 1)), np.tile(np.sin(ang).T, (2, 1))], 1).astype(f)
    rot = np.zeros((P, P), f)
    for b in range(0, P, 32):
        for j in range(16):
            rot[b + 16 + j, b + j] = -1
            rot[b + j, b + 16 + j] = 1
    io["rotm"] = rot
    io["final_g"] = _cols(v["final_g_2"])
    return {k_: np.ascontiguousarray(a_) for k_, a_ in io.items()}, places


def kernel(**inputs):
    import concourse.bacc as bacc
    from concourse.bass_utils import run_bass_kernel_spmd

    arrays, places = _layout({k: np.asarray(v) for k, v in inputs.items()})
    nc = bacc.Bacc("TRN2", target_bir_lowering=False, num_devices=1)
    io = {n: nc.dram_tensor("in_" + n, a.shape, F32, kind="ExternalInput").ap() for n, a in arrays.items()}
    io["out"] = nc.dram_tensor("out_0", (P, KD, S), F32, kind="ExternalOutput").ap()
    program(nc, io, places)
    r = run_bass_kernel_spmd(nc, [{"in_" + n: a for n, a in arrays.items()}], core_ids=[0])
    got = r.results[0]["out_0"]
    return np.ascontiguousarray(got.transpose(2, 1, 0).reshape(1, S, D))
```

```python
import math
from contextlib import ExitStack

import numpy as np

import concourse.bass as bass
from concourse import mybir

F32 = mybir.dt.float32
F32R = mybir.dt.float32r
U32 = mybir.dt.uint32
ALU = mybir.AluOpType
ACT = mybir.ActivationFunctionType
AX = mybir.AxisListType.X

P = 128
D = 1024
KD = D // P
S = 256
NB = S // P
DEPTH = 2
EPS = 1e-6
HD = 64
NH = 8
ND = 4
NKEYS = 128
TOPK = 16
PH = 8
SLOTS = PH * TOPK
DFF = 2816
KF = DFF // P
NMOD = 9
NEG = -1e30
RING = 8
UW = 1024
SPLIT = 4
GROUP = 8
ADA_BUFS = 4


ORDER = ("one0", "ffn00", "one1", "ab", "ffn01", "ffn00", "ab", "ffn01", "ffn10", "mla", "ffn11")


def lam_init(layer):
    return 0.8 - 0.6 * math.exp(-0.3 * layer)


class Queues:

    ENGINES = ("pe", "act", "dve", "pool", "sp")

    def __init__(self, sem):
        self.sem = {e: sem(f"{e}_done") for e in self.ENGINES}
        self.count = {e: 0 for e in self.ENGINES}
        self.work = {e: [] for e in self.ENGINES}
        self.seen = {e: {} for e in self.ENGINES}

    def wait(self, e, eng, tokens):
        for s, v in tokens:
            if self.seen[e].get(id(s), 0) < v:
                eng.wait_ge(s, v)
                self.seen[e][id(s)] = v

    def op(self, e, tokens, emit):
        self.count[e] += 1

        def run(eng):
            self.wait(e, eng, tokens)
            emit(eng).then_inc(self.sem[e], 1)
        self.work[e].append(run)
        return (self.sem[e], self.count[e])

    def many(self, e, tokens, emits):
        self.count[e] += 1

        def run(eng):
            self.wait(e, eng, tokens)
            for emit in emits:
                last = emit(eng)
            last.then_inc(self.sem[e], 1)
        self.work[e].append(run)
        return (self.sem[e], self.count[e])

    def part(self, e, tokens, run_part):
        def run(eng):
            self.wait(e, eng, tokens)
            run_part(eng)
        self.work[e].append(run)

    def dma(self, e, tokens, out, in_, sem_count):
        sem_count[1] += 16
        value = sem_count[1]

        def run(eng):
            self.wait(e, eng, tokens)
            eng.dma_start(out, in_).then_inc(sem_count[0], 16)
        self.work[e].append(run)
        return (sem_count[0], value)


def turns(eng, n, body, head=0, tail=0, width=RING):
    for st in range(head):
        body(0, st)
    k = (n - head - tail) // width
    at = head
    if k >= 2:
        with eng.Fori(0, k) as i:
            for j in range(width):
                body(i, head + j)
        at = head + k * width
    for st in range(at, n):
        body(0, st)


class Steps:

    def __init__(self, steps):
        self.steps, self.live, self.result = steps, True, None

    def step(self):
        try:
            next(self.steps)
        except StopIteration as end:
            self.live, self.result = False, end.value

    def finish(self):
        while self.live:
            self.step()
        return self.result


def drain(steps):
    return Steps(steps).finish()


def program(nc, io, places):
    with ExitStack() as ctx:
        sem = lambda name: ctx.enter_context(nc.semaphore(name))
        q = Queues(sem)
        pe = lambda t, f: q.op("pe", t, f)
        act = lambda t, f: q.op("act", t, f)
        dve = lambda t, f: q.op("dve", t, f)

        bank = [ctx.enter_context(nc.psum_tensor(f"bank{i}", [P, 512], F32)) for i in range(8)]

        def sb(stack, name, shape, dt=F32):
            return stack.enter_context(nc.sbuf_tensor(name, shape, dt))

        ring = sb(ctx, "ring", [P, RING, UW])
        slot_full = [sem(f"slot_full{i}") for i in range(RING)]
        unit_done = sem("unit_done")
        evac = sem("evac")
        w_high = sem("w_high")
        w_low = sem("w_low")
        f_high, f_low = sem("f_high"), sem("f_low")
        ada_full = [sem(f"ada_full{i}") for i in range(ADA_BUFS)]
        ada_kept = sem("ada_kept")
        ada_used = sem("ada_used")
        half_done = sem("half_done")
        state = dict(unit=0, evac=0, half=0, split=0, fsplit=0)
        segments = [places[name] for name in ORDER]
        n_units = sum(n for _, n in segments)

        loads = [sem("loads"), 0]
        small = {}

        def load(name, stack=ctx):
            a = io[name]
            small[name] = sb(stack, name + "_sb", list(a.shape))
            return q.dma("act", [], small[name][:], a, loads)

        load("ident")
        load("half")
        for name in ("ada_b", "norm_g", "ones", "cdft", "tdft"):
            load(name)
        stat = sb(ctx, "stat", [P, 2, 16])
        attn_p = sb(ctx, "attn_p", [P, 2, 512])
        attn_pt = sb(ctx, "attn_pt", [P, 2, 512])
        bufs = dict(p=[attn_p[:, i, :] for i in range(2)], pt=[attn_pt[:, i, :] for i in range(2)], stat=stat)
        hT = sb(ctx, "hT", [P, KD, S])
        xc = sb(ctx, "xc", [P, KD, S])
        ctxK = sb(ctx, "ctxK", [P, 4, S])
        ctxV = sb(ctx, "ctxV", [P, NB, 512])
        gs = sb(ctx, "gs", [P, 2, 512])
        rs = sb(ctx, "rs", [P, 2, 512])
        mods = sb(ctx, "mods", [P, DEPTH, NMOD * KD, 2])
        gA = sb(ctx, "gA", [P, DEPTH, 3, KD, 2])
        mod_now = sb(ctx, "mod_now", [P, KD, 2])
        junk = sb(ctx, "junk", [P, D])
        q.dma("act", [], xc[:], io["ctxT"], loads)

        block1 = ExitStack()
        x = sb(block1, "x", [P, NB, D])
        loaded = q.dma("act", [], x[:], io["x"], loads)
        for name in ("causal", "norm1_g", "norm2_g", "final_norm_g", "subln_g", "lam", "b_forget",
                     "tri", "pick", "relb", "w_ff", "keysT", "iota16"):
            loaded = load(name, block1)
        ident = small["ident"]

        def stream(sp):
            u0 = 0
            for start, n in segments:
                def step(i, st, start=start, u0=u0):
                    u = u0 + st
                    if u >= RING:
                        sp.wait_ge(unit_done, i * RING + (u - RING + 1))
                    sp.dma_start(ring[:, u % RING, :], io["stream"][i * RING + start + st]
                                 ).then_inc(slot_full[u % RING], 16)
                turns(sp, n, step, head=0 if u0 else RING)
                u0 += n
        q.part("sp", [], stream)

        def unit_wait(eng, u0, i, st):
            u = u0 + st
            eng.wait_ge(slot_full[u % RING], (i + (u // RING + 1)) * 16)
            return ring[:, u % RING, :]

        def project(after, n, mms, evacs, dve_evac=False):
            u0, e0 = state["unit"], state["evac"]
            state["unit"] += n
            state["evac"] += n

            def pe_part(eng):
                def step(i, st):
                    w = unit_wait(eng, u0, i, st)
                    eng.wait_ge(evac, i * RING + max(0, e0 + st - 3))
                    out = bank[st % 4]
                    for cols, terms in mms(w, st):
                        for t, (lhsT, rhs) in enumerate(terms):
                            last = eng.matmul(out[:, cols], lhsT, rhs, start=(t == 0), stop=(t == len(terms) - 1))
                    last.then_inc(unit_done, 1)
                turns(eng, n, step, head=4 if n >= 4 else 0)
            q.part("pe", after, pe_part)

            def out_part(eng):
                def step(i, st):
                    eng.wait_ge(unit_done, i * RING + (u0 + st + 1))
                    evacs(eng, bank[st % 4], i * RING + st).then_inc(evac, 1)
                turns(eng, n, step, head=4 if n >= 4 else 0)
            q.part("dve" if dve_evac else "act", after, out_part)
            return [(evac, e0 + n)]

        def two_heads(e, bk, dst, t, first, T):
            for m in range(2):
                last = e.activation(dst[:, first + 2 * t + m, 0:T], bk[:, 0:T], ACT.Copy, scale=small["half"][:, m:m + 1])
            return last

        def feature_major(w, actT, cols, kt=KD, first=0):
            return [(slice(0, cols.stop - cols.start),
                     [(w[:, (first + k) * P:(first + k + 1) * P], actT[:, k, cols]) for k in range(kt)])]

        def token_major(after, n, act_of, width, kpu, blocks):
            u0 = state["unit"]
            state["unit"] += n

            def pe_part(eng):
                for st in range(n):
                    w = unit_wait(eng, u0, 0, st)
                    for kk in range(kpu):
                        k = st * kpu + kk
                        for b in range(blocks):
                            for c in range(width // 512):
                                last = eng.matmul(bank[b * (width // 512) + c][:, :], act_of(k, b),
                                                  w[:, kk * width + c * 512:kk * width + (c + 1) * 512],
                                                  start=(k == 0), stop=(k == n * kpu - 1))
                    last.then_inc(unit_done, 1)
            q.part("pe", after, pe_part)
            return [(unit_done, u0 + n)]

        def unit_mm(tokens, mms):
            u0 = state["unit"]
            state["unit"] += 1

            def part(eng):
                w = unit_wait(eng, u0, 0, 0)
                for o, a, b, first, last_ in mms(w):
                    last = eng.matmul(o, a, b, start=first, stop=last_)
                last.then_inc(unit_done, 1)
            q.part("pe", tokens, part)
            return (unit_done, u0 + 1)

        def attention(after, jobs, bufs):
            hist = []
            for n, job in enumerate(jobs):
                g, nk = job["g"], job["nk"]
                lb, tb, ob = bank[n % 2], bank[2 + n % 2], bank[4 + n % 2]
                pr, pt = bufs["p"][n % 2], bufs["pt"][n % 2]
                mx, sm = bufs["stat"][:, n % 2, 0:g], bufs["stat"][:, n % 2, 4:4 + g]
                rc = bufs["stat"][:, n % 2, 8:8 + g]
                old = hist[n - 2] if n >= 2 else None
                lw = after + (old["exp"] if old else [])
                mm = []
                parts = job["logits"]
                wide = g * nk // len(parts)
                for gg, terms in enumerate(parts):
                    for t, (lhsT, rhs) in enumerate(terms):
                        mm.append(lambda e, o=lb[:, gg * wide:(gg + 1) * wide], a=lhsT, b=rhs, s=(t == 0),
                                  z=(t == len(terms) - 1): e.matmul(o, a, b, start=s, stop=z))
                lg = q.many("pe", lw, mm)
                l3 = lb[:, 0:g * nk].rearrange("p (g k) -> p g k", g=g)
                mt = dve([lg] + (old["exp"] + old["w"] if old else []),
                         lambda e, o=mx, i=l3: e.tensor_reduce(o, i, AX, ALU.max, negate=True))
                ex = []
                for gg in range(g):
                    ex.append(act([mt] + ([old["tr"]] if old else []),
                                  lambda e, o=pr[:, gg * nk:(gg + 1) * nk], i=lb[:, gg * nk:(gg + 1) * nk],
                                  b=mx[:, gg:gg + 1], s=sm[:, gg:gg + 1]:
                                  e.activation(o, i, ACT.Exp, bias=b, accum_out=s)))
                rt = dve([ex[-1]], lambda e, o=rc, i=sm: e.reciprocal(o, i))
                wt = []
                if job.get("mix") is not None:
                    lt = dve([rt], lambda e, o=rc[:, 1:2], m=job["mix"]: e.tensor_scalar(o, o, m, None, ALU.mult))
                    w0 = dve([rt], lambda e, o=pr[:, 0:nk], r=rc[:, 0:1]: e.tensor_scalar(o, o, r, None, ALU.mult))
                    wt = [dve([lt, w0], lambda e, o=pr[:, 0:nk], i=pr[:, nk:2 * nk], r=rc[:, 1:2]:
                              e.scalar_tensor_tensor(out=o, in0=i, scalar=r, in1=o, op0=ALU.mult, op1=ALU.add))]
                    wide = nk
                else:
                    wide = g * nk
                    for gg in range(g):
                        wt.append(dve([rt], lambda e, o=pr[:, gg * nk:(gg + 1) * nk], r=rc[:, gg:gg + 1]:
                                      e.tensor_scalar(o, o, r, None, ALU.mult)))
                nt = wide // P
                hist.append(dict(exp=ex, w=wt, wide=wide, nt=nt, job=job, wt=wt, pr=pr, pt=pt, tb=tb, ob=ob))
                if n >= 2:
                    weigh_values(hist, n - 2)
                if n >= 1:
                    transpose_weights(hist, n - 1)
                yield
            n = len(jobs)
            if n > 1:
                weigh_values(hist, n - 2)
            transpose_weights(hist, n - 1)
            weigh_values(hist, n - 1)
            return [hist[-1]["out"], hist[-1]["copy"]] + ([hist[-2]["out"]] if len(hist) > 1 else [])

        def transpose_weights(hist, n):
            h = hist[n]
            old = hist[n - 2] if n >= 2 else None
            pr, pt, tb, nt = h["pr"], h["pt"], h["tb"], h["nt"]
            h["tr"] = q.many("pe", h["wt"] + ([old["copy"]] if old else []), [
                (lambda e, c=c: e.transpose(tb[:, c * P:(c + 1) * P], pr[:, c * P:(c + 1) * P], ident[:]))
                for c in range(nt)])
            h["copy"] = act([h["tr"]] + ([old["pv"]] if old else []),
                            lambda e: e.activation(pt[:, 0:nt * P], tb[:, 0:nt * P], ACT.Copy))

        def weigh_values(hist, n):
            h = hist[n]
            old = hist[n - 2] if n >= 2 else None
            job, pt, ob = h["job"], h["pt"], h["ob"]
            mm = []
            for orow, terms in job["values"](pt):
                for t, (lhsT, rhs) in enumerate(terms):
                    mm.append(lambda e, o=ob[orow, 0:P], a=lhsT, b=rhs, s=(t == 0), z=(t == len(terms) - 1):
                              e.matmul(o, a, b, start=s, stop=z))
            h["pv"] = q.many("pe", [h["copy"]] + ([old["out"]] if old else []), mm)
            h["out"] = job["out"]([h["pv"]], ob)

        def rstd_of(after, ss, tmp, scale):
            a = dve(after, lambda e: e.tensor_scalar(tmp, ss, scale, EPS, ALU.mult, ALU.add))
            b = act([a], lambda e: e.activation(ss, tmp, ACT.Sqrt))
            c = dve([b], lambda e: e.reciprocal(tmp, ss))
            return dve([c], lambda e: e.tensor_copy(ss, tmp))

        t_tok = sb(block1, "t_tok", [P, NB, D])
        sq = sb(block1, "sq", [P, NB, D])
        qkT = sb(block1, "qkT", [P, 24, S])
        gring = sb(block1, "gring", [P, GROUP, D])
        gateT = gring[:, 0:4, :].rearrange("p a (b t) -> p (a b) t", t=S)
        mergedT = gring[:, 4:6, :].rearrange("p a (b t) -> p (a b) t", t=S)
        v_tok = gring[:, 6:8, :]
        heads = sb(block1, "heads", [P, 2 * ND, S])
        dT, fT1 = heads[:, 0:ND, :], heads[:, ND:2 * ND, :]
        cand = sb(block1, "cand", [P, 2, TOPK * TOPK])
        scores = [qkT[:, 16:24, :].rearrange("p a (b n) -> p (a b) n", n=NKEYS),
                  heads[:, :, :].rearrange("p a (b n) -> p (a b) n", n=NKEYS)]
        ss = sb(block1, "ss", [P, 8])
        ss2 = sb(block1, "ss2", [P, 8])
        fl = sb(block1, "fl", [P, 4, NB * NH])
        cT = sb(block1, "cT", [NH, S])
        lamb = sb(block1, "lamb", [P, 8])
        lprod = sb(block1, "lprod", [P, 2, HD])
        topv = sb(block1, "topv", [P, 2 * PH, TOPK])
        topi = sb(block1, "topi", [P, 2 * PH, TOPK], U32)
        topf = sb(block1, "topf", [P, 2 * PH, TOPK])
        bestv = sb(block1, "bestv", [P, PH, TOPK])
        besti = sb(block1, "besti", [P, PH, TOPK], U32)
        bi2 = sb(block1, "bi2", [P, 2, PH, TOPK], U32)
        bf2 = sb(block1, "bf2", [P, 2, PH, TOPK])
        expf = sb(block1, "expf", [P, NB, SLOTS])
        gates = sb(block1, "gates", [P, NB, SLOTS])
        gsum = sb(block1, "gsum", [P, PH])
        idx = sb(block1, "idx", [P, 2, GROUP], U32)
        pre = sb(block1, "pre", [P, 2, GROUP])
        gel = sb(block1, "gel", [P, GROUP])
        wts = sb(block1, "wts", [P, GROUP])

        def norm_tokens(after, g, out_tok=None, outT=hT, cols=0):
            s0 = [act(after, lambda e, b=b: e.activation(sq[:, b, :], x[:, b, :], ACT.Square,
                                                        accum_out=ss[:, b:b + 1])) for b in range(NB)]
            r = rstd_of(s0, ss[:, 0:NB], ss2[:, 0:NB], 1.0 / D)
            n = [dve([r], lambda e, b=b: e.tensor_scalar(sq[:, b, :], x[:, b, :], ss[:, b:b + 1], None, ALU.mult))
                 for b in range(NB)]
            ends = []
            for b in range(NB):
                for c in range(2):
                    i = b * 2 + c
                    tr = q.many("pe", [n[b]] + after, [
                        (lambda e, i=i, k=k, b=b, c=c: e.transpose(
                            bank[i][:, k * P:(k + 1) * P], sq[:, b, (c * 4 + k) * P:(c * 4 + k + 1) * P], ident[:]))
                        for k in range(4)])
                    for k in range(4):
                        kk = c * 4 + k
                        o, s, gg = outT[:, kk, cols + b * P:cols + (b + 1) * P], bank[i][:, k * P:(k + 1) * P], g[:, kk:kk + 1]
                        if c:
                            ends.append(dve([tr], lambda e, o=o, s=s, gg=gg: e.tensor_scalar(o, s, gg, None, ALU.mult)))
                        else:
                            ends.append(act([tr], lambda e, o=o, s=s, gg=gg: e.activation(o, s, ACT.Copy, scale=gg)))
            if out_tok is not None:
                gr = io_rows["norm2"]
                ends += [dve([n[b]] + gr[1], lambda e, b=b: e.tensor_tensor(out_tok[:, b, :], sq[:, b, :], gr[0], ALU.mult))
                         for b in range(NB)]
            return ends

        g2row = sb(block1, "g2row", [P, D])
        io_rows = {}

        ada_w = [t_tok[:, 0, :], t_tok[:, 1, :], gring[:, 4, :], gring[:, 5, :]]
        cond = [gs[:, :, :].rearrange("p a b -> p (a b)"), rs[:, :, :].rearrange("p a b -> p (a b)")]

        class Modulation:

            def __init__(self, L, after):
                self.L, self.n, self.at = L, NMOD * KD, 0
                self.u0 = L * self.n
                cl = [q.dma("act", after, cond[s], io["cond"][s], loads) for s in range(2)]
                self.cond = [act(cl, lambda e, s=s: e.activation(cond[s], cond[s], ACT.Silu)) for s in range(2)]

                def load_units(eng):
                    def step(i, st):
                        u = self.u0 + st
                        if u >= ADA_BUFS:
                            eng.wait_ge(ada_used, i * (2 * RING) + 2 * (u - ADA_BUFS + 1))
                        eng.dma_start(ada_w[u % ADA_BUFS], io["ada"][i * RING + u]).then_inc(ada_full[u % ADA_BUFS], 16)
                    turns(eng, self.n, step, head=RING)
                q.part("pool", after, load_units)

            def unit(self, eng, i, u, sums):
                w = ada_w[u % ADA_BUFS]
                eng.wait_ge(ada_full[u % ADA_BUFS], i * (RING // ADA_BUFS * 16) + (u // ADA_BUFS + 1) * 16)
                if u:
                    eng.wait_ge(ada_used, i * (2 * RING) + (2 * u - 1))
                for s, out in enumerate((junk[:], w)):
                    eng.tensor_tensor_reduce(out=out, in0=w, in1=cond[s], scale=1.0, scalar=0.0, op0=ALU.mult,
                                             op1=ALU.add, accum_out=sums[:, s:s + 1]).then_inc(ada_used, 1)

            def vectors(self, n):
                v0 = self.L * n
                self.at = n * KD

                def part(eng):
                    with eng.Fori(0, n) as i:
                        eng.wait_ge(ada_kept, i + v0)
                        for k in range(KD):
                            self.unit(eng, i, self.u0 + k, mod_now[:, k, :])
                        eng.wait_ge(ada_used, i * (2 * KD) + 2 * (self.u0 + KD))
                        eng.tensor_copy(mods[:, self.L, bass.ds(i * KD, KD), :], mod_now[:]).then_inc(ada_kept, 1)
                q.part("dve", self.cond, part)

            def product(self):
                at = self.at
                self.at += 1
                q.part("dve", self.cond, lambda eng: self.unit(eng, 0, self.u0 + at, mods[:, self.L, at, :]))

            def finish(self):
                assert self.at == self.n
                L, n = self.L, self.n
                a = dve([(ada_used, 2 * (self.u0 + n)), (ada_kept, (L + 1) * (n // KD - 2))], lambda e: e.tensor_tensor(
                    mods[:, L], mods[:, L], small["ada_b"][:, L, :].unsqueeze(2).to_broadcast([P, n, 2]), ALU.add))
                for j in range(3):
                    b = dve([a], lambda e, j=j: e.tensor_scalar(gA[:, L, j], mods[:, L, (3 * j + 1) * KD:(3 * j + 2) * KD, :],
                                                                1.0, None, ALU.add))
                    r = dve([b], lambda e, j=j: e.tensor_tensor(
                        gA[:, L, j], gA[:, L, j], small["norm_g"][:, L, j, :].unsqueeze(2).to_broadcast([P, KD, 2]), ALU.mult))
                    if j != 1:
                        gate = mods[:, L, (3 * j + 2) * KD:(3 * j + 3) * KD, :]
                        r = dve([a], lambda e, gate=gate: e.tensor_scalar(gate, gate, 0.5, None, ALU.mult))
                return [r]

        def layer_one(layer, after):
            L = layer
            rowt = q.dma("act", after, g2row[:], io["norm2_rows"][L], loads)
            io_rows["norm2"] = (g2row[:, :], [rowt])
            h = norm_tokens(after, small["norm1_g"][:, L])
            lm = small["lam"]
            a = [dve(after, lambda e, j=j: e.tensor_tensor(lprod[:, j, :], lm[:, L, 2 * j, :], lm[:, L, 2 * j + 1, :], ALU.mult))
                 for j in range(2)]
            a = dve(a, lambda e: e.tensor_reduce(lamb[:, 0:2], lprod[:], AX, ALU.add))
            a = act([a], lambda e: e.activation(lamb[:, 2:4], lamb[:, 0:2], ACT.Exp))
            a = dve([a], lambda e: e.tensor_tensor(lamb[:, 4:5], lamb[:, 3:4], lamb[:, 2:3], ALU.subtract))
            neg_lam = dve([a], lambda e: e.tensor_scalar(lamb[:, 5:6], lamb[:, 4:5], -lam_init(L), None, ALU.add))
            sg = dve([neg_lam], lambda e: e.tensor_scalar(lamb[:, 6:7], small["subln_g"][:, L:L + 1], 1.0 - lam_init(L),
                                                          None, ALU.mult))
            ada = Modulation(L, after)
            allT = slice(0, S)
            qd = project(h, 8, lambda w, t: feature_major(w, hT, allT),
                         lambda e, b, t: two_heads(e, b, qkT, t, 0, S))
            kd = project([], 8, lambda w, t: feature_major(w, hT, allT),
                         lambda e, b, t: e.activation(qkT[:, t + 16, :], b[:, 0:S], ACT.Copy))
            gd = project([], 16, lambda w, t: feature_major(w, hT, allT),
                         lambda e, b, t: e.activation(gateT[:, t, :], b[:, 0:S], ACT.Sigmoid))
            ada.vectors(NMOD - 2)
            vd = token_major(gd, KD, lambda k, b: hT[:, k, b * P:(b + 1) * P], D, 1, NB)
            ve = []
            for b in range(NB):
                for c in range(2):
                    f = act if c else dve
                    ve.append(f(vd, lambda e, b=b, c=c: (e.activation(v_tok[:, b, c * 512:(c + 1) * 512], bank[2 * b + c][:], ACT.Copy)
                                                         if c else e.tensor_copy(v_tok[:, b, c * 512:(c + 1) * 512], bank[2 * b + c][:]))))
            ffm = q.many("pe", vd + gd, [
                (lambda e, k=k, b=b: e.matmul(bank[4 + b][:, 0:NH], hT[:, k, b * P:(b + 1) * P], small["w_ff"][:, L, k, :],
                                              start=(k == 0), stop=(k == KD - 1)))
                for b in range(NB) for k in range(KD)])
            z, az, ez, ls = (fl[:, j, :] for j in range(4))
            a = [dve([ffm], lambda e, b=b: e.tensor_tensor(z[:, b * NH:(b + 1) * NH], bank[4 + b][:, 0:NH],
                                                           small["b_forget"][:, L, :], ALU.add)) for b in range(NB)]
            b_ = dve(a, lambda e: e.tensor_scalar(az, z, -1.0, None, ALU.mult))
            b_ = dve([b_], lambda e: e.tensor_tensor(az, az, z, ALU.min))
            b_ = act([b_], lambda e: e.activation(ez, az, ACT.Exp))
            b_ = dve([b_], lambda e: e.tensor_scalar(ez, ez, 1.0, None, ALU.add))
            b_ = act([b_], lambda e: e.activation(az, ez, ACT.Ln))
            b_ = dve([b_], lambda e: e.scalar_tensor_tensor(out=ls, in0=z, scalar=0.0, in1=az, op0=ALU.min, op1=ALU.subtract))
            cm = q.many("pe", [b_], [
                (lambda e, b=b: e.matmul(bank[6][0:NH, 0:S], ls[:, b * NH:(b + 1) * NH], small["tri"][:, b, :],
                                         start=(b == 0), stop=(b == NB - 1))) for b in range(NB)])
            cd = act([cm], lambda e: e.activation(cT[:, :], bank[6][0:NH, 0:S], ACT.Copy))
            ready = ve + [cd, neg_lam, sg] + qd + kd
            jobs = []
            o_tok = sq
            for b in range(NB):
                nk = (b + 1) * P
                for hh in range(ND):
                    def out_diff(t, ob, b=b, hh=hh):
                        c = dve(t, lambda e: e.tensor_copy(o_tok[:, b, hh * P:(hh + 1) * P], ob[:, 0:P]))
                        return act([c], lambda e: e.activation(o_tok[:, b, 512 + hh * P:512 + (hh + 1) * P],
                                                               o_tok[:, b, hh * P:(hh + 1) * P], ACT.Square,
                                                               accum_out=ss[:, b * ND + hh:b * ND + hh + 1]))
                    qs = [qkT[:, 2 * hh + m, b * P:(b + 1) * P] for m in range(2)]
                    ks = qkT[:, 16 + hh, 0:nk]
                    jobs.append(dict(
                        g=2, nk=nk, mix=lamb[:, 5:6],
                        logits=[[(qs[m], ks),
                                 (ident[:], small["relb"][:, hh, S - nk:S])] for m in range(2)],
                        values=lambda pt, b=b, hh=hh: [(slice(0, P), [
                            (pt[:, kb * P:(kb + 1) * P], v_tok[:, kb, hh * P:(hh + 1) * P]) for kb in range(b + 1)])],
                        out=out_diff))
            for b in range(NB):
                nk = (b + 1) * P
                for hp in range(NH // 2):
                    qs = [qkT[:, 8 + 2 * hp + m, b * P:(b + 1) * P] for m in range(2)]
                    ks = qkT[:, 20 + hp, 0:nk]
                    jobs.append(dict(
                        g=2, nk=nk,
                        logits=[[(qs[m], ks),
                                 (ident[:], small["causal"][:, S - nk:S]),
                                 (cT[:, b * P:(b + 1) * P], small["pick"][:, 2 * hp + m:2 * hp + m + 1].to_broadcast([NH, nk])),
                                 (small["pick"][:, NH + 2 * hp + m:NH + 2 * hp + m + 1].to_broadcast([NH, P]), cT[:, 0:nk])] for m in range(2)],
                        values=lambda pt, b=b, hp=hp, nk=nk: [(slice(m * HD, (m + 1) * HD), [
                            (v_tok[:, kb, 512 + (2 * hp + m) * HD:512 + (2 * hp + m + 1) * HD],
                             pt[:, m * nk + kb * P:m * nk + (kb + 1) * P]) for kb in range(b + 1)]) for m in range(2)],
                        out=lambda t, ob, b=b, hp=hp: dve(t, lambda e: e.tensor_copy(
                            fT1[:, hp, b * P:(b + 1) * P], ob[:, 0:P]))))
            attn = Steps(attention(ready, jobs, bufs))
            for _ in range(2 * KD):
                attn.step()
                ada.product()
            at = attn.finish()
            modulated = ada.finish()
            r = rstd_of(at, ss[:, 0:8], ss2[:, 0:8], 1.0 / P)
            dd = []
            for b in range(NB):
                n = [dve([r], lambda e, b=b, hh=hh: e.tensor_scalar(
                    o_tok[:, b, hh * P:(hh + 1) * P], o_tok[:, b, hh * P:(hh + 1) * P],
                    ss[:, b * ND + hh:b * ND + hh + 1], None, ALU.mult)) for hh in range(ND)]
                tr = q.many("pe", [n[-1]] + at, [
                    (lambda e, b=b, hh=hh: e.transpose(bank[b][:, hh * P:(hh + 1) * P], o_tok[:, b, hh * P:(hh + 1) * P], ident[:]))
                    for hh in range(ND)])
                dd.append(act([tr], lambda e, b=b: e.activation(
                    dT[:, :, b * P:(b + 1) * P], bank[b][:, :].rearrange("p (h t) -> p h t", h=ND), ACT.Copy,
                    scale=lamb[:, 6:7])))
            u0, e0 = state["unit"], state["evac"]
            state["unit"] += KD
            state["evac"] += KD

            def merge_pe(eng):
                for st in range(KD):
                    w = unit_wait(eng, u0, 0, st)
                    eng.wait_ge(evac, e0 + st - 3)
                    for j, src in enumerate((dT, fT1)):
                        for k in range(ND):
                            last = eng.matmul(bank[st % 4][:, j * S:(j + 1) * S], w[:, (j * ND + k) * P:(j * ND + k + 1) * P],
                                              src[:, k, :], start=(k == 0), stop=(k == ND - 1))
                    last.then_inc(unit_done, 1)
            q.part("pe", dd + at, merge_pe)
            tok = dd + at
            for st in range(KD):
                bk = bank[st % 4]
                m1 = dve(tok + [(unit_done, u0 + st + 1)], lambda e, st=st, bk=bk: e.tensor_tensor(
                    mergedT[:, st, :], bk[:, 0:S], gateT[:, st, :], ALU.mult))
                m2 = dve([], lambda e, st=st, bk=bk: e.tensor_tensor(
                    sq[:, 0, (st % 2) * S:(st % 2 + 1) * S], bk[:, S:2 * S], gateT[:, KD + st, :], ALU.mult))
                q.part("dve", [m1, m2], lambda e, st=st: e.tensor_tensor(
                    mergedT[:, st, :], mergedT[:, st, :], sq[:, 0, (st % 2) * S:(st % 2 + 1) * S], ALU.add).then_inc(evac, 1))
            od = token_major([(evac, e0 + KD)], KD, lambda k, b: mergedT[:, k, b * P:(b + 1) * P], D, 1, NB)
            xe = []
            for b in range(NB):
                for c in range(2):
                    xs = x[:, b, c * 512:(c + 1) * 512]
                    xe.append(dve(od, lambda e, xs=xs, b=b, c=c: e.tensor_tensor(xs, bank[2 * b + c][:], xs, ALU.add)))
            h = norm_tokens(xe, small["norm2_g"][:, L], out_tok=t_tok)
            ev, sc0, tops = [], [], []

            def scores_of(b, h, bk, after):
                m = q.many("pe", after, [
                    (lambda e, c=c: e.matmul(bk[:, c * P:(c + 1) * P], qkT[:, 2 * h + c, b * P:(b + 1) * P],
                                             small["keysT"][:, L, c, :], start=True, stop=True)) for c in range(2)])
                return act([m], lambda e: e.activation(
                    scores[b][:, 2 * h:2 * h + 2, :], bk[:, 0:S].rearrange("p (c n) -> p c n", c=2), ACT.Copy))

            for hh in range(PH + 1):
                if hh < PH:
                    for t in (2 * hh, 2 * hh + 1):
                        bk = bank[t % 4][:, 0:S]
                        m = unit_mm(h + ev[t - 4:t - 3] if t >= 4 else h, lambda w, bk=bk: [
                            (bk, w[:, k * P:(k + 1) * P], hT[:, k, :], k == 0, k == KD - 1) for k in range(KD)])
                        ev.append(act([m], lambda e, t=t, bk=bk: e.activation(qkT[:, t, :], bk, ACT.Copy)))
                if hh:
                    sc0.append(scores_of(0, hh - 1, bank[4 + hh % 2], ev[2 * hh - 1:2 * hh] + sc0[-2:-1]))
                    tops.append(drain(route_head(0, hh - 1, [sc0[-1]])))
            sc1 = [scores_of(1, hh, bank[6 + hh % 2], h + ev[-1:]) if hh < 2 else None for hh in range(2)]
            for hh in range(2, PH):
                sc1.append(scores_of(1, hh, bank[6 + hh % 2], [sc1[hh - 2]]))
            done = drain(route_end(0, tops[-1]))
            side = Steps(chain(route(1, [sc1[-1]]), context_before_ffn(modulated) if L == 0 else mixer_ctx()))
            first = gather(L, 0, done, 0, SLOTS // GROUP, side=side)
            d1, ctx_ready = side.finish()
            up = FfnUp(ctx_ready, hT, qkT)
            down = up.down()
            gather(L, 1, d1 + first, 0, up.groups, beside=up)
            last = gather(L, 1, [], up.groups, SLOTS // GROUP - up.groups)
            ctx_done = residuals(down, 0, 2 * L, [CTX])
            return last + ctx_done[-1:]

        def chain(a, b):
            a, b = Steps(a), Steps(b)
            while a.live or b.live:
                for one in (a, b):
                    if one.live:
                        one.step()
                yield
            return a.result, b.result

        def top16(src, vals, ids, after):
            a = dve(after, lambda e: e.max(out=vals[:, 0:8], in_=src))
            i = dve([a], lambda e: e.max_index(out=ids[:, 0:8], in_max=vals[:, 0:8], in_values=src))
            m = dve([i], lambda e: e.match_replace(out=src, in_to_replace=vals[:, 0:8], in_values=src, imm_value=-3e38))
            a = dve([m], lambda e: e.max(out=vals[:, 8:16], in_=src))
            return dve([a], lambda e: e.max_index(out=ids[:, 8:16], in_max=vals[:, 8:16], in_values=src))

        def route_head(b, h, after):
            for hp in (2 * h, 2 * h + 1):
                e = top16(scores[b][:, hp, :], topv[:, hp, :], topi[:, hp, :], after)
                yield
            c3 = cand[:, h % 2, :].rearrange("p (i j) -> p i j", i=TOPK)
            v1 = topv[:, 2 * h, :].unsqueeze(2).to_broadcast([P, TOPK, TOPK])
            v2 = topv[:, 2 * h + 1, :].unsqueeze(1).to_broadcast([P, TOPK, TOPK])
            c = dve([e], lambda e: e.tensor_tensor(c3, v1, v2, ALU.add))
            return top16(cand[:, h % 2, :], bestv[:, h, :], besti[:, h, :], [c])

        def route(b, after):
            for h in range(PH):
                g = yield from route_head(b, h, after)
                if h < PH - 1:
                    yield
            return (yield from route_end(b, g))

        def route_end(b, g):
            f = dve([g], lambda e: e.tensor_copy(topf[:], topi[:]))
            a = dve([g], lambda e: e.tensor_scalar(bi2[:, 0], besti[:], 4, None, ALU.logical_shift_right))
            c = dve([g], lambda e: e.tensor_scalar(bi2[:, 1], besti[:], 15, None, ALU.bitwise_and))
            a = dve([a, c], lambda e: e.tensor_copy(bf2[:], bi2[:]))
            oh = scores[b].rearrange("p a n -> p (a n)").rearrange("p (h s j) -> p h s j", h=PH, s=TOPK)
            t3 = topf[:, :, :].rearrange("p (h two) j -> p h two j", two=2)
            for half in range(2):
                yield
                sel = bf2[:, half].unsqueeze(3).to_broadcast([P, PH, TOPK, TOPK])
                io4 = small["iota16"][:, :].unsqueeze(1).unsqueeze(1).to_broadcast([P, PH, TOPK, TOPK])
                src = t3[:, :, half, :].unsqueeze(2).to_broadcast([P, PH, TOPK, TOPK])
                c = dve([a, f], lambda e, sel=sel, io4=io4: e.tensor_tensor(oh, sel, io4, ALU.is_equal))
                c = dve([c], lambda e, src=src: e.tensor_tensor(oh, oh, src, ALU.mult))
                a = dve([c], lambda e, half=half: e.tensor_reduce(bf2[:, half], oh, AX, ALU.add))
            ex = expf[:, b, :].rearrange("p (h s) -> p h s", h=PH)
            a = dve([a], lambda e: e.scalar_tensor_tensor(out=ex, in0=bf2[:, 0], scalar=float(NKEYS), in1=bf2[:, 1],
                                                          op0=ALU.mult, op1=ALU.add))
            gt = gates[:, b, :].rearrange("p (h s) -> p h s", h=PH)
            c = dve([g], lambda e: e.tensor_tensor(gt, bestv[:], bestv[:, :, 0:1].to_broadcast([P, PH, TOPK]), ALU.subtract))
            c = act([c], lambda e: e.activation(gates[:, b, :], gates[:, b, :], ACT.Exp))
            c = dve([c], lambda e: e.tensor_reduce(gsum[:], gt, AX, ALU.add))
            c = dve([c], lambda e: e.reciprocal(gsum[:], gsum[:]))
            c = dve([c], lambda e: e.tensor_tensor(gt, gt, gsum[:].unsqueeze(2).to_broadcast([P, PH, TOPK]), ALU.mult))
            return [a, c]

        row_full = [sem(f"row_full{i}") for i in range(GROUP)]
        rows_used, g_idx, g_gel, g_wts, g_iss = (sem(n) for n in (
            "rows_used", "idx_ready", "gelu_ready", "weights_ready", "gathers_issued"))
        state["g"] = 0
        NG = SLOTS // GROUP

        def gather(L, b, after, first, n, beside=None, side=None):
            g0 = state["g"]
            state["g"] += n
            per = 2 * GROUP

            def used(eng, i, g, value):
                if value + (g0 + g) * per > 0:
                    eng.wait_ge(rows_used, i * (2 * per) + ((g0 + g) * per + value))

            def pool_part(eng):
                def step(i, g):
                    eng.wait_ge(g_idx, i * 2 + (g0 + g + 1))
                    for t, tab in enumerate((io[f"expert_u{L}"], io[f"expert_v{L}"])):
                        for s in range(GROUP):
                            used(eng, i, g, (t - 1) * GROUP + s + 1)
                            eng.sem_inc(g_iss, 1)
                            eng.indirect_dma_start(
                                out=gring[:, s, :], out_offset=None, in_=tab,
                                in_offset=bass.IndirectOffsetOnAxis(ap=idx[:, (first + g) % 2, s:s + 1], axis=0)
                            ).then_inc(row_full[s], 16)
                turns(eng, n, step, head=1 if n % 2 else 2, width=2)
            q.part("pool", after, pool_part)

            def take(eng, i, g):
                used(eng, i, g - 1, 0)
                eng.activation(idx[:, (first + g) % 2, :], expf[:, b, bass.ds(i * (2 * GROUP) + (first + g) * GROUP, GROUP)],
                               ACT.Copy).then_inc(g_idx, 1)

            def act_step(eng, i, g):
                if first + g < NG - 1:
                    take(eng, i, g + 1)
                if beside:
                    beside.act(eng, i, g)
                used(eng, i, g, GROUP)
                if g0 + g > 0:
                    eng.wait_ge(g_wts, i * 2 + (g0 + g))
                eng.activation(gel[:], pre[:, (first + g) % 2, :], ACT.Gelu).then_inc(g_gel, 1)

            def dots(eng, i, g):
                for s in range(GROUP):
                    eng.wait_ge(row_full[s], i * 64 + (2 * (g0 + g) + 1) * 16)
                    eng.tensor_tensor_reduce(out=gring[:, s, :], in0=gring[:, s, :], in1=t_tok[:, b, :],
                                             scale=1.0, scalar=0.0, op0=ALU.mult, op1=ALU.add,
                                             accum_out=pre[:, (first + g) % 2, s:s + 1]).then_inc(rows_used, 1)
                if beside:
                    beside.dve(eng, i, g)

            def sums(eng, i, g):
                eng.wait_ge(g_gel, i * 2 + (g0 + g + 1))
                used(eng, i, g, 0)
                eng.tensor_tensor(wts[:], gel[:], gates[:, b, bass.ds(i * (2 * GROUP) + (first + g) * GROUP, GROUP)],
                                  ALU.mult).then_inc(g_wts, 1)
                eng.wait_ge(g_wts, i * 2 + (g0 + g + 1))
                for s in range(GROUP):
                    eng.wait_ge(row_full[s], i * 64 + (2 * (g0 + g) + 2) * 16)
                    used(eng, i, g, GROUP + s)
                    eng.scalar_tensor_tensor(out=x[:, b, :], in0=gring[:, s, :], scalar=wts[:, s:s + 1],
                                             in1=x[:, b, :], op0=ALU.mult, op1=ALU.add).then_inc(rows_used, 1)

            def dve_step(eng, i, g):
                dots(eng, i, g)
                sums(eng, i, g)

            if first == 0:
                q.part("act", after, lambda eng: take(eng, 0, 0))
            if side is None:
                q.part("act", after, lambda eng: turns(eng, n, lambda i, g: act_step(eng, i, g), head=1 if n % 2 else 2,
                                                       tail=2 if first + n == NG else 0, width=2))
                q.part("dve", after, lambda eng: turns(eng, n, lambda i, g: dve_step(eng, i, g), head=1 if n % 2 else 2, width=2))
            else:
                for g in range(n):
                    q.part("act", after, lambda eng, g=g: act_step(eng, 0, g))
                    q.part("dve", after, lambda eng, g=g: dots(eng, 0, g))
                    if side.live:
                        side.step()
                    q.part("dve", after, lambda eng, g=g: sums(eng, 0, g))
                    if g < n - 1 and side.live:
                        side.step()
            return [(rows_used, (g0 + n) * per), (g_gel, g0 + n), (g_wts, g0 + n)]

        LAT, CTX = 0, 1
        xs = [hT, xc]
        onesT = {D: small["ones"][:, 0, :], 384: small["ones"][:, 1, :], P: small["ones"][:, 2, :]}

        def quarter(n, wide=1):
            return (gs[:, :, :].rearrange("p a b -> p (a b)") if n % 8 < 4 else junk[:])[:, (n % 4) * S:(n % 4 + wide) * S]

        def feature_rstd(after, tiles):
            return drain(feature_rstd_steps(after, tiles))

        def feature_rstd_steps(after, tiles, bk=None, ready=None):
            bk, mm, n = bk or bank[7], [], len(tiles[0])
            T = n * S
            for k, pieces in enumerate(tiles):
                held = mm[k - 8 // n:k - 8 // n + 1] if k >= 8 // n else []
                for m, piece in enumerate(pieces):
                    a = act((ready[k:k + 1] if ready else after) + held,
                            lambda e, o=quarter(n * k + m), t=piece: e.activation(o, t, ACT.Square))
                sq_ = quarter(n * k, n)
                mm.append(pe([a] + (ready[k:k + 1] if ready else after), lambda e, k=k, sq_=sq_: e.matmul(
                    bk[:, 0:T], onesT[len(tiles) * P], sq_, start=(k == 0), stop=(k == len(tiles) - 1))))
            yield
            a = dve([mm[-1]] + after, lambda e: e.tensor_scalar(rs[:, 1, 0:T], bk[:, 0:T], EPS, None, ALU.add))
            a = act([a], lambda e: e.activation(rs[:, 0, 0:T], rs[:, 1, 0:T], ACT.Sqrt))
            yield
            return dve([a], lambda e: e.reciprocal(rs[:, 1, 0:T], rs[:, 0, 0:T]))

        def mod_norm(after, L, j, streams, out):
            ready = after if len(after) == KD else None
            return drain(mod_norm_steps(after[-1:] if ready else after, L, j, streams, out, ready))

        def mod_norm_steps(after, L, j, streams, out, ready=None):
            pair = isinstance(out, tuple)
            r = yield from feature_rstd_steps(after, [[xs[s][:, k, :] for s in streams] for k in range(KD)],
                                              bank[0] if ready else None, ready)
            items = [(k, n, s) for k in range(KD) for n, s in enumerate(streams)]
            high, low = [], []

            def rest(i):
                k, n, s = items[i]
                cols = slice(n * S, (n + 1) * S)
                low.append(dve([high[i]], lambda e: e.scalar_tensor_tensor(
                    out=out[1][:, k, cols], in0=quarter(i), scalar=mods[:, L, 3 * j * KD + k, s:s + 1],
                    in1=out[0][:, k, cols], op0=ALU.add, op1=ALU.subtract)))
            for i, (k, n, s) in enumerate(items):
                if i % 4 == 3:
                    yield
                cols = slice(n * S, (n + 1) * S)
                held = (low if pair else high)[i - 8:i - 7] if i >= 8 else []
                a = dve([r] + held, lambda e, i=i, k=k, n=n, s=s, cols=cols: e.scalar_tensor_tensor(
                    out=quarter(i), in0=xs[s][:, k, :], scalar=gA[:, L, j, k, s:s + 1], in1=rs[:, 1, cols],
                    op0=ALU.mult, op1=ALU.mult))
                o = (out[0] if pair else out)[:, k, cols]
                high.append(act([a], lambda e, o=o, i=i, k=k, s=s: e.activation(
                    o, quarter(i), ACT.Identity, bias=mods[:, L, 3 * j * KD + k, s:s + 1])))
                if pair and i >= 2:
                    rest(i - 2)
            if pair:
                rest(len(items) - 2)
                rest(len(items) - 1)
            return [high[-1]] + low[-1:]

        def residual(after, L, j, streams, k, bk):
            for n, s in enumerate(streams):
                r = dve(after, lambda e, n=n, s=s: e.scalar_tensor_tensor(
                    out=xs[s][:, k, :], in0=bk[:, n * S:(n + 1) * S], scalar=mods[:, L, (3 * j + 2) * KD + k, s:s + 1],
                    in1=xs[s][:, k, :], op0=ALU.mult, op1=ALU.add))
            return r

        def residuals(after, L, j, streams):
            return [residual(after, L, j, streams, k, bank[k]) for k in range(KD)]

        class FfnUp:

            def __init__(self, after, h, f):
                self.h, self.f = h, f
                self.u0, self.e0, self.h0 = state["unit"], state["evac"], state["half"]
                state["unit"] += 3 * KF
                state["evac"] += KF
                state["half"] += KF
                self.groups = KF // 2
                q.part("pe", after, self.pe)

            def place(self, st):
                return bank[(st // 2) % 4][:, (st % 2) * S:(st % 2 + 1) * S]

            def pe(self, eng):
                def step(i, st):
                    w = unit_wait(eng, self.u0, i, st)
                    if st % 2 == 0:
                        eng.wait_ge(evac, i * (RING // 2) + (self.e0 + max(0, st // 2 - 3)))
                    for k in range(KD):
                        last = eng.matmul(self.place(st), w[:, k * P:(k + 1) * P], self.h[:, k, :],
                                          start=(k == 0), stop=(k == KD - 1))
                    last.then_inc(unit_done, 1)
                turns(eng, 2 * KF, step, head=4)

            def act(self, eng, i, g):
                for m in (2 * g, 2 * g + 1):
                    eng.wait_ge(unit_done, i * RING + (self.u0 + 2 * m + 2))
                    eng.wait_ge(evac, i * (RING // 2) + (self.e0 + max(0, m - 1)))
                    eng.activation(gs[:, m % 2, 0:S], self.place(2 * m), ACT.Silu).then_inc(half_done, 1)

            def dve(self, eng, i, g):
                for m in (2 * g, 2 * g + 1):
                    eng.wait_ge(half_done, i * (RING // 2) + (self.h0 + m + 1))
                    eng.tensor_tensor(self.f[:, i * (RING // 2) + m, :], gs[:, m % 2, 0:S], self.place(2 * m + 1),
                                      ALU.mult).then_inc(evac, 1)

            def down(self):
                d0 = self.u0 + 2 * KF

                def part(eng):
                    def step(i, st):
                        w = unit_wait(eng, d0, i, st)
                        for m in range(KD):
                            last = eng.matmul(bank[m][:, 0:S], w[:, m * P:(m + 1) * P], self.f[:, i * RING + st, :],
                                              start=(st == 0), stop=(isinstance(i, int) and st == KF - 1))
                        last.then_inc(unit_done, 1)
                    turns(eng, KF, step, head=3, tail=3)
                q.part("pe", [(evac, self.e0 + KF), (half_done, self.h0 + KF)], part)
                return [(unit_done, d0 + KF)]

        def split_high(eng, u0, s0, i, st):
            w = unit_wait(eng, u0, i, st)
            eng.wait_ge(unit_done, i * RING + (u0 + st - SPLIT + 1))
            eng.activation(wr[:, (s0 + st) % SPLIT, :], w, ACT.Copy).then_inc(w_high, 1)

        def split_low(eng, u0, s0, i, st):
            eng.wait_ge(w_high, i * RING + (s0 + st + 1))
            eng.tensor_tensor(wl[:, (s0 + st) % SPLIT, :], ring[:, (u0 + st) % RING, :], wr[:, (s0 + st) % SPLIT, :],
                              ALU.subtract).then_inc(w_low, 1)

        def three(eng, out, wh, wlow, ah, al, first, last_):
            eng.matmul(out, wh, ah, start=first, stop=False)
            eng.matmul(out, wh, al, start=False, stop=False)
            return eng.matmul(out, wlow, ah, start=False, stop=last_)

        def ffn(after, L, j, streams):
            T = S * len(streams)
            u0, e0, h0, s0, f0 = (state[k_] for k_ in ("unit", "evac", "half", "split", "fsplit"))
            state["unit"] += 3 * KF
            state["evac"] += KF
            state["half"] += KF
            state["split"] += 3 * KF
            state["fsplit"] += KF
            deep = 4 if T == S else 2
            q.part("act", [], lambda eng: [split_high(eng, u0, s0, 0, st) for st in range(2)])
            q.part("dve", [], lambda eng: [split_low(eng, u0, s0, 0, st) for st in range(2)])
            hh = mod_norm(after, L, j, streams, (hr, hl))

            def place(st):
                if T == S:
                    return bank[(st // 2) % 4][:, (st % 2) * S:(st % 2 + 1) * S]
                return bank[st % 4][:, 0:T]

            def pe_up(eng):
                def step(i, st):
                    eng.wait_ge(w_low, i * RING + (s0 + st + 1))
                    if st % 2 == 0:
                        eng.wait_ge(evac, i * (RING // 2) + (e0 + max(0, st // 2 - deep + 1)))
                    sl = (s0 + st) % SPLIT
                    for k in range(KD):
                        ks = slice(k * P, (k + 1) * P)
                        last = three(eng, place(st), wr[:, sl, ks], wl[:, sl, ks], hr[:, k, 0:T], hl[:, k, 0:T],
                                     k == 0, k == KD - 1)
                    last.then_inc(unit_done, 1)
                turns(eng, 2 * KF, step, head=4)

            def act_up(eng):
                def step(i, m):
                    if m < KF - 1:
                        split_high(eng, u0, s0, i, 2 * m + 2)
                        split_high(eng, u0, s0, i, 2 * m + 3)
                    eng.wait_ge(unit_done, i * RING + (u0 + 2 * m + (2 if T == S else 1)))
                    eng.wait_ge(evac, i * (RING // 2) + (e0 + max(0, m - 1)))
                    eng.activation(gs[:, m % 2, 0:T], place(2 * m), ACT.Silu).then_inc(half_done, 1)
                turns(eng, KF, step, head=2, tail=1, width=RING // 2)

            def dve_up(eng):
                def step(i, m):
                    if m < KF - 1:
                        split_low(eng, u0, s0, i, 2 * m + 2)
                        split_low(eng, u0, s0, i, 2 * m + 3)
                    eng.wait_ge(unit_done, i * RING + (u0 + 2 * m + 2))
                    eng.wait_ge(half_done, i * (RING // 2) + (h0 + m + 1))
                    eng.tensor_tensor(fT[:, i * (RING // 2) + m, 0:T], gs[:, m % 2, 0:T], place(2 * m + 1),
                                      ALU.mult).then_inc(evac, 1)
                turns(eng, KF, step, head=2, tail=1, width=RING // 2)

            q.part("pe", hh, pe_up)
            q.part("act", hh, act_up)
            q.part("dve", hh, dve_up)
            d0, t0 = u0 + 2 * KF, s0 + 2 * KF

            def act_down(eng):
                def step(i, st):
                    split_high(eng, d0, t0, i, st)
                    if st == 0:
                        eng.wait_ge(evac, e0 + KF)
                    eng.wait_ge(unit_done, i * RING + (d0 + st - 1))
                    eng.activation(fr[:, st % 2, 0:T], fT[:, i * RING + st, 0:T], ACT.Copy).then_inc(f_high, 1)
                turns(eng, KF, step)

            def dve_down(eng):
                def step(i, st):
                    split_low(eng, d0, t0, i, st)
                    eng.wait_ge(f_high, i * RING + (f0 + st + 1))
                    eng.tensor_tensor(fl_[:, st % 2, 0:T], fT[:, i * RING + st, 0:T], fr[:, st % 2, 0:T],
                                      ALU.subtract).then_inc(f_low, 1)
                turns(eng, KF, step)

            def pe_down(eng):
                def step(i, st):
                    eng.wait_ge(w_low, i * RING + (t0 + st + 1))
                    eng.wait_ge(f_low, i * RING + (f0 + st + 1))
                    sl = (t0 + st) % SPLIT
                    for m in range(KD):
                        ms = slice(m * P, (m + 1) * P)
                        last = three(eng, bank[m][:, 0:T], wr[:, sl, ms], wl[:, sl, ms], fr[:, st % 2, 0:T],
                                     fl_[:, st % 2, 0:T], st == 0, isinstance(i, int) and st == KF - 1)
                    last.then_inc(unit_done, 1)
                turns(eng, KF, step, head=3, tail=3)

            q.part("act", [], act_down)
            q.part("dve", [(evac, e0 + KF)], dve_down)
            q.part("pe", [(evac, e0 + KF), (half_done, h0 + KF)], pe_down)
            return residuals([(unit_done, d0 + KF)] + hh, L, j, streams)


        def context_before_ffn(after):
            return (yield from mod_norm_steps(after, 0, 0, [CTX], hT))

        def mixer_ctx():
            r = yield from mixer_ab([], CTX, hT, qkT, hT)
            return (yield from mod_norm_steps(r, 0, 2, [CTX], hT))

        def back(after, L, streams, src):
            T = S * len(streams)
            rs_ = []
            for st in range(KD):
                t = unit_mm(after, lambda w, st=st: [(bank[st][:, 0:T], w[:, k * P:(k + 1) * P], src(k), k == 0, k == KD - 1)
                                                     for k in range(KD)])
                rs_.append(residual(after + [t], L, 1, streams, st, bank[st]))
                if st % 2:
                    yield
            return rs_

        def mixer_ab(after, s, h, f, y, bias_ready=[]):
            ready = after if s == LAT else None
            n = yield from mod_norm_steps(after[-1:] if ready else after, 0, 1, [s], h, ready)
            kt = ctxK if s == CTX else f[:, 12:16, :]
            vt = ctxV if s == CTX else f[:, 16:20, :].rearrange("p (b c) t -> p b (c t)", b=NB)
            yield
            ev = []
            for t in range(12):
                m = unit_mm(n + ev[t - 4:t - 3] if t >= 4 else n, lambda w, t=t: [
                    (bank[t % 4][:, 0:S], w[:, k * P:(k + 1) * P], h[:, k, 0:S], k == 0, k == KD - 1) for k in range(KD)])
                bk = bank[t % 4][:, 0:S]
                if t < 4:
                    ev.append(act([m], lambda e, t=t, bk=bk: e.activation(f[:, t, :], bk, ACT.Copy)))
                elif t < 8:
                    for head in range(2):
                        e_ = act([m], lambda e, t=t, bk=bk, head=head: e.activation(
                            f[:, 4 + 2 * (t - 4) + head, :], bk, ACT.Copy, scale=small["half"][:, head:head + 1]))
                    ev.append(e_)
                else:
                    ev.append(act([m], lambda e, t=t, bk=bk: e.activation(kt[:, t - 8, :], bk, ACT.Copy)))
                if t % 2:
                    yield
            for i in range(4):
                vm = unit_mm(n, lambda w, i=i: [(bank[4 + b][:, :], h[:, 2 * i + kk, b * P:(b + 1) * P],
                                                 w[:, kk * 512:(kk + 1) * 512], i == 0 and kk == 0, i == 3 and kk == 1)
                                                for kk in range(2) for b in range(NB)])
            ve = [act([vm], lambda e, b=b: e.activation(vt[:, b, :], bank[4 + b][:], ACT.Copy)) for b in range(NB)]
            yield
            cd, td = small["cdft"], small["tdft"]
            ready = ev[-4:] + ve
            out, second = [], []
            for g in range(4):
                bk, bo, buf = bank[g % 2], bank[2 + g % 2], attn_p[:, g % 2, :]
                m = q.many("pe", ready + second[g - 2:g - 1] * (g >= 2), [
                    (lambda e, b=b, g=g, bk=bk: e.matmul(bk[:, b * 256:(b + 1) * 256], f[:, g, b * P:(b + 1) * P], cd[:, :],
                                                         start=True, stop=True)) for b in range(NB)])
                c = act([m] + (second[g - 2:g - 1] if g >= 2 else []), lambda e, bk=bk, buf=buf: e.activation(buf, bk[:], ACT.Copy))
                second.append(q.many("pe", [c] + (out[g - 2:g - 1] if g >= 2 else []), [
                    (lambda e, b=b, r=r, bo=bo, buf=buf: e.matmul(
                        bo[:, 0:S], buf[:, b * 256 + r * P:b * 256 + (r + 1) * P], td[:, b, r, :],
                        start=(b == 0 and r == 0), stop=(b == 1 and r == 1))) for b in range(NB) for r in range(2)]))
                out.append(act([second[-1]] + ready, lambda e, g=g, bo=bo: e.activation(y[:, g, 0:S], bo[:, 0:S], ACT.Copy)))
                yield
            jobs = []
            for b in range(NB):
                if s == LAT:
                    for hh in range(NH):
                        r_ = slice((hh % 2) * HD, (hh % 2 + 1) * HD)
                        qs = f[:, 4 + hh, b * P:(b + 1) * P]
                        jobs.append(dict(
                            g=1, nk=2 * S,
                            logits=[[(qs, kt[:, hh // 2, :]), (ident[:], small["na_bias"][:, b * NH + hh, :])],
                                    [(qs, ctxK[:, hh // 2, :])]],
                            values=lambda pt, hh=hh: [(slice(0, HD), [
                                ((vt if kb < NB else ctxV)[:, kb % NB, hh * HD:(hh + 1) * HD], pt[:, kb * P:(kb + 1) * P])
                                for kb in range(4)])],
                            out=lambda t, ob, b=b, hh=hh, r_=r_: dve(t, lambda e: e.tensor_copy(
                                y[r_, 4 + hh // 2, b * P:(b + 1) * P], ob[0:HD, 0:P]))))
                else:
                    for hp in range(NH // 2):
                        jobs.append(dict(
                            g=2, nk=S,
                            logits=[[(f[:, 4 + 2 * hp + m, b * P:(b + 1) * P], kt[:, hp, :])] for m in range(2)],
                            values=lambda pt, hp=hp: [(slice(m * HD, (m + 1) * HD), [
                                (vt[:, kb, (2 * hp + m) * HD:(2 * hp + m + 1) * HD],
                                 pt[:, m * S + kb * P:m * S + (kb + 1) * P]) for kb in range(2)]) for m in range(2)],
                            out=lambda t, ob, b=b, hp=hp: act(t, lambda e: e.activation(
                                y[:, 4 + hp, b * P:(b + 1) * P], ob[:, 0:P], ACT.Copy))))
            at = yield from attention(out[-2:] + ready + bias_ready, jobs, bufs)
            return (yield from back(at, 0, [s], lambda k: y[:, k, 0:S]))

        def mixer_mla(after):
            h = mod_norm(after, 1, 1, [LAT, CTX], hT2)
            both = slice(0, 2 * S)
            ckv = mT[:, 3, :]
            kr = mT[:, 4, :]
            a = project(h, 5, lambda w, t: feature_major(w, hT2, both),
                        lambda e, b, t: e.activation(mT[:, t, :], b[:, :], ACT.Copy))
            r = feature_rstd(a, [[mT[:, k, 0:S]] for k in range(3)])
            n = [dve([r], lambda e, k=k: e.scalar_tensor_tensor(
                out=mT[:, k, 0:S], in0=mT[:, k, 0:S], scalar=small["mla_gq"][:, k:k + 1], in1=rs[:, 1, 0:S],
                op0=ALU.mult, op1=ALU.mult)) for k in range(3)]
            r = feature_rstd([n[-1]], [[mT[:, 3, 0:S], mT[:, 3, S:2 * S]]])
            n2 = dve([r], lambda e: e.scalar_tensor_tensor(
                out=mT[:, 3, :], in0=mT[:, 3, :], scalar=small["mla_gkv"][:, 0:1], in1=rs[:, 1, :],
                op0=ALU.mult, op1=ALU.mult))
            sc = (P + HD) ** -0.5
            u_q = project([n2], 8, lambda w, t: [(slice(m * S, (m + 1) * S), [
                (w[:, m * 384 + k * P:m * 384 + (k + 1) * P], mT[:, k, 0:S]) for k in range(3)]) for m in range(2)],
                lambda e, b, t: e.activation(mT[:, t + 5, :], b[:, :], ACT.Copy, scale=sc))
            qt = lambda m: mT[:, 5 + m // 2, (m % 2) * S:(m % 2 + 1) * S]
            u0 = state["unit"]
            state["unit"] += 2
            kt_ = lambda hh: hT2[:, hh, :]
            ke = []

            def kpart(eng):
                w = unit_wait(eng, u0, 0, 0)
                for hh in range(KD):
                    last = eng.matmul(bank[hh][:, :], w[:, hh * P:(hh + 1) * P], ckv, start=True, stop=True)
                last.then_inc(unit_done, 1)
            q.part("pe", u_q, kpart)
            ke = [(act if hh % 2 else dve)([(unit_done, u0 + 1)] + a, lambda e, hh=hh: (
                e.activation(kt_(hh), bank[hh][:], ACT.Copy) if hh % 2 else e.tensor_copy(kt_(hh), bank[hh][:])))
                for hh in range(KD)]

            def vpart(eng):
                w = unit_wait(eng, u0, 0, 1)
                for b in range(4):
                    for c in range(2):
                        last = eng.matmul(bank[2 * b + c][:, :], ckv[:, b * P:(b + 1) * P], w[:, c * 512:(c + 1) * 512],
                                          start=True, stop=True)
                last.then_inc(unit_done, 1)
            q.part("pe", ke[-2:], vpart)
            vt = lambda b, hh: mT[:, 13 + 2 * b + hh // 4, (hh % 4) * P:(hh % 4 + 1) * P]
            ve = [(act if c else dve)([(unit_done, u0 + 2)], lambda e, b=b, c=c: (
                e.activation(mT[:, 13 + 2 * b + c, :], bank[2 * b + c][:], ACT.Copy) if c
                else e.tensor_copy(mT[:, 13 + 2 * b + c, :], bank[2 * b + c][:]))) for b in range(4) for c in range(2)]
            rope = small["rope"]
            ends = []
            for n_, t_ in enumerate([qt(8 + m) for m in range(8)] + [kr[:, 0:S]]):
                m = pe(ve[-2:] + ke[-2:] + (ends[n_ - 4:n_ - 3] if n_ >= 4 else []),
                       lambda e, n_=n_, t_=t_: e.matmul(bank[n_ % 4][:, 0:S], small["rotm"][:, :], t_, start=True, stop=True))
                c = dve([m] + ends[-1:], lambda e, n_=n_: e.tensor_tensor(gs[:, n_ % 2, 0:S], bank[n_ % 4][:, 0:S], rope[:, 1, :], ALU.mult))
                d = dve([m], lambda e, t_=t_: e.tensor_tensor(t_, t_, rope[:, 0, :], ALU.mult))
                ends.append(dve([c, d], lambda e, n_=n_, t_=t_: e.tensor_tensor(t_, t_, gs[:, n_ % 2, 0:S], ALU.add)))
            jobs = []
            for b in range(NB):
                for hh in range(NH):
                    r_ = slice((hh % 2) * HD, (hh % 2 + 1) * HD)
                    jobs.append(dict(
                        g=1, nk=2 * S,
                        logits=[[(qt(hh)[:, b * P:(b + 1) * P], kt_(hh)),
                                 (qt(8 + hh)[:, b * P:(b + 1) * P], kr)]],
                        values=lambda pt, hh=hh: [(slice(0, P), [
                            (vt(kb, hh), pt[:, kb * P:(kb + 1) * P]) for kb in range(4)])],
                        out=lambda t, ob, b=b, hh=hh: dve(t, lambda e: e.tensor_copy(
                            attn_o[:, hh, b * P:(b + 1) * P], ob[:, 0:P]))))
            at = drain(attention(ends + ve + ke, jobs, bufs))
            return drain(back(at, 1, [LAT], lambda k: attn_o[:, k, :]))

        done = [loaded]
        for layer in range(DEPTH):
            done = layer_one(layer, done)

        h = norm_tokens(done, small["final_norm_g"])
        block1.close()
        wr = sb(ctx, "wr", [P, SPLIT, UW], F32R)
        wl = sb(ctx, "wl", [P, SPLIT, UW], F32R)
        loads2 = [sem("loads2"), 0]
        for name in ("mla_gq", "mla_gkv", "rope", "rotm", "final_g"):
            a = io[name]
            small[name] = sb(ctx, name + "_sb", list(a.shape))
            l2 = q.dma("act", h, small[name][:], a, loads2)
        with ExitStack() as for_ffn:
            fT = sb(for_ffn, "fT", [P, KF, 2 * S])
            hr = sb(for_ffn, "hr", [P, KD, 2 * S], F32R)
            hl = sb(for_ffn, "hl", [P, KD, 2 * S], F32R)
            fr = sb(for_ffn, "fr", [P, 2, 2 * S], F32R)
            fl_ = sb(for_ffn, "fl_", [P, 2, 2 * S], F32R)
        with ExitStack() as for_mixers:
            hT2 = sb(for_mixers, "hT2", [P, KD, 2 * S])
            mT = sb(for_mixers, "mT", [P, KF, 2 * S])
            attn_o = sb(for_mixers, "attn_o", [P, NH, S])
            small["na_bias"] = sb(for_mixers, "na_bias_sb", list(io["na_bias"].shape))
        mT_one = mT[:, 0:KF // 2, :].rearrange("p a (b t) -> p (a b) t", t=S)
        hT_one = hT2[:, 0:4, :].rearrange("p a (b t) -> p (a b) t", t=S)
        done = ffn(h, 0, 0, [LAT])
        bias_load = q.dma("act", done + [l2], small["na_bias"][:], io["na_bias"], [sem("bias_load"), 0])
        done = drain(mixer_ab(done, LAT, hT_one, mT_one, hT_one, [bias_load]))
        done = ffn(done, 0, 2, [LAT])
        done = ffn(done, 1, 0, [LAT, CTX])
        done = mixer_mla(done)
        done = ffn(done, 1, 2, [LAT])
        r = drain(feature_rstd_steps(done[-1:], [[xs[LAT][:, k, :]] for k in range(KD)], bank[0], done))
        f = [dve([r], lambda e, k=k: e.scalar_tensor_tensor(
            out=hT_one[:, k, :], in0=xs[LAT][:, k, :], scalar=small["final_g"][:, k:k + 1], in1=rs[:, 1, 0:S],
            op0=ALU.mult, op1=ALU.mult)) for k in range(KD)]
        stored = [sem("stored"), 0]
        o = q.dma("act", f, io["out"], hT_one, stored)
        q.part("act", [o], lambda e: None)
        assert state["unit"] == n_units, (state["unit"], n_units)

        block = ctx.enter_context(nc.Block())
        for name, deco in (("sp", block.sync), ("pe", block.tensor), ("act", block.scalar),
                           ("dve", block.vector), ("pool", block.gpsimd)):
            @deco
            def _(eng, name=name):
                for run in q.work[name]:
                    run(eng)


def _tiles(w):
    K, M = w.shape
    return w.reshape(K // P, P, M // P, P).transpose(2, 1, 0, 3).reshape(M // P, P, K)


def _rows(w, kpu=1):
    K, N = w.shape
    return w.reshape(K // P // kpu, kpu, P, N).transpose(0, 2, 1, 3).reshape(-1, P, kpu * N)


def _cols(a):
    a = np.asarray(a)
    b = a.reshape(a.shape[:-1] + (a.shape[-1] // P, P))
    return np.ascontiguousarray(np.moveaxis(b, -1, 0))


def _bucket(dist):
    n = np.maximum(dist, 0)
    nf = np.maximum(n, 1).astype(np.float32)
    large = 16 + (np.log(nf / np.float32(16)) / np.float32(math.log(8)) * np.float32(16)).astype(np.int32)
    return np.where(n < 16, n, np.minimum(large, 31))


def _layout(v):
    f = np.float32
    runs = {}
    for L in range(DEPTH):
        w = v["w_in"][L]
        dq, dk, dv, fq, fk, fv = (w[:, i * 512:(i + 1) * 512] for i in range(6))
        g = w[:, 3080:]
        runs[f"one{L}"] = [_tiles(dq), _tiles(fq), _tiles(dk), _tiles(fk), _tiles(g),
                           _rows(np.concatenate([dv, fv], 1)),
                           np.concatenate([_tiles(v["w_diff_o"][L]), _tiles(v["w_fox_o"][L])], 2),
                           _rows(v["w_out"][L]), _tiles(v["w_query"][L])]
        for j in range(2):
            gu = np.stack([_tiles(v["ffn_w_gate_2"][L, j]), _tiles(v["ffn_w_up_2"][L, j])], 1)
            runs[f"ffn{L}{j}"] = [gu.reshape(2 * KF, P, UW), _rows(v["ffn_w_down_2"][L, j])]
    ab = v["ab_w_in_2"][0]
    runs["ab"] = [_tiles(ab[:, 0:1536]), _rows(ab[:, 1536:], 2), _tiles(v["ab_w_out_2"][0])]
    wi = v["mla_w_in_2"][0]
    uq = v["mla_w_uq_2"][0].reshape(384, 8, 192)
    wr = np.concatenate([uq[:, :, 128:], np.zeros((384, 8, HD), f)], 2)
    uq = np.concatenate([uq[:, :, :128].reshape(384, 1024), wr.reshape(384, 1024)], 1)
    uq = _tiles(uq).reshape(8, 2, P, 384).transpose(0, 2, 1, 3).reshape(8, P, 768)
    uq = np.concatenate([uq, np.zeros((8, P, UW - 768), f)], 2)
    runs["mla"] = [_tiles(np.concatenate([wi, wi[:, 512:]], 1)), uq,
                   v["mla_w_uk_2"][0][None], v["mla_w_uv_2"][0][None], _tiles(v["mla_w_o_2"][0])]
    places, at = {}, 0
    for name, parts in runs.items():
        n = sum(a.shape[0] for a in parts)
        places[name] = (at, n)
        at += n
    io = {"stream": np.concatenate([a for parts in runs.values() for a in parts], 0)}
    io["x"] = v["x"][0].reshape(NB, P, D).transpose(1, 0, 2)
    io["half"] = np.kron(np.eye(2), np.full((HD, 1), HD ** -0.5)).astype(f)
    io["ident"] = np.eye(P, dtype=f)
    p = np.arange(P)[:, None]
    dist = P + p - np.arange(S)[None]
    io["causal"] = np.where(dist >= 0, 0, NEG).astype(f)
    rel = v["rel_bias"][_bucket(dist)].transpose(0, 2, 1)
    io["relb"] = np.where(dist[:, None, :] >= 0, rel, f(NEG))
    for n in ("norm1_g", "norm2_g", "final_norm_g"):
        io[n] = _cols(v[n])
    io["norm2_rows"] = np.repeat(v["norm2_g"][:, None], P, 1)
    io["subln_g"] = v["diff_subln_g"].T
    io["lam"] = np.repeat(v["diff_lambda"][None], P, 0)
    io["b_forget"] = np.repeat(v["b_forget"][None], P, 0)
    tri = (np.arange(S)[:, None] <= np.arange(S)[None]).astype(f)
    io["tri"] = tri.reshape(NB, P, S).transpose(1, 0, 2)
    io["pick"] = np.concatenate([np.eye(NH), -np.eye(NH)], 1).astype(f)
    io["w_ff"] = v["w_in"][:, :, 3072:3080].reshape(DEPTH, KD, P, NH).transpose(2, 0, 1, 3)
    io["keysT"] = v["sub_keys"].transpose(3, 0, 1, 2)
    io["iota16"] = np.repeat(np.arange(TOPK, dtype=f)[None], P, 0)
    for L in range(DEPTH):
        io[f"expert_u{L}"], io[f"expert_v{L}"] = v["expert_u"][L], v["expert_v"][L]
    io["ctxT"] = v["ctx_2"][0].T.reshape(KD, P, S).transpose(1, 0, 2)
    io["ada"] = np.concatenate([w.T.reshape(NMOD * KD, P, D) for w in v["ada_w_2"]], 0)
    io["cond"] = np.repeat(np.stack([v["c_2"][0], v["c_ctx_2"]])[:, None], P, 1)
    io["ada_b"] = _cols(v["ada_b_2"])
    io["norm_g"] = _cols(v["norm_g_2"])
    io["ones"] = np.stack([np.full((P, P), 1.0 / n, f) for n in (D, 384, P)], 1)
    col = np.arange(64)
    start = np.clip(col - 8, 0, 48)
    inside = (col[None] >= start[:, None]) & (col[None] < start[:, None] + 16)
    off = np.clip(col[None] - col[:, None] + 15, 0, 30)
    row = np.arange(4)[None] - np.arange(4)[:, None] + 7
    rp = v["ab_rpb_2"][0][:, row[:, None, :, None], off[None, :, None, :]]
    rp = np.where(inside[None, None, :, None, :], rp, f(NEG)).reshape(NH, NB, P, S)
    io["na_bias"] = rp.transpose(2, 1, 0, 3).reshape(P, NB * NH, S)
    k = np.arange(P)
    a = 2 * np.pi * ((k[:, None] * k[None]) % P) / P
    io["cdft"] = np.concatenate([np.cos(a), np.sin(a)], 1).astype(f)
    k = np.arange(S)
    a = 2 * np.pi * ((k[:, None] * k[None]) % S) / S
    s = 1 / math.sqrt(S * P)
    td = np.stack([np.cos(a) * s, -np.sin(a) * s], 1).astype(f)
    io["tdft"] = td.reshape(NB, P, 2, S).transpose(1, 0, 2, 3)
    io["mla_gq"] = _cols(v["mla_g_q_2"][0])
    io["mla_gkv"] = _cols(v["mla_g_kv_2"][0])
    pos = np.arange(S)
    inv = f(10000.0) ** (-np.arange(0, 32, 2, dtype=f) / f(32))
    ar, ac = (pos // 64).astype(f)[:, None] * inv, (pos % 64).astype(f)[:, None] * inv
    ang = np.concatenate([ar, ar, ac, ac], -1)
    io["rope"] = np.stack([np.tile(np.cos(ang).T, (2, 1)), np.tile(np.sin(ang).T, (2, 1))], 1).astype(f)
    rot = np.zeros((P, P), f)
    for b in range(0, P, 32):
        for j in range(16):
            rot[b + 16 + j, b + j] = -1
            rot[b + j, b + 16 + j] = 1
    io["rotm"] = rot
    io["final_g"] = _cols(v["final_g_2"])
    return {k_: np.ascontiguousarray(a_) for k_, a_ in io.items()}, places


def kernel(**inputs):
    import concourse.bacc as bacc
    from concourse.bass_utils import run_bass_kernel_spmd

    arrays, places = _layout({k: np.asarray(v) for k, v in inputs.items()})
    nc = bacc.Bacc("TRN2", target_bir_lowering=False, num_devices=1)
    io = {n: nc.dram_tensor("in_" + n, a.shape, F32, kind="ExternalInput").ap() for n, a in arrays.items()}
    io["out"] = nc.dram_tensor("out_0", (P, KD, S), F32, kind="ExternalOutput").ap()
    program(nc, io, places)
    r = run_bass_kernel_spmd(nc, [{"in_" + n: a for n, a in arrays.items()}], core_ids=[0])
    got = r.results[0]["out_0"]
    return np.ascontiguousarray(got.transpose(2, 1, 0).reshape(1, S, D))
```
